# Optimizing a Trainium2 kernel written in Bass

```python
import math
import jax, jax.numpy as jnp
from jax import lax
import numpy as np

D_MODEL = 2048
BATCH = 1
SEQ = 512
DEPTH = 1

CHUNK = 64
SB_BLOCK = 128
N_MEM = 256
D_MIX = D_MODEL
N_GROUPS = 4
GROUP_WIDTH = D_MIX // N_GROUPS
N_GROUP_HEADS = 4
HEAD_DIM = GROUP_WIDTH // N_GROUP_HEADS
GLA_DK = HEAD_DIM // 2
GLA_LOWRANK = 16
GLA_NORMALIZER = 16.0
DN_CONV = 4
ROPE_THETA = 10000.0
N_CROSS_HEADS = 4
CROSS_HEAD_DIM = D_MODEL // N_CROSS_HEADS
D_FF = 4 * D_MODEL
NORM_EPS = 1e-6

RET_COLS = (GROUP_WIDTH, GROUP_WIDTH, GROUP_WIDTH, GROUP_WIDTH)
GLA_COLS = (N_GROUP_HEADS * GLA_DK, N_GROUP_HEADS * GLA_DK, GROUP_WIDTH, GROUP_WIDTH, GLA_LOWRANK)
SB_COLS = (GROUP_WIDTH, GROUP_WIDTH, GROUP_WIDTH)
DN_COLS = (3 * GROUP_WIDTH, GROUP_WIDTH, N_GROUP_HEADS, N_GROUP_HEADS)
IN_SPLITS = RET_COLS + GLA_COLS + SB_COLS + DN_COLS
D_IN = sum(IN_SPLITS)

kernel_name = "hybrid_parallel_group_streaming_encoder"

def rms_norm(x, gain):
    xf = x.astype(jnp.float32)
    y = xf * lax.rsqrt(jnp.mean(xf * xf, axis=-1, keepdims=True) + NORM_EPS)
    return (y * gain.astype(jnp.float32)).astype(x.dtype)

def head_rms_norm(o, gain):
    b, s, h, d = o.shape
    return rms_norm(o, gain.reshape(h, d)).reshape(b, s, h * d)

def split_heads(t):
    return t.reshape(t.shape[0], t.shape[1], N_GROUP_HEADS, -1)

def l2_normalize(t):
    return t * lax.rsqrt(jnp.sum(t * t, axis=-1, keepdims=True) + 1e-6)

def chunk_heads(t):
    b, s, h, d = t.shape
    return t.reshape(b, s // CHUNK, CHUNK, h, d).transpose(1, 0, 3, 2, 4)

def unchunk_heads(t):
    n, b, h, c, d = t.shape
    return t.transpose(1, 0, 3, 2, 4).reshape(b, n * c, h, d)

def chunk_scalars(t):
    b, s, h = t.shape
    return t.reshape(b, s // CHUNK, CHUNK, h).transpose(1, 0, 3, 2)

def rotary_tables(positions):
    inv_freq = ROPE_THETA ** (-jnp.arange(0, HEAD_DIM, 2, dtype=jnp.float32) / HEAD_DIM)
    ang = positions.astype(jnp.float32)[..., None] * inv_freq
    return jnp.cos(ang)[:, :, None, :], jnp.sin(ang)[:, :, None, :]

def apply_rotary(t, cos, sin):
    t1, t2 = jnp.split(t, 2, axis=-1)
    return jnp.concatenate([t1 * cos - t2 * sin, t1 * sin + t2 * cos], axis=-1)

def retention_mixer(q, k, v, cos, sin):
    f32 = jnp.float32
    q = apply_rotary(q.astype(f32), cos, sin)
    k = apply_rotary(k.astype(f32), cos, sin) * HEAD_DIM ** -0.5
    v = v.astype(f32)
    log_gamma = jnp.log1p(-jnp.exp2(-5.0 - jnp.arange(N_GROUP_HEADS, dtype=f32)))
    pos = jnp.arange(CHUNK, dtype=f32)
    intra_decay = jnp.exp(log_gamma[:, None, None] * jnp.abs(pos[:, None] - pos[None, :]))
    query_decay = jnp.exp(log_gamma[:, None] * (pos + 1.0))[..., None]
    key_decay = jnp.exp(log_gamma[:, None] * (CHUNK - 1.0 - pos))[..., None]
    chunk_decay = jnp.exp(log_gamma * CHUNK)[:, None, None]

    def step(state, inp):
        qc, kc, vc = inp
        scores = jnp.einsum('bhid,bhjd->bhij', qc, kc) * intra_decay
        out = (jnp.einsum('bhij,bhje->bhie', scores, vc)
               + jnp.einsum('bhid,bhde->bhie', qc, state) * query_decay)
        state = chunk_decay * state + jnp.einsum('bhjd,bhje->bhde', kc * key_decay, vc)
        return state, out

    b, _, h, d = q.shape
    state0 = jnp.zeros((b, h, d, v.shape[-1]), f32)
    _, out = lax.scan(step, state0, (chunk_heads(q), chunk_heads(k), chunk_heads(v)))
    return unchunk_heads(out)

def gla_mixer(q, k, v, log_gate):
    f32 = jnp.float32
    q = q.astype(f32) * GLA_DK ** -0.5
    k = k.astype(f32)
    v = v.astype(f32)
    log_gate = log_gate.astype(f32)
    tri = jnp.tril(jnp.ones((CHUNK, CHUNK), dtype=bool))[:, :, None]

    def step(state, inp):
        qc, kc, vc, gc = inp
        b_cum = jnp.cumsum(gc, axis=2)
        diff = b_cum[:, :, :, None, :] - b_cum[:, :, None, :, :]
        pair_decay = jnp.where(tri, jnp.exp(jnp.where(tri, diff, 0.0)), 0.0)
        scores = jnp.einsum('bhijd,bhjd->bhij', qc[:, :, :, None, :] * pair_decay, kc)
        b_last = b_cum[:, :, -1:, :]
        out = (jnp.einsum('bhij,bhje->bhie', scores, vc)
               + jnp.einsum('bhid,bhde->bhie', qc * jnp.exp(b_cum), state))
        state = (jnp.exp(b_last[:, :, 0, :])[..., None] * state
                 + jnp.einsum('bhjd,bhje->bhde', kc * jnp.exp(b_last - b_cum), vc))
        return state, out

    b, _, h, dk = q.shape
    state0 = jnp.zeros((b, h, dk, v.shape[-1]), f32)
    _, out = lax.scan(step, state0, (chunk_heads(q), chunk_heads(k), chunk_heads(v), chunk_heads(log_gate)))
    return unchunk_heads(out)

def stick_breaking_mixer(q, k, v):
    f32 = jnp.float32
    q = q.astype(f32).transpose(0, 2, 1, 3)
    k = k.astype(f32).transpose(0, 2, 1, 3)
    v = v.astype(f32).transpose(0, 2, 1, 3)
    seq = q.shape[2]
    scale = HEAD_DIM ** -0.5
    outs = []
    for blk in range(seq // SB_BLOCK):
        start, end = blk * SB_BLOCK, (blk + 1) * SB_BLOCK
        logits = jnp.einsum('bhtd,bhsd->bhts', q[:, :, start:end], k[:, :, :end]) * scale
        t_idx = start + jnp.arange(SB_BLOCK)
        s_idx = jnp.arange(end)
        mask = s_idx[None, :] < t_idx[:, None]
        log_beta = jax.nn.log_sigmoid(logits)
        log_keep = jnp.where(mask, jax.nn.log_sigmoid(-logits), 0.0)
        log_later = lax.cumsum(log_keep, axis=3, reverse=True) - log_keep
        weights = jnp.where(mask, jnp.exp(log_beta + log_later), 0.0)
        outs.append(jnp.einsum('bhts,bhsd->bhtd', weights, v[:, :, :end]))
    return jnp.concatenate(outs, axis=2).transpose(0, 2, 1, 3)

def causal_depthwise_conv(x, w):
    return lax.conv_general_dilated(
        x, w.astype(x.dtype)[:, None, :], window_strides=(1,), padding=((DN_CONV - 1, 0),),
        dimension_numbers=('NWC', 'WIO', 'NWC'), feature_group_count=x.shape[-1])

def gated_deltanet_mixer(q, k, v, beta, log_decay):
    f32 = jnp.float32
    q = l2_normalize(q.astype(f32)) * HEAD_DIM ** -0.5
    k = l2_normalize(k.astype(f32))
    v = v.astype(f32)
    dv = v.shape[-1]
    tri_incl = jnp.tril(jnp.ones((CHUNK, CHUNK), dtype=bool))
    strict = jnp.tril(jnp.ones((CHUNK, CHUNK), dtype=f32), k=-1)
    eye = jnp.eye(CHUNK, dtype=f32)

    def step(state, inp):
        qc, kc, vc, bc, gc = inp
        g_cum = jnp.cumsum(gc, axis=-1)
        diff = g_cum[..., :, None] - g_cum[..., None, :]
        decay = jnp.where(tri_incl, jnp.exp(jnp.where(tri_incl, diff, 0.0)), 0.0)
        kb = kc * bc[..., None]
        lower = jnp.einsum('bhid,bhjd->bhij', kb, kc) * decay * strict
        rhs = jnp.concatenate([vc * bc[..., None], kb * jnp.exp(g_cum)[..., None]], axis=-1)
        sol = lax.linalg.triangular_solve(eye + lower, rhs, left_side=True, lower=True, unit_diagonal=True)
        u, w = sol[..., :dv], sol[..., dv:]
        v_new = u - jnp.einsum('bhcd,bhde->bhce', w, state)
        scores = jnp.einsum('bhid,bhjd->bhij', qc, kc) * decay
        out = (jnp.einsum('bhid,bhde->bhie', qc * jnp.exp(g_cum)[..., None], state)
               + jnp.einsum('bhij,bhje->bhie', scores, v_new))
        g_last = g_cum[..., -1]
        state = (jnp.exp(g_last)[..., None, None] * state
                 + jnp.einsum('bhjd,bhje->bhde', kc * jnp.exp(g_last[..., None] - g_cum)[..., None], v_new))
        return state, out

    b, _, h, dk = q.shape
    state0 = jnp.zeros((b, h, dk, dv), f32)
    _, out = lax.scan(step, state0, (chunk_heads(q), chunk_heads(k), chunk_heads(v),
                                     chunk_scalars(beta.astype(f32)), chunk_scalars(log_decay.astype(f32))))
    return unchunk_heads(out)

def hybrid_mixer(h, cos, sin, w_in, gla_w_up, gla_b_up, dn_conv_w, dn_a_log, dn_dt_bias, head_gain, w_out):
    dt = h.dtype
    proj = jnp.einsum('bsd,de->bse', h, w_in)
    split_points = np.cumsum(IN_SPLITS)[:-1].tolist()
    (ret_q, ret_k, ret_v, ret_g,
     gla_q, gla_k, gla_v, gla_g, gla_lr,
     sb_q, sb_k, sb_v,
     dn_qkv, dn_z, dn_b, dn_a) = jnp.split(proj, split_points, axis=-1)
    gains = jnp.split(head_gain, N_GROUPS)

    ret = retention_mixer(split_heads(ret_q), split_heads(ret_k), split_heads(ret_v), cos, sin).astype(dt)
    y_ret = jax.nn.silu(ret_g) * head_rms_norm(ret, gains[0])

    gla_logit = jnp.einsum('bsr,re->bse', gla_lr, gla_w_up) + gla_b_up
    gla_log_gate = jax.nn.log_sigmoid(gla_logit.astype(jnp.float32)) / GLA_NORMALIZER
    gla = gla_mixer(split_heads(gla_q), split_heads(gla_k), split_heads(gla_v), split_heads(gla_log_gate)).astype(dt)
    y_gla = jax.nn.silu(gla_g) * head_rms_norm(gla, gains[1])

    sb = stick_breaking_mixer(split_heads(sb_q), split_heads(sb_k), split_heads(sb_v)).astype(dt)
    y_sb = head_rms_norm(sb, gains[2])

    dn_qkv = jax.nn.silu(causal_depthwise_conv(dn_qkv, dn_conv_w))
    dn_q, dn_k, dn_v = jnp.split(dn_qkv, 3, axis=-1)
    dn_beta = jax.nn.sigmoid(dn_b.astype(jnp.float32))
    dn_log_decay = -jnp.exp(dn_a_log.astype(jnp.float32)) * jax.nn.softplus(
        dn_a.astype(jnp.float32) + dn_dt_bias.astype(jnp.float32))
    dn = gated_deltanet_mixer(split_heads(dn_q), split_heads(dn_k), split_heads(dn_v), dn_beta, dn_log_decay).astype(dt)
    y_dn = head_rms_norm(dn, gains[3]) * jax.nn.silu(dn_z)

    y = jnp.concatenate([y_ret, y_gla, y_sb, y_dn], axis=-1)
    return jnp.einsum('bse,ed->bsd', y, w_out)

def cross_attention(h, m, w_q, w_kv, w_o):
    b, s, _ = h.shape
    q = jnp.einsum('bsd,de->bse', h, w_q).reshape(b, s, N_CROSS_HEADS, CROSS_HEAD_DIM)
    k, v = jnp.split(jnp.einsum('bmd,de->bme', m, w_kv), 2, axis=-1)
    k = k.reshape(b, m.shape[1], N_CROSS_HEADS, CROSS_HEAD_DIM)
    v = v.reshape(b, m.shape[1], N_CROSS_HEADS, CROSS_HEAD_DIM)
    scores = jnp.einsum('bshd,bmhd->bhsm', q.astype(jnp.float32), k.astype(jnp.float32)) * CROSS_HEAD_DIM ** -0.5
    p = jax.nn.softmax(scores, axis=-1)
    o = jnp.einsum('bhsm,bmhd->bshd', p, v.astype(jnp.float32)).astype(h.dtype).reshape(b, s, D_MODEL)
    return jnp.einsum('bse,ed->bsd', o, w_o)

def squared_relu_mlp(h, w_up, w_down):
    u = jax.nn.relu(jnp.einsum('bsd,df->bsf', h, w_up))
    return jnp.einsum('bsf,fd->bsd', u * u, w_down)

def setup_inputs(seed: int = 0) -> dict:
    key = jax.random.key(seed)
    ks = jax.random.split(key, 21)
    f32 = jnp.float32
    nrm = lambda k, shape, scale: jax.random.normal(k, shape, f32) * scale
    gain = lambda k, shape: 1.0 + 0.02 * jax.random.normal(k, shape, f32)
    offset = jax.random.randint(ks[2], (BATCH, 1), 0, 4096, dtype=jnp.int32)
    positions = offset + jnp.arange(SEQ, dtype=jnp.int32)[None, :]
    dt0 = jnp.exp(jax.random.uniform(ks[9], (DEPTH, N_GROUP_HEADS), f32,
                                     minval=math.log(1e-3), maxval=math.log(1e-1)))
    return {
        "x": jax.random.normal(ks[0], (BATCH, SEQ, D_MODEL), f32),
        "mem": jax.random.normal(ks[1], (BATCH, N_MEM, D_MODEL), f32),
        "positions": positions,
        "ln_mix": gain(ks[3], (DEPTH, D_MODEL)),
        "w_in": nrm(ks[4], (DEPTH, D_MODEL, D_IN), D_MODEL ** -0.5),
        "gla_w_up": nrm(ks[5], (DEPTH, GLA_LOWRANK, N_GROUP_HEADS * GLA_DK), GLA_LOWRANK ** -0.5),
        "gla_b_up": nrm(ks[6], (DEPTH, N_GROUP_HEADS * GLA_DK), 0.02),
        "dn_conv_w": nrm(ks[7], (DEPTH, DN_CONV, 3 * GROUP_WIDTH), DN_CONV ** -0.5),
        "dn_a_log": jnp.log(jax.random.uniform(ks[8], (DEPTH, N_GROUP_HEADS), f32, minval=1.0, maxval=16.0)),
        "dn_dt_bias": dt0 + jnp.log(-jnp.expm1(-dt0)),
        "mix_head_norm": gain(ks[10], (DEPTH, D_MIX)),
        "w_mix_out": nrm(ks[11], (DEPTH, D_MIX, D_MODEL), D_MIX ** -0.5),
        "ln_cross": gain(ks[12], (DEPTH, D_MODEL)),
        "ln_mem": gain(ks[13], (DEPTH, D_MODEL)),
        "w_cross_q": nrm(ks[14], (DEPTH, D_MODEL, D_MODEL), D_MODEL ** -0.5),
        "w_cross_kv": nrm(ks[15], (DEPTH, D_MODEL, 2 * D_MODEL), D_MODEL ** -0.5),
        "w_cross_o": nrm(ks[16], (DEPTH, D_MODEL, D_MODEL), D_MODEL ** -0.5),
        "ln_mlp": gain(ks[17], (DEPTH, D_MODEL)),
        "w_mlp_up": nrm(ks[18], (DEPTH, D_MODEL, D_FF), D_MODEL ** -0.5),
        "w_mlp_down": nrm(ks[19], (DEPTH, D_FF, D_MODEL), D_FF ** -0.5),
        "ln_final": gain(ks[20], (D_MODEL,)),
    }

def reference(x, mem, positions, ln_mix, w_in, gla_w_up, gla_b_up, dn_conv_w, dn_a_log, dn_dt_bias,
              mix_head_norm, w_mix_out, ln_cross, ln_mem, w_cross_q, w_cross_kv, w_cross_o,
              ln_mlp, w_mlp_up, w_mlp_down, ln_final):
    cos, sin = rotary_tables(positions)
    for layer in range(DEPTH):
        h = rms_norm(x, ln_mix[layer])
        x = x + hybrid_mixer(h, cos, sin, w_in[layer], gla_w_up[layer], gla_b_up[layer], dn_conv_w[layer],
                             dn_a_log[layer], dn_dt_bias[layer], mix_head_norm[layer], w_mix_out[layer])
        h = rms_norm(x, ln_cross[layer])
        m = rms_norm(mem, ln_mem[layer])
        x = x + cross_attention(h, m, w_cross_q[layer], w_cross_kv[layer], w_cross_o[layer])
        h = rms_norm(x, ln_mlp[layer])
        x = x + squared_relu_mlp(h, w_mlp_up[layer], w_mlp_down[layer])
    return rms_norm(x, ln_final)


_drawn_inputs = setup_inputs


def setup_inputs(seed=0):
    import zlib

    import numpy as np

    out = dict(_drawn_inputs(seed))
    spreads = {}
    factors = {'ln_mix': 2.877,
     'gla_b_up': 8.0,
     'mix_head_norm': 4.556,
     'ln_cross': 8.0,
     'ln_mem': 8.0,
     'ln_mlp': 10.645,
     'ln_final': 8.301}
    for name, (base, spread) in spreads.items():
        noise = np.random.default_rng([zlib.crc32(name.encode()), seed]).standard_normal(out[name].shape)
        drawn = base * np.exp(spread * noise) if base else spread * noise
        out[name] = __import__('jax').numpy.asarray(drawn.astype(out[name].dtype))
    for name, factor in factors.items():
        out[name] = (out[name] * factor).astype(out[name].dtype)
    return out
```

```python
import math
from contextlib import ExitStack

import concourse.bass as bass
from concourse import mybir

F32 = mybir.dt.float32
F32R = mybir.dt.float32r
I32 = mybir.dt.int32
ALU = mybir.AluOpType
ACT = mybir.ActivationFunctionType
AX = mybir.AxisListType

P = 128
EPS = 1e-6
HOP, SEG = "hop", "segment"
TWO_PI_PARTS = (6.28125, 0.0019350051879882812, 3.019916e-07)
ROUND_MAGIC = 12582912.0
FAR = -30000.0
GATE_FLOOR = -40.0


class Count:

    def __init__(self, start=0):
        self.outer, self.n, self.first, self.stack = 0, start, start, []

    def at(self, d=0):
        return self.outer + (self.n + d)

    def step(self, k=1):
        self.n += k
        self.first += k

    def enter(self, i, per):
        self.stack.append((self.outer, self.n, per))
        self.outer, self.n = i * per + (self.outer + self.n), 0

    def leave(self, times):
        outer, n, per = self.stack.pop()
        assert self.n == per, f"the loop's body counts {self.n}, not {per}"
        self.outer, self.n = outer, n + times * per
        self.first += (times - 1) * per


class Chain:

    def __init__(self, eng, sem):
        self.eng, self.sem, self.count = eng, sem, Count()

    def put(self, ins):
        ins.then_inc(self.sem, 1)
        self.count.step()

    def sync(self):
        self.eng.wait_ge(self.sem, self.count.at())

    def link(self, ins):
        self.put(ins)
        self.sync()


def run_segment(mixer):
    if mixer is not None:
        for step in mixer:
            if step == SEG:
                break


SEMS = """
 special_in vec_in small_in pos_in raw_zero slab_hi slab_lo slab_mul slab_out consts heads_done
x_turned x_even x_odd xg_hi act_ready act_free x_ssq x_diag x_bcast rstd_ready vec_turned vec_ready x_parked mem_in
mem_scaled mem_turned mem_out mem_parked mem_back mem_hi mem_split
rows_ready cols_turned cols_ready bcast_ps
pos_bcast pos_ready ang_ready trig_ready dist_ready
gate_clamped gate_sig gate_ready o_ready sq_ready norm_sum norm_ready vt_ready vtok_ready
ret_rot ret_qk ret_scores ret_w
dn_clamped dn_sig dn_silu dn_sq dn_l2 dn_inv dn_qk dn_dd dn_dt dn_b1 dn_b2 dn_pair dn_tok
dn_c1t dn_x dn_ct dn_u dn_uev dn_v dn_uw dn_uwev dn_eg dn_qg dn_ws dn_vnew dn_ds dn_state
gla_z gla_l gla_qs gla_diag gla_d gla_e gla_qe gla_lv gla_lvout gla_topout bcast_rows dn_gram dn_bvk dn_gbev dn_cols kv_turned
sb_scores sb_x sb_masked sb_l sb_lk sb_cum sb_z sb_w
kv_vout xsq_ready xacc_ready
cx_scores cx_max cx_exp cx_p cx_pt cx_ptok cx_o
up_in mlp_relu mlp_uhi u_ready fin_sq fin_sum fin_rstd fin_x fin_turned fin_even fin_odd x_total x_rstd dec_exp dn_colexp cx_done rows_out rows_act
act_chain dve_chain pool_chain 
""".split()


def build(nc, x_in, mem_in, positions, ln_mix, w_in, gla_w_up, gla_b_up, dn_conv_w, dn_a_log, dn_dt_bias,
          mix_head_norm, w_mix_out, ln_cross, ln_mem, w_cross_q, w_cross_kv, w_cross_o, ln_mlp,
          w_mlp_up, w_mlp_down, ln_final, inv_freq, out, park="Internal"):
    S, D = x_in.shape[1], x_in.shape[2]
    NMEM = mem_in.shape[1]
    KT, NT, MT = D // P, S // P, NMEM // P
    DFF = w_mlp_up.shape[2]
    GW = D // 4
    NH = GW // P
    RANK = gla_w_up.shape[1]
    DK = P // 2
    CONV = dn_conv_w.shape[1]
    CH = 64
    C_RET, C_GLA = 0, 4 * GW
    C_LR = C_GLA + 3 * GW
    C_SB = C_LR + RANK
    C_DN = C_SB + 3 * GW
    C_B = C_DN + 4 * GW
    C_A = C_B + NH
    SLAB = KT * P
    MC = 1024 // P
    NCH = DFF // (MC * P)
    WID = [S - P * j for j in range(NT)]
    OFF = [sum(WID[:j]) for j in range(NT)]
    PK = sum(WID)
    LOG_GAMMA = [math.log1p(-2.0 ** (-5 - h)) for h in range(NH)]
    QSCALE, CSCALE = P ** -0.5, GW ** -0.5
    LEVELS = [64, 32, 16, 8, 4, 2, 1]
    Y_RET, Y_GLA, Y_SB, Y_DN = 0, NH, 2 * NH, 3 * NH
    H_RET, H_DN, H_GLA, H_SB = 0, NH, 2 * NH, 3 * NH
    V_MIX, V_HEAD, V_CROSS, V_MEM, V_MLP, V_FINAL = (KT * j for j in range(6))
    V_N = 6 * KT
    C_BUP = CONV * 3 * NH
    C_N = C_BUP + 2
    KV0 = 1 + 4 * NH + 4 * NH + 6 * NH // 2 + 6 * NH // 2
    OUT0 = KV0 + 2 * KT
    BETA, DECAY = 32, 64

    kview = lambda w: w[0].rearrange("(k p) n -> p k n", p=P)
    w_in_v, w_out_v, w_cq_v, w_ckv_v, w_co_v, w_up_v = map(
        kview, (w_in, w_mix_out, w_cross_q, w_cross_kv, w_cross_o, w_mlp_up))
    w_dn_v = kview(w_mlp_down)

    def dram(name, shape):
        return nc.dram_tensor(name, shape, F32, kind=park).ap()

    x_park = dram("x_park", (KT, P, S))
    y_park = dram("y_park", (KT, P, S))
    m_park = dram("m_park", (KT, P, NMEM))
    k_park = dram("k_park", (KT, P, NMEM))
    v_park = dram("v_park", (KT, P, NMEM))

    with ExitStack() as ctx:
        def alloc(scope):
            return lambda name, shape, dt=F32: scope.enter_context(nc.sbuf_tensor(name, shape, dt))

        on = {name: ctx.enter_context(nc.semaphore(name)) for name in SEMS}
        raw_in = [ctx.enter_context(nc.semaphore(f"raw_in{j}")) for j in range(2)]
        x_loaded = [ctx.enter_context(nc.semaphore(f"x_loaded{j}")) for j in range(NT)]
        main_back = [ctx.enter_context(nc.semaphore(f"main_back{j}")) for j in range(4)]
        y_parked = [ctx.enter_context(nc.semaphore(f"y_parked{j}")) for j in range(2)]
        kv_tile_parked = [ctx.enter_context(nc.semaphore(f"kv_tile_parked{j}")) for j in range(2)]
        kv_loaded = [ctx.enter_context(nc.semaphore(f"kv_loaded{j}")) for j in range(2)]
        out_done = [ctx.enter_context(nc.semaphore(f"out_done{j}")) for j in range(2)]

        G = [ctx.enter_context(nc.psum_tensor(f"slab_ps{j}", [P, S], F32)) for j in range(2)]
        M = [ctx.enter_context(nc.psum_tensor(f"mix_ps{j}", [P, S], F32)) for j in range(6)]

        sb = alloc(ctx)
        act_hi = sb("act_hi", [P, KT, S], F32R)
        act_lo = sb("act_lo", [P, KT, S], F32R)
        w_raw = sb("w_raw", [P, 2, SLAB])
        w_hi = sb("w_hi", [P, 2, SLAB], F32R)
        w_lo = sb("w_lo", [P, 2, SLAB], F32R)
        ident = sb("ident", [P, P])
        ones = sb("ones", [P, P])
        vecs = sb("vecs", [P, V_N])
        convs = sb("convs", [P, C_N])
        rstd = sb("rstd", [P, S])
        eps_col = sb("eps_col", [P, 1])
        cols = sb("cols", [P, 32])
        rcols = sb("rcols", [P, NT, 2 * NH])

        mix = ctx.enter_context(ExitStack())
        sb = alloc(mix)
        tri_suffix = sb("tri_suffix", [P, P])
        tri_incl = sb("tri_incl", [P, P])
        tri_strict = sb("tri_strict", [P, P])
        lvl_mask = sb("lvl_mask", [P, 7, P])
        with ExitStack() as scope:
            sb = alloc(scope)
            x_t = sb("x_t", [P, KT, S])
            x_tok = sb("x_tok", [P, NT, D])
            mem_t = sb("mem_t", [P, KT, NMEM])
            vec_rows = sb("vec_rows", [V_N, P])
            conv_rows = sb("conv_rows", [C_N, P])
            diag_r = sb("diag_r", [P, NT, P])
        sb = alloc(mix)
        stage = sb("stage", [P, 2, 6, S])
        rows = sb("rows", [P, S])
        vtok = sb("vtok", [P, NT, P])
        gate = sb("gate", [P, S])
        gtmp = sb("gtmp", [P, S])
        sq = sb("sq", [P, S])
        nrm = sb("nrm", [P, S])
        ytile = sb("ytile", [P, 2, S])
        with ExitStack() as scope:
            sb = alloc(scope)
            rot = sb("rot", [P, P])
            cos_t = sb("cos_t", [P, S])
            sin_t = sb("sin_t", [P, S])
            ret_dec = sb("ret_dec", [P, NH, S])
            dist = sb("dist", [P, S])
            ret_q = sb("ret_q", [P, S])
            ret_k = sb("ret_k", [P, S])
            ret_t = sb("ret_t", [P, 2, S])
            ret_wt = sb("ret_wt", [P, PK])
            pos_row = sb("pos_row", [1, S], I32)
            pos_rowf = sb("pos_rowf", [1, S])
            freq_col = sb("freq_col", [P, 1])
            ang = sb("ang", [P, S])
        with ExitStack() as scope:
            sb = alloc(scope)
            dn_rows = sb("dn_rows", [P, S])
            dn_gb = sb("dn_gb", [P, S])
            dn_c = sb("dn_c", [P, 3, S])
            dn_s = sb("dn_s", [P, 3, S])
            dn_dt = sb("dn_dt", [P, S])
            dn_bs = sb("dn_bs", [P, S])
            dn_lt = sb("dn_lt", [P, S])
            dn_at = sb("dn_at", [P, S])
            dn_ctt = sb("dn_ctt", [P, 2, S])
            dn_xx = sb("dn_xx", [P, S])
            dn_xt = sb("dn_xt", [P, S])
            dn_uu = sb("dn_uu", [P, S])
            dn_bv = sb("dn_bv", [P, S])
            dn_kdec = sb("dn_kdec", [P, S])
            dn_st = sb("dn_st", [P, P])
            dn_vn = sb("dn_vn", [P, P])
            dn_cols = sb("dn_cols", [P, 8, NT])
        dn_kbe, dn_wt, dn_qg = dn_s[:, 0], dn_s[:, 1], dn_s[:, 2]
        with ExitStack() as scope:
            sb = alloc(scope)
            b_loc = sb("b_loc", [P, 2, S])
            b_all = sb("b_all", [P, 2, S])
            gla_t = sb("gla_t", [P, 2, S])
            restart = sb("restart", [P, S])
            gla_qs = sb("gla_qs", [P, S])
            gla_e = sb("gla_e", [P, 2, S])
            gla_qk = sb("gla_qk", [P, 2, S])
            gla_s = sb("gla_s", [P, 2, S])
            gla_o = sb("gla_o", [P, 2, PK - S])
            gla_up = sb("gla_up", [RANK, 2 * P])
        with ExitStack() as scope:
            sb = alloc(scope)
            sb_x = sb("sb_x", [P, PK])
            sb_l = sb("sb_l", [P, PK])
            sb_m = sb("sb_m", [P, PK])
            mem_back = sb("mem_back", [P, KT, NMEM])
            kv_t = sb("kv_t", [P, 2, NMEM])
            v_t = sb("v_t", [P, 2, NMEM])
        mix.close()

        main = alloc(ctx)("main", [P, KT, S])
        sb = alloc(ctx)
        xsq = sb("xsq", [P, 2, S])
        xacc = sb("xacc", [P, S])
        with ExitStack() as scope:
            sb = alloc(scope)
            cstage = sb("cstage", [P, 2, NH, S])
            kh = sb("kh", [P, 2, NH, NMEM])
            vh = sb("vh", [P, 2, NH, NMEM])
            prob = sb("prob", [P, NT, NMEM])
            prob_t = sb("prob_t", [P, MT, S])
            ccols = sb("ccols", [P, 4, NT])
        with ExitStack() as scope:
            sb = alloc(scope)
            u_hi = sb("u_hi", [P, MC, S], F32R)
            u_lo = sb("u_lo", [P, MC, S], F32R)
            relu = sb("relu", [P, 2, S])
            uf = sb("uf", [P, 2, S])

        flat3 = lambda t: t.rearrange("p (t s) -> p t s", s=P)
        per_tile = lambda c: c.unsqueeze(2).broadcast_to([P, NT, P])
        every_tile = lambda m: m.unsqueeze(1).broadcast_to([P, NT, P])

        def packed(t, j):
            return t[:, OFF[j]:OFF[j] + WID[j]]

        SC = [(3, 0), (4, 0), (5, 0), (5, WID[2])]

        def score_ps(j):
            bank, at = SC[j]
            return M[bank][:, at:at + WID[j]]

        block = ctx.enter_context(nc.Block())

        @block.sync
        def _(sp):
            for t in range(NT):
                sp.dma_start(x_tok[:, t], x_in[0, t * P:(t + 1) * P, :]).then_inc(x_loaded[t], 16)
            slabs = Count()

            first = w_raw[:, 0].rearrange("p (k n) -> p k n", k=KT)
            sp.wait_ge(on["raw_zero"], 1)
            for at, col, n in ((0, C_LR, RANK), (BETA, C_B, NH), (DECAY, C_A, NH)):
                sp.dma_start(first[:, :, at:at + n], w_in_v[:, :, col:col + n]).then_inc(on["special_in"], 16)
            slabs.step()

            def load(src):
                slot = slabs.first % 2
                if slabs.first >= 2:
                    sp.wait_ge(on["slab_lo"], slabs.at(-1))
                dst = w_raw[:, slot].rearrange("p (k n) -> p k n", k=src.shape[1])
                sp.dma_start(dst, src).then_inc(raw_in[slot], 16)
                slabs.step()

            def head4(col):
                for t in range(4):
                    load(w_in_v[:, :, bass.ds(col + t * GW, P)])

            head4(C_RET)
            with sp.Fori(1, NH) as h:
                slabs.enter(h - 1, 4)
                head4(h * P + C_RET)
            slabs.leave(NH - 1)
            with sp.Fori(0, NH) as h:
                slabs.enter(h, 4)
                head4(h * P + C_DN)
            slabs.leave(NH)
            with sp.Fori(0, 2) as p:
                slabs.enter(p, 6)
                load(w_in_v[:, :, bass.ds(p * P + C_GLA, P)])
                load(w_in_v[:, :, bass.ds(p * P + (C_GLA + GW // 2), P)])
                for t in (GW, 2 * GW):
                    for j in range(2):
                        load(w_in_v[:, :, bass.ds(p * 2 * P + (C_GLA + t + j * P), P)])
            slabs.leave(2)
            with sp.Fori(0, 2) as p:
                slabs.enter(p, 6)
                for j in range(2):
                    for t in range(3):
                        load(w_in_v[:, :, bass.ds(p * 2 * P + (C_SB + t * GW + j * P), P)])
            slabs.leave(2)

            def matrix(w, n):
                with sp.Fori(0, n // 2) as i:
                    slabs.enter(i, 2)
                    for j in range(2):
                        load(w[:, :, bass.ds(i * 2 * P + j * P, P)])
                slabs.leave(n // 2)

            matrix(w_ckv_v, 2 * KT)
            matrix(w_out_v, KT)
            matrix(w_cq_v, KT)
            matrix(w_co_v, KT)
            with sp.Fori(0, NCH) as c:
                slabs.enter(c, 2 * MC)
                for j in range(MC):
                    load(w_up_v[:, :, bass.ds(c * MC * P + j * P, P)])
                for j in range(MC):
                    load(w_dn_v[:, bass.ds(c * MC, MC), j * 2 * P:(j + 1) * 2 * P])
            slabs.leave(NCH)

            for t in range(NT):
                sp.wait_ge(on["fin_even"], 2 * t + 2)
                sp.wait_ge(on["fin_odd"], 2 * t + 2)
                sp.dma_start(out[0, t * P:(t + 1) * P, :], w_raw[:, t % 2]).then_inc(out_done[t % 2], 16)
            for j in range(2):
                sp.wait_ge(out_done[j], 16 * NT // 2)

        @block.gpsimd
        def _(pool):
            chain = Chain(pool, on["pool_chain"])
            chain.put(nc.gpsimd.memset(ident[:], 0.0))
            chain.put(nc.gpsimd.memset(ones[:], 1.0))
            chain.put(nc.gpsimd.memset(eps_col[:], EPS))
            chain.sync()
            nc.gpsimd.affine_select(out=ident[:], in_=ident[:], compare_op=ALU.not_equal, fill=1.0, base=0,
                                    pattern=[[-1, P]], channel_multiplier=1).then_inc(on["consts"], 1)
            at = 0
            for v in (ln_mix[0], mix_head_norm[0], ln_cross[0], ln_mem[0], ln_mlp[0], ln_final):
                pool.dma_start(vec_rows[at:at + KT, :], v.rearrange("(k p) -> k p", p=P)).then_inc(on["vec_in"], 16)
                at += KT
            pool.dma_start(conv_rows[0:C_BUP, :], dn_conv_w[0].rearrange("i (t p) -> (i t) p", p=P)).then_inc(
                on["vec_in"], 16)
            pool.dma_start(conv_rows[C_BUP:C_N, :], gla_b_up[0].rearrange("(t p) -> t p", p=P)).then_inc(
                on["vec_in"], 16)
            pool.dma_start(cols[DECAY:DECAY + NH, 20:21], dn_a_log.rearrange("a h -> h a")).then_inc(
                on["small_in"], 16)
            pool.dma_start(cols[DECAY:DECAY + NH, 21:22], dn_dt_bias.rearrange("a h -> h a")).then_inc(
                on["small_in"], 16)
            for slot in range(2):
                pool.dma_start(cols[DECAY:DECAY + NH, 24 + slot:25 + slot], dn_a_log.rearrange("a h -> h a")).then_inc(
                    y_parked[slot], 16)

            def triangle(t, sign, base, op):
                chain.link(nc.gpsimd.memset(t, 1.0))
                chain.put(nc.gpsimd.affine_select(out=t, in_=t, compare_op=op, fill=0.0, base=base,
                                                  pattern=[[-sign, P]], channel_multiplier=sign))

            triangle(tri_suffix[:], 1, 0, ALU.is_ge)
            triangle(tri_incl[:], -1, 0, ALU.is_ge)
            triangle(tri_strict[:], -1, 0, ALU.is_gt)
            for n, h in enumerate(LEVELS):
                nb = P // (2 * h)
                chain.link(nc.gpsimd.memset(lvl_mask[:, n], 0.0))
                upper = lvl_mask[:, n].rearrange("p (b two h) -> p b two h", two=2, h=h)[:, :, 1, :]
                chain.link(nc.gpsimd.memset(upper, 1.0))
                chain.link(nc.gpsimd.affine_select(out=upper, in_=upper, compare_op=ALU.is_ge, fill=0.0, base=0,
                                                   pattern=[[-2 * h, nb], [0, h]], channel_multiplier=1))
                chain.put(nc.gpsimd.affine_select(out=upper, in_=upper, compare_op=ALU.is_ge, fill=0.0, base=h - 1,
                                                  pattern=[[2 * h, nb], [0, h]], channel_multiplier=-1))
            chain.sync()
            nc.gpsimd.memset(cols[0:1, 31:32], 0.0).then_inc(on["consts"], 1)

            for k in range(KT):
                pool.wait_ge(on["x_even"], k // 2 + 1)
                if k % 2:
                    pool.wait_ge(on["x_odd"], k // 2 + 1)
                pool.dma_start(x_park[k], x_t[:, k]).then_inc(on["x_parked"], 16)
            pool.wait_ge(on["x_turned"], KT)
            pool.wait_ge(on["x_ssq"], 1)
            for t in range(MT):
                pool.dma_start(x_tok[:, t], mem_in[0, t * P:(t + 1) * P, :]).then_inc(on["mem_in"], 16)
            pool.wait_ge(on["mem_out"], KT)
            pool.dma_start(m_park.rearrange("k p m -> p k m"), mem_t[:]).then_inc(on["mem_parked"], 16)

            pool.wait_ge(on["mem_parked"], 16)
            pool.wait_ge(on["x_parked"], 16 * KT)
            pool.wait_ge(on["act_ready"], KT)
            pool.wait_ge(on["rstd_ready"], 1)
            pool.wait_ge(on["vec_ready"], 2)
            chain.link(nc.gpsimd.memset(rot[:], 0.0))
            for m0, base, fill in ((0, -CH, -1.0), (CH, 0, 1.0)):
                half = rot[:, m0:m0 + CH]
                chain.put(nc.gpsimd.affine_select(out=half, in_=half, compare_op=ALU.not_equal, fill=fill, base=base,
                                                  pattern=[[-1, CH]], channel_multiplier=1))
            pool.dma_start(pos_row[:], positions).then_inc(on["pos_in"], 16)
            pool.dma_start(freq_col[:], inv_freq).then_inc(on["pos_in"], 16)
            chain.link(nc.gpsimd.iota(dist[:], pattern=[[1, S]], base=0, channel_multiplier=-1,
                                      allow_small_or_imprecise_dtypes=True))
            nc.gpsimd.memset(pos_rowf[:], 0.0).then_inc(on["dist_ready"], 1)

            slabs, heads = Count(5), Count()

            def park_y(tile):
                pool.wait_ge(on["heads_done"], heads.at(2))
                slot = heads.first % 2
                pool.dma_start(y_park[bass.ds(tile, 1), :, :].rearrange("a p s -> p a s"),
                               ytile[:, slot:slot + 1, :]).then_inc(y_parked[slot], 16)
                heads.step()

            def make_gate(g):
                pool.wait_ge(on["gate_sig"], heads.at(1))
                nc.gpsimd.tensor_tensor(gate[:], g, gtmp[:], ALU.mult).then_inc(on["gate_ready"], 1)

            with pool.Fori(0, NH // 2) as i:
                slabs.enter(i, 8)
                heads.enter(i, 2)
                for par in range(2):
                    make_gate(stage[:, par, 3])
                    park_y(i * 2 + (Y_RET + par))
                    slabs.step(4)
            slabs.leave(NH // 2)
            heads.leave(NH // 2)

            with pool.Fori(0, NH // 2) as i:
                slabs.enter(i, 8)
                heads.enter(i, 2)
                for par in range(2):
                    hd = i * 2 + par
                    make_gate(stage[:, par, 3])
                    pool.wait_ge(on["dn_dt"], hd + 1)
                    nc.gpsimd.tensor_tensor(flat3(dn_dt[:]), flat3(dn_dt[:]), every_tile(tri_incl[:]),
                                            ALU.mult).then_inc(on["dn_b1"], 1)
                    pool.wait_ge(on["dn_pair"], hd + 1)
                    for n in range(7):
                        if n == 2:
                            pool.wait_ge(on["dn_x"], hd * 7 + 1)
                        if n >= 3:
                            pool.wait_ge(on["dn_u"], hd * 6 + (n - 2))
                        lvl = lvl_mask[:, 6 - n]
                        nc.gpsimd.tensor_tensor(flat3(dn_ctt[:, n % 2]), flat3(dn_lt[:]), every_tile(lvl),
                                                ALU.mult).then_inc(on["dn_ct"], 1)
                    park_y(i * 2 + (Y_DN + par))
                    slabs.step(4)
            slabs.leave(NH // 2)
            heads.leave(NH // 2)

            slabs.step(2)
            pool.wait_ge(on["heads_done"], heads.at(1))
            pool.dma_start(gla_up[:], gla_w_up[0]).then_inc(on["up_in"], 16)
            for par in range(2):
                for hh in range(2):
                    make_gate(stage[:, par, 4 + hh])
                    park_y(Y_GLA + 2 * par + hh)
                slabs.step(6)

            pool.dma_start(mem_back[:], m_park.rearrange("k p m -> p k m")).then_inc(on["mem_back"], 16)

            def park_kv(ready, base, tiles, dst, i, slot):
                pool.wait_ge(on[ready], i * 2 + (base + slot + 1))
                pool.dma_start(dst[bass.ds(i * 2 + slot, 1), :, :].rearrange("a p s -> p a s"),
                               tiles[:, slot:slot + 1, :]).then_inc(kv_tile_parked[slot], 16)

            keys_beside = {2: ((), (0, 1)), 3: ((2,), (3, 4))}
            for hd in range(NH):
                before, after = keys_beside.get(hd, ((), ()))
                for idx in before:
                    park_kv("slab_out", KV0, kv_t, k_park, idx // 2, idx % 2)
                pool.wait_ge(on["sb_x"], hd + 1)
                for j in range(NT):
                    d = packed(sb_x, j)[:, 0:P]
                    last = nc.gpsimd.affine_select(out=d, in_=d, compare_op=ALU.is_gt, fill=FAR, base=0,
                                                   pattern=[[1, P]], channel_multiplier=-1)
                    last.then_inc(on["sb_masked"], 1)
                for idx in after:
                    park_kv("slab_out", KV0, kv_t, k_park, idx // 2, idx % 2)
                park_y(Y_SB + hd)

            pool.wait_ge(on["heads_done"], 4 * NH + 1)
            for j in range(2):
                pool.wait_ge(y_parked[j], 16 * (2 * NH + 1))
            for q in range(4):
                pool.dma_start(main[:, 4 * q:4 * q + 4], y_park[4 * q:4 * q + 4].rearrange("k p s -> p k s")).then_inc(
                    main_back[q], 16)

            park_kv("slab_out", KV0, kv_t, k_park, 2, 1)
            with pool.Fori(3, KT // 2) as i:
                for slot in range(2):
                    park_kv("slab_out", KV0, kv_t, k_park, i, slot)
            with pool.Fori(0, KT // 2) as i:
                for slot in range(2):
                    park_kv("kv_vout", 0, v_t, v_park, i, slot)

            pool.wait_ge(on["x_parked"], 16 * KT)
            for q in range(4):
                pool.wait_ge(on["act_ready"], KT + 4 * q + 4)
                pool.dma_start(main[:, 4 * q:4 * q + 4], x_park[4 * q:4 * q + 4].rearrange("k p s -> p k s")).then_inc(
                    main_back[q], 16)

            squares = Count()

            def sum_squares(park=False):
                for k in range(KT):
                    if park:
                        pool.wait_ge(on["slab_out"], OUT0 + k + 1)
                        pool.dma_start(x_park[k], main[:, k]).then_inc(on["x_parked"], 16)
                    pool.wait_ge(on["xsq_ready"], squares.at(1))
                    if k == 0:
                        ins = nc.gpsimd.tensor_copy(xacc[:], xsq[:, 0])
                    else:
                        pool.wait_ge(on["xacc_ready"], squares.at())
                        ins = nc.gpsimd.tensor_tensor(xacc[:], xacc[:], xsq[:, k % 2], ALU.add)
                    ins.then_inc(on["xacc_ready"], 1)
                    squares.step()

            sum_squares(park=True)

            for j in range(2):
                pool.wait_ge(kv_tile_parked[j], 16 * KT)
            with pool.Fori(0, NH // 2) as i:
                for par in range(2):
                    pool.wait_ge(on["cx_done"], i * 2 + (par + 1))
                    for dst, src in ((kh, k_park), (vh, v_park)):
                        pool.dma_start(dst[:, par], src[bass.ds(i * 2 * NH + par * NH, NH)].rearrange(
                            "k p m -> p k m")).then_inc(kv_loaded[par], 16)
            pool.wait_ge(on["x_parked"], 2 * 16 * KT)
            for q in range(4):
                pool.wait_ge(on["act_ready"], 3 * KT + 4 * q + 4)
                pool.dma_start(main[:, 4 * q:4 * q + 4], x_park[4 * q:4 * q + 4].rearrange("k p s -> p k s")).then_inc(
                    main_back[q], 16)
            sum_squares()

        @block.tensor
        def _(pe):
            slabs, act, act_out, heads, levels = Count(), Count(), Count(), Count(), Count()
            mm = nc.tensor.matmul

            def hi_lo(ps, wh, wl, xh, xl, first, last):
                mm(ps, wh, xh, start=first, stop=False)
                mm(ps, wh, xl, start=False, stop=False)
                return mm(ps, wl, xh, start=False, stop=last)

            def window(mixer=None, n=S, new_act=False, last_use=False):
                slot = slabs.first % 2
                pe.wait_ge(on["slab_lo"], slabs.at(1))
                if slabs.first >= 2:
                    pe.wait_ge(on["slab_out"], slabs.at(-1))
                wh = w_hi[:, slot].rearrange("p (k n) -> p k n", k=KT)
                wl = w_lo[:, slot].rearrange("p (k n) -> p k n", k=KT)
                running = mixer is not None
                for k in range(KT):
                    if new_act:
                        pe.wait_ge(on["act_ready"], act.at(k + 1))
                    last = hi_lo(G[slot][:, 0:n], wh[:, k], wl[:, k], act_hi[:, k, 0:n], act_lo[:, k, 0:n],
                                 k == 0, k == KT - 1)
                    if k == KT - 1:
                        last.then_inc(on["slab_mul"], 1)
                    elif last_use:
                        last.then_inc(on["act_free"], 1)
                    if running and k >= 3:
                        running = next(mixer) != SEG
                if running:
                    run_segment(mixer)
                if new_act:
                    act.step(KT)
                slabs.step()

            def turn(dst, src, done, n=NT):
                for t in range(n):
                    last = nc.tensor.transpose(dst[:, t * P:(t + 1) * P], src(t), ident[:])
                last.then_inc(on[done], 1)

            def head_starts():
                pe.wait_ge(on["heads_done"], heads.at(1))

            def norm_sum():
                pe.wait_ge(on["sq_ready"], heads.at(1))
                mm(M[1][:], ones[:], sq[:], start=True, stop=True).then_inc(on["norm_sum"], 1)

            def scores(k, q, done):
                for j in range(NT):
                    last = mm(score_ps(j), k[:, j * P:(j + 1) * P], q[:, j * P:S], start=True, stop=True)
                last.then_inc(on[done], 1)

            def attend(weights):
                pe.wait_ge(on["vtok_ready"], heads.at(1))
                for j in range(NT):
                    last = mm(M[0][:, j * P:S], vtok[:, j], packed(weights, j), start=j == 0, stop=j == NT - 1)
                last.then_inc(on["o_ready"], 1)

            pe.wait_ge(on["consts"], 1)
            pe.wait_ge(on["vec_in"], 16 * 8)
            nc.tensor.transpose(G[0][:, 0:V_N], vec_rows[:], ident[0:V_N, 0:V_N])
            nc.tensor.transpose(G[1][:, 0:C_N], conv_rows[:], ident[0:C_N, 0:C_N]).then_inc(on["vec_turned"], 1)
            for t in range(NT):
                pe.wait_ge(x_loaded[t], 16)
            for k in range(KT):
                if k >= 6:
                    pe.wait_ge(on["x_odd" if k % 2 else "x_even"], (k - 6) // 2 + 1)
                turn(M[k % 6], lambda t: x_tok[:, t, k * P:(k + 1) * P], "x_turned")
            pe.wait_ge(on["x_diag"], 1)
            pe.wait_ge(on["x_even"], KT // 2)
            mm(M[0][:], ones[:], diag_r[:].rearrange("p t s -> p (t s)"), start=True, stop=True).then_inc(
                on["x_bcast"], 1)

            def turn_mem():
                pe.wait_ge(on["x_odd"], KT // 2)
                pe.wait_ge(on["mem_scaled"], 1)
                for k in range(KT):
                    if k >= 8 and k % 2 == 0:
                        pe.wait_ge(on["mem_out"], k - 6)
                    for t in range(MT):
                        last = nc.tensor.transpose(M[2 + (k // 2) % 4][:, (k % 2) * NMEM + t * P:][:, 0:P],
                                                   x_tok[:, t, k * P:(k + 1) * P], ident[:])
                    if k % 2:
                        last.then_inc(on["mem_turned"], 1)
                    if k % 4 == 3:
                        yield HOP
                yield SEG

            def tables():
                pe.wait_ge(on["pos_ready"], 1)
                mm(M[0][:], ones[0:1, :], pos_rowf[:], start=True, stop=True).then_inc(on["pos_bcast"], 1)
                yield SEG
                yield SEG
                pe.wait_ge(on["rows_ready"], 1)
                for n, r in enumerate((BETA, DECAY)):
                    for t in range(NT):
                        last = nc.tensor.transpose(M[1 + n][:, t * NH:(t + 1) * NH], rows[r:r + NH, t * P:(t + 1) * P],
                                                   ident[r:r + NH, r:r + NH])
                last.then_inc(on["cols_turned"], 1)
                yield SEG
                yield SEG

            def retention(par):
                q, k, v = (stage[:, par, t] for t in range(3))
                head_starts()
                pe.wait_ge(on["slab_out"], slabs.at())
                mm(M[0][:], rot[:], q, start=True, stop=True)
                mm(M[1][:], rot[:], k, start=True, stop=True).then_inc(on["ret_rot"], 1)
                turn(M[2], lambda t: v[:, t * P:(t + 1) * P], "vt_ready")
                yield SEG
                pe.wait_ge(on["ret_qk"], heads.at(1))
                scores(ret_k, ret_q, "ret_scores")
                yield SEG
                pe.wait_ge(on["ret_w"], heads.at(1))
                attend(ret_wt)
                yield HOP
                yield HOP
                yield HOP
                norm_sum()
                heads.step()
                yield SEG
                yield SEG

            def delta(par, hd):
                v = dn_c[:, 2]
                tile = lambda t, c: t[:, c * P:(c + 1) * P]
                head_starts()
                pe.wait_ge(on["bcast_rows"], hd + 1)
                mm(M[2][:], ones[DECAY:DECAY + NH, :], dn_rows[DECAY:DECAY + NH, :], start=True, stop=True)
                mm(M[3][:], ones[BETA:BETA + NH, :], dn_rows[BETA:BETA + NH, :], start=True, stop=True).then_inc(
                    on["bcast_ps"], 1)
                for _ in range(8):
                    yield HOP
                for n, t in enumerate((dn_uu, dn_xx)):
                    pe.wait_ge(on["dn_sq"], hd * 2 + (n + 1))
                    mm(M[4 + n][:], ones[:], t[:], start=True, stop=True).then_inc(on["dn_l2"], 1)
                yield SEG
                pe.wait_ge(on["dn_qk"], hd + 1)
                turn(M[4], lambda t: v[:, t * P:(t + 1) * P], "vt_ready")
                turn(M[5], lambda t: dn_c[:, 1, t * P:(t + 1) * P], "dn_tok")
                pe.wait_ge(on["dn_b2"], hd + 1)
                for c in range(NT):
                    mm(tile(M[2], c), tile(dn_c[:, 1], c), tile(dn_c[:, 1], c), start=True, stop=True)
                    last = mm(tile(M[3], c), tile(dn_c[:, 1], c), tile(dn_c[:, 0], c), start=True, stop=True)
                last.then_inc(on["dn_gram"], 1)
                yield HOP
                yield HOP
                pe.wait_ge(on["dn_bvk"], hd + 1)
                pe.wait_ge(on["dn_ct"], hd * 7 + 1)
                turn(M[4], lambda t: dn_ctt[:, 0, t * P:(t + 1) * P], "dn_c1t")
                yield HOP
                for n in range(1, 7):
                    pe.wait_ge(on["dn_ct"], hd * 7 + (n + 1))
                    pe.wait_ge(on["dn_x"], hd * 7 + n)
                    for c in range(NT):
                        last = mm(tile(M[2], c), tile(dn_ctt[:, n % 2], c), tile(dn_xx, c), start=True, stop=True)
                    last.then_inc(on["dn_u"], 1)
                    yield HOP
                    yield HOP
                    pe.wait_ge(on["dn_uev"], hd * 6 + n)
                    for c in range(NT):
                        if n < 6:
                            mm(tile(M[3], c), tile(dn_xt, c), tile(dn_uu, c), start=True, stop=True)
                        last = mm(tile(M[4], c), tile(dn_uu, c), tile(dn_xt, c), start=True, stop=True)
                    last.then_inc(on["dn_v"], 1)
                    yield SEG if n in (2, 5) else HOP
                pe.wait_ge(on["dn_x"], hd * 7 + 7)
                for c in range(NT):
                    mm(tile(M[2], c), tile(dn_xt, c), tile(dn_bv, c), start=True, stop=True)
                    last = mm(tile(M[3], c), tile(dn_kbe, c), tile(dn_xt, c), start=True, stop=True)
                last.then_inc(on["dn_uw"], 1)
                yield HOP
                pe.wait_ge(on["dn_uwev"], hd + 1)
                pe.wait_ge(on["dn_qg"], hd + 1)
                for c in range(NT):
                    if c:
                        pe.wait_ge(on["dn_state"], hd * 3 + c)
                        mm(M[4][:, 0:P], tile(dn_wt, c), dn_st[:], start=True, stop=True).then_inc(on["dn_ws"], 1)
                        mm(tile(M[0], c), dn_st[:], tile(dn_qg, c), start=True, stop=False)
                        pe.wait_ge(on["dn_vnew"], hd * 3 + c)
                    v_new = dn_vn[:] if c else tile(dn_uu, 0)
                    last = mm(tile(M[0], c), v_new, tile(dn_at, c), start=c == 0, stop=True)
                    if c < NT - 1:
                        mm(M[5][:, 0:P], tile(dn_kdec, c), v_new, start=True, stop=True).then_inc(on["dn_ds"], 1)
                        yield HOP
                last.then_inc(on["o_ready"], 1)
                yield HOP
                norm_sum()
                heads.step()
                yield SEG

            def gla_logits():
                head_starts()
                pe.wait_ge(on["up_in"], 16)
                for p in range(2):
                    mm(M[p][:], gla_up[:, p * P:(p + 1) * P], rows[0:RANK, :], start=True, stop=True).then_inc(
                        on["gla_z"], 1)
                yield SEG
                yield SEG

            def gla(par):
                half = lambda t, hh: t[hh * DK:(hh + 1) * DK]
                cut = lambda t, a, b: t[:, a * P:b * P]
                k = stage[:, par, 1]
                head_starts()
                pe.wait_ge(on["gla_qs"], par + 1)
                for hh in range(2):
                    for c in range(NT):
                        last = mm(cut(M[2 + hh], c, c + 1), cut(half(k, hh), c, c + 1),
                                  cut(half(gla_qs, hh), c, c + 1), start=True, stop=True)
                last.then_inc(on["gla_diag"], 1)
                turn(M[0], lambda t: stage[:, par, 2, t * P:(t + 1) * P], "vt_ready")
                yield HOP
                for n in range(9):
                    qk = gla_qk[:, n % 2]
                    pe.wait_ge(on["gla_qe"], par * 9 + n + 1)
                    ps = [M[4 + hh] if n % 2 == 0 else M[2 + hh] for hh in range(2)]
                    if n == 1:
                        pe.wait_ge(on["gla_lvout"], par * 8 + 1)
                    elif n in (2, 3):
                        pe.wait_ge(on["gla_topout"], par * 2 + n - 1)
                    elif n >= 4:
                        pe.wait_ge(on["gla_lvout"], par * 8 + n - 2)
                    for hh in range(2):
                        if n == 0:
                            for c in range(2):
                                last = mm(cut(ps[hh], 2 * c, 2 * c + 2), cut(half(qk, hh), c, c + 1),
                                          cut(half(qk, hh), 2, 4), start=True, stop=True)
                        elif n == 1:
                            for c in range(2):
                                last = mm(cut(ps[hh], c, c + 1), cut(half(qk, hh), 2 * c, 2 * c + 1),
                                          cut(half(qk, hh), 2 * c + 1, 2 * c + 2), start=True, stop=True)
                        else:
                            for c in range(NT):
                                last = mm(cut(ps[hh], c, c + 1), cut(half(qk, hh), c, c + 1),
                                          cut(half(qk, hh), c, c + 1), start=True, stop=True)
                    last.then_inc(on["gla_lv"], 1)
                    yield SEG if n in (1, 3, 5, 7) else HOP
                for hh in range(2):
                    if hh:
                        head_starts()
                        turn(M[1], lambda t: stage[:, par, 3, t * P:(t + 1) * P], "vt_ready")
                        yield HOP
                        yield HOP
                    pe.wait_ge(on["gla_lvout"], par * 8 + 8)
                    pe.wait_ge(on["gla_topout"], par * 2 + 2)
                    pe.wait_ge(on["vtok_ready"], heads.at(1))
                    s, o = gla_s[:, hh], gla_o[:, hh]
                    for c in range(NT):
                        for kt in range(c):
                            at = (0, 3 * P, 5 * P)[kt] + (c - 1 - kt) * P
                            mm(cut(M[0], c, c + 1), vtok[:, kt], o[:, at:at + P], start=kt == 0, stop=False)
                        last = mm(cut(M[0], c, c + 1), vtok[:, c], cut(s, c, c + 1), start=c == 0, stop=True)
                    last.then_inc(on["o_ready"], 1)
                    yield HOP
                    yield HOP
                    norm_sum()
                    heads.step()
                    yield SEG

            def stick(par):
                for hh in range(2):
                    q, k, v = (stage[:, par, 3 * hh + t] for t in range(3))
                    hd = 2 * par + hh
                    head_starts()
                    if hh == 0:
                        pe.wait_ge(on["slab_out"], slabs.at())
                    turn(M[2], lambda t: v[:, t * P:(t + 1) * P], "vt_ready")
                    scores(k, q, "sb_scores")
                    yield SEG
                    pe.wait_ge(on["sb_lk"], hd + 1)
                    for i in range(NT):
                        bank, at = SC[i]
                        for j in range(i, NT):
                            w = WID[j]
                            last = mm(M[bank][:, at + (j - i) * P:at + WID[i]], (tri_suffix if j == i else ones)[:],
                                      packed(sb_m, j), start=j == i, stop=j == NT - 1)
                    last.then_inc(on["sb_cum"], 1)
                    yield SEG
                    pe.wait_ge(on["sb_w"], hd + 1)
                    attend(sb_x)
                    yield HOP
                    yield HOP
                    norm_sum()
                    heads.step()
                    yield SEG

            window(turn_mem(), new_act=True)
            mixer = tables()
            for _ in range(4):
                window(mixer)
            with pe.Fori(0, NH // 2) as i:
                slabs.enter(i, 8)
                heads.enter(i, 2)
                for par in range(2):
                    mixer = retention(par)
                    for _ in range(4):
                        window(mixer)
            slabs.leave(NH // 2)
            heads.leave(NH // 2)
            with pe.Fori(0, NH // 2) as i:
                slabs.enter(i, 8)
                heads.enter(i, 2)
                for par in range(2):
                    mixer = delta(par, i * 2 + par)
                    for _ in range(4):
                        window(mixer)
            slabs.leave(NH // 2)
            heads.leave(NH // 2)
            mixer = gla_logits()
            for _ in range(2):
                window(mixer)
            for par in range(2):
                mixer = gla(par)
                for _ in range(6):
                    window(mixer)
            mixer = stick(0)
            for n in range(6):
                window(mixer)

            mixer = stick(1)
            pe.wait_ge(on["mem_split"], 1)
            for _ in range(6):
                window(mixer, n=NMEM)
            with pe.Fori(0, (KT - 6) // 2) as i:
                slabs.enter(i, 2)
                for _ in range(2):
                    window(n=NMEM)
            slabs.leave((KT - 6) // 2)

            def turn_values(idx, slot):
                pe.wait_ge(on["slab_out"], slabs.at())
                for t in range(MT):
                    last = nc.tensor.transpose(M[slot][:, t * P:(t + 1) * P], kv_t[:, slot, t * P:(t + 1) * P], ident[:])
                last.then_inc(on["kv_turned"], 1)
                yield SEG

            window(n=NMEM)
            window(turn_values(0, 0), n=NMEM)
            with pe.Fori(1, KT // 2 - 1) as i:
                slabs.enter(i - 1, 2)
                window(turn_values(i * 2 - 1, 1), n=NMEM)
                window(turn_values(i * 2, 0), n=NMEM)
            slabs.leave(KT // 2 - 2)
            window(turn_values(KT - 3, 1), n=NMEM)
            window(turn_values(KT - 2, 0), n=NMEM, last_use=True)
            window(turn_values(KT - 1, 1), new_act=True)

            def matrix(n, first=True):
                with pe.Fori(0, n // 2) as i:
                    slabs.enter(i, 2)
                    window()
                    window()
                slabs.leave(n // 2)

            def total(n):
                for _ in range(6):
                    yield HOP
                pe.wait_ge(on["xacc_ready"], n * KT)
                mm(M[5][:], ones[:], xacc[:], start=True, stop=True).then_inc(on["x_total"], 1)
                yield SEG

            matrix(KT - 2)
            window(last_use=True)

            def attention(par, hd):
                tile = lambda t, c: t[:, c * P:(c + 1) * P]
                pe.wait_ge(on["slab_out"], slabs.at())
                pe.wait_ge(on["cx_done"], hd + 2)
                pe.wait_ge(kv_loaded[par], 32 * (hd // 2 + 1))
                
                for st in range(NT):
                    for k in range(NH):
                        last = mm(M[st // 2][:, (st % 2) * NMEM:(st % 2 + 1) * NMEM], tile(cstage[:, par, k], st),
                                  kh[:, par, k], start=k == 0, stop=k == NH - 1)
                last.then_inc(on["cx_scores"], 1)
                for _ in range(6):
                    yield HOP
                pe.wait_ge(on["cx_p"], hd + 1)
                for st in range(NT):
                    for mt in range(MT):
                        last = nc.tensor.transpose(tile(M[2 + mt], st), prob[:, st, mt * P:(mt + 1) * P], ident[:])
                last.then_inc(on["cx_pt"], 1)
                yield SEG
                pe.wait_ge(on["cx_ptok"], hd + 1)
                for k in range(NH):
                    bank = (4, 5, 0, 1)[k]
                    for mt in range(MT):
                        last = mm(M[bank][:], vh[:, par, k, mt * P:(mt + 1) * P], prob_t[:, mt], start=mt == 0,
                                  stop=mt == MT - 1)
                    last.then_inc(on["cx_o"], 1)
                yield SEG
                yield SEG
                yield SEG

            window(total(1), new_act=True)
            for _ in range(3):
                window()
            for hd in range(NH - 1):
                mixer = attention(hd % 2, hd)
                for n in range(4):
                    window(mixer, last_use=hd == NH - 2 and n == 3)
            mixer = attention((NH - 1) % 2, NH - 1)
            for _ in range(4):
                run_segment(mixer)

            window(new_act=True)
            matrix(KT - 2)
            window(last_use=True)

            def down(c):
                slot = slabs.first % 2
                pe.wait_ge(on["slab_lo"], slabs.at(1))
                pe.wait_ge(on["slab_out"], slabs.at(-1))
                wh = w_hi[:, slot].rearrange("p (k n) -> p k n", k=MC)
                wl = w_lo[:, slot].rearrange("p (k n) -> p k n", k=MC)
                for j in range(2):
                    for k in range(MC):
                        pe.wait_ge(on["u_ready"], c * MC + (k + 1))
                        last = hi_lo(M[2 * slot + j][:], wh[:, k, j * P:(j + 1) * P], wl[:, k, j * P:(j + 1) * P],
                                     u_hi[:, k], u_lo[:, k], k == 0, k == MC - 1)
                last.then_inc(on["slab_mul"], 1)
                slabs.step()

            window(total(2), new_act=True)
            for _ in range(MC - 1):
                window()
            for _ in range(MC):
                down(0)
            with pe.Fori(1, NCH) as c:
                slabs.enter(c - 1, 2 * MC)
                for _ in range(MC):
                    window()
                for _ in range(MC):
                    down(c)
            slabs.leave(NCH - 1)

            pe.wait_ge(on["slab_out"], slabs.at())
            for k in range(KT):
                pe.wait_ge(on["fin_sq"], k + 1)
                mm(M[5][:], ones[:], xsq[:, k % 2], start=k == 0, stop=k == KT - 1).then_inc(on["fin_sum"], 1)
            for n in range(NT * 4):
                t, g = n // 4, n % 4
                if t == 0:
                    pe.wait_ge(on["fin_x"], 4 * g + 4)
                if n >= 4:
                    pe.wait_ge(on["fin_odd" if n % 2 else "fin_even"], (n - 4) // 2 + 1)
                turn(M[n % 4], lambda k: main[:, 4 * g + k, t * P:(t + 1) * P], "fin_turned")

        @block.scalar
        def _(act):
            chain = Chain(act, on["act_chain"])
            slabs, heads = Count(), Count()
            fn = nc.scalar.activation
            RET_LINKS, DN_LINKS = 3, 13

            def split_hi():
                nxt = slabs.first + 1
                slot = nxt % 2
                act.wait_ge(raw_in[slot], slabs.at(1) * 8 + 8 * slot)
                if nxt >= 2:
                    act.wait_ge(on["slab_mul"], slabs.at())
                fn(w_hi[:, slot], w_raw[:, slot], ACT.Copy).then_inc(on["slab_hi"], 1)

            def window(mixer=None, last=False):
                if not last:
                    split_hi()
                run_segment(mixer)
                slabs.step()

            def silu_part(t):
                chain.link(fn(t, t, ACT.Exp, scale=-1.0))
                chain.link(fn(t, t, ACT.Ln, bias=1.0))
                return fn(t, t, ACT.Exp, scale=-1.0)

            def rsqrt(dst, src, scale, eps=True, power=-0.5):
                chain.link(fn(dst, src, ACT.Ln, scale=scale, bias=eps_col[:]))
                return fn(dst, dst, ACT.Exp, scale=power)

            def head_starts():
                act.wait_ge(on["heads_done"], heads.at(1))

            def values(bank):
                act.wait_ge(on["vt_ready"], heads.at(1))
                fn(vtok[:].rearrange("p t s -> p (t s)"), bank[:], ACT.Copy).then_inc(on["vtok_ready"], 1)

            def gate_sigmoid(gated):
                act.wait_ge(on["gate_clamped"], gated + 1)
                silu_part(gtmp[:]).then_inc(on["gate_sig"], 1)

            def norm():
                act.wait_ge(on["o_ready"], heads.at(1))
                fn(sq[:], M[0][:], ACT.Square).then_inc(on["sq_ready"], 1)
                act.wait_ge(on["norm_sum"], heads.at(1))
                rsqrt(nrm[:], M[1][:], 1.0 / P).then_inc(on["norm_ready"], 1)
                heads.step()

            nc.scalar.preload_act_table_set("natural_log_exp_and_others")
            for t in range(NT):
                act.wait_ge(x_loaded[t], 16)
                if t >= 2:
                    act.wait_ge(chain.sem, t - 1)
                chain.put(fn(mem_t[:].rearrange("p k m -> p (k m)")[:, (t % 2) * D:(t % 2 + 1) * D], x_tok[:, t],
                             ACT.Square, accum_out=cols[:, t:t + 1]))
            act.wait_ge(on["consts"], 1)
            chain.sync()
            chain.link(rsqrt(cols[:, 4:8], cols[:, 0:4], 1.0 / D))
            nc.scalar.copy(cols[:, 8:12], cols[:, 4:8]).then_inc(on["x_ssq"], 1)
            act.wait_ge(on["vec_turned"], 1)
            fn(vecs[:], G[0][:, 0:V_N], ACT.Copy).then_inc(on["vec_ready"], 1)
            fn(convs[:], G[1][:, 0:C_N], ACT.Copy).then_inc(on["vec_ready"], 1)
            for k in range(0, KT, 2):
                act.wait_ge(on["x_turned"], k + 1)
                fn(x_t[:, k], M[k % 6][:], ACT.Copy).then_inc(on["x_even"], 1)
            act.wait_ge(on["special_in"], 48)
            fn(w_hi[:, 0], w_raw[:, 0], ACT.Copy).then_inc(on["slab_hi"], 1)
            act.wait_ge(on["vec_ready"], 2)
            for k in range(KT):
                act.wait_ge(on["x_odd" if k % 2 else "x_even"], k // 2 + 1)
                fn(act_hi[:, k], x_t[:, k], ACT.Copy, scale=vecs[:, V_MIX + k:V_MIX + k + 1]).then_inc(on["xg_hi"], 1)
            act.wait_ge(on["x_bcast"], 1)
            fn(rstd[:], M[0][:], ACT.Copy).then_inc(on["rstd_ready"], 1)

            def mem_norm():
                act.wait_ge(on["mem_in"], 16 * MT)
                for t in range(MT):
                    chain.put(fn(mem_t[:].rearrange("p k m -> p (k m)")[:, t * D:(t + 1) * D], x_tok[:, t],
                                 ACT.Square, accum_out=cols[:, 12 + t:13 + t]))
                chain.sync()
                chain.link(rsqrt(cols[:, 14:14 + MT], cols[:, 12:12 + MT], 1.0 / D))
                for t in range(MT):
                    chain.put(fn(x_tok[:, t], x_tok[:, t], ACT.Copy, scale=cols[:, 14 + t:15 + t]))
                chain.sync()
                nc.scalar.copy(cols[:, 16:17], cols[:, 14:15]).then_inc(on["mem_scaled"], 1)
                for k in range(KT):
                    act.wait_ge(on["mem_turned"], k // 2 + 1)
                    fn(mem_t[:, k], M[2 + (k // 2) % 4][:, (k % 2) * NMEM:(k % 2 + 1) * NMEM], ACT.Copy,
                       scale=vecs[:, V_MEM + k:V_MEM + k + 1]).then_inc(on["mem_out"], 1)
                yield SEG

            def tables():
                b, a = slice(BETA, BETA + NH), slice(DECAY, DECAY + NH)
                act.wait_ge(on["small_in"], 32)
                act.wait_ge(on["rows_out"], 1)
                chain.put(fn(sq[b], rows[b], ACT.Exp, scale=-1.0))
                chain.put(fn(cols[a, 22:23], cols[a, 20:21], ACT.Exp))
                chain.link(fn(gtmp[a], rows[a], ACT.Identity, bias=cols[a, 21:22]))
                chain.link(fn(sq[a], gtmp[a], ACT.Abs))
                chain.link(fn(sq[a], sq[a], ACT.Exp, scale=-1.0))
                fn(sq[a], sq[a], ACT.Ln, bias=1.0).then_inc(on["rows_act"], 1)
                yield SEG
                act.wait_ge(on["dist_ready"], 1)
                chain.link(fn(dist[:], dist[:], ACT.Abs))
                for h in range(NH):
                    last = fn(ret_dec[:, h], dist[:], ACT.Exp, scale=LOG_GAMMA[h])
                    if h < NH - 1:
                        chain.put(last)
                last.then_inc(on["dec_exp"], 1)
                chain.sync()
                yield SEG
                act.wait_ge(on["ang_ready"], 1)
                chain.put(fn(sin_t[:], sin_t[:], ACT.Sin))
                chain.link(fn(cos_t[:], cos_t[:], ACT.Sin))
                nc.scalar.copy(cols[:, 17:18], cols[:, 16:17]).then_inc(on["trig_ready"], 1)
                nc.scalar.preload_act_table_set("natural_log_exp_and_others")
                yield SEG
                act.wait_ge(on["cols_turned"], 1)
                for n in range(2):
                    last = fn(rcols[:, :, n * NH:(n + 1) * NH], M[1 + n][:, 0:NT * NH].rearrange("p (t h) -> p t h", h=NH),
                              ACT.Copy)
                last.then_inc(on["cols_ready"], 1)
                yield SEG

            def retention():
                head_starts()
                values(M[2])
                gate_sigmoid(heads.at())
                yield SEG
                yield SEG
                norm()
                yield SEG
                yield SEG

            def delta(hd):
                head_starts()
                act.wait_ge(on["bcast_ps"], hd + 1)
                fn(dn_gb[:], M[2][:], ACT.Copy).then_inc(on["dn_gbev"], 1)
                for t in range(3):
                    act.wait_ge(on["dn_clamped"], hd * 3 + (t + 1))
                    silu_part(dn_s[:, t]).then_inc(on["dn_sig"], 1)
                for n, t in enumerate((dn_uu, dn_xx)):
                    act.wait_ge(on["dn_silu"], hd * 3 + (n + 1))
                    fn(t[:], dn_c[:, n], ACT.Square).then_inc(on["dn_sq"], 1)
                for n, t in enumerate((dn_uu, dn_xx)):
                    act.wait_ge(on["dn_l2"], hd * 2 + (n + 1))
                    rsqrt(t[:], M[4 + n][:], 1.0).then_inc(on["dn_inv"], 1)
                act.wait_ge(on["dn_cols"], hd + 1)
                chain.put(fn(dn_cols[:, 0:3].rearrange("p a t -> p (a t)"), dn_cols[:, 4:7].rearrange("p a t -> p (a t)"),
                             ACT.Exp))
                chain.sync()
                nc.scalar.copy(cols[:, 18:19], cols[:, 17:18]).then_inc(on["dn_colexp"], 1)
                act.wait_ge(on["dn_dd"], hd + 1)
                fn(dn_dt[:], dn_dt[:], ACT.Exp).then_inc(on["dn_dt"], 1)
                yield SEG
                gate_sigmoid(heads.at())
                fn(dn_gb[:], dn_gb[:], ACT.Exp).then_inc(on["dn_eg"], 1)
                for n in range(1, 7):
                    act.wait_ge(on["dn_u"], hd * 6 + n)
                    fn(dn_uu[:], M[2][:], ACT.Copy).then_inc(on["dn_uev"], 1)
                    if n in (2, 5):
                        yield SEG
                act.wait_ge(on["dn_uw"], hd + 1)
                chain.put(fn(dn_uu[:], M[2][:], ACT.Copy))
                chain.sync()
                fn(dn_wt[:], M[3][:], ACT.Copy).then_inc(on["dn_uwev"], 1)
                norm()
                yield SEG

            def gla_logits():
                head_starts()
                for p in range(2):
                    act.wait_ge(on["gla_z"], p + 1)
                    chain.link(fn(gla_t[:, p], M[p][:], ACT.Identity, bias=convs[:, C_BUP + p:C_BUP + p + 1]))
                    chain.link(fn(gla_e[:, p], gla_t[:, p], ACT.Abs))
                    chain.link(fn(gla_e[:, p], gla_e[:, p], ACT.Exp, scale=-1.0))
                    fn(gla_e[:, p], gla_e[:, p], ACT.Ln, bias=1.0).then_inc(on["gla_l"], 1)
                yield SEG
                yield SEG

            def gla(par):
                head_starts()
                values(M[0])
                gate_sigmoid(heads.at())
                for n in range(9):
                    act.wait_ge(on["gla_d"], par * 9 + n + 1)
                    fn(gla_e[:, n % 2], gla_e[:, n % 2], ACT.Exp, scale=1.0 / 16).then_inc(on["gla_e"], 1)
                    if n < 2:
                        act.wait_ge(on["gla_lv"], par * 9 + n + 1)
                        for hh in range(2):
                            bank, o = M[4 - 2 * n + hh], gla_o[:, hh]
                            if n == 0:
                                last = fn(o[:, P:5 * P], bank[:], ACT.Copy)
                            else:
                                chain.put(fn(o[:, 0:P], bank[:, 0:P], ACT.Copy))
                                last = fn(o[:, 5 * P:6 * P], bank[:, P:2 * P], ACT.Copy)
                            if hh == 0:
                                chain.put(last)
                        chain.sync()
                        last.then_inc(on["gla_topout"], 1)
                    if n in (1, 3, 5, 7):
                        yield SEG
                norm()
                yield SEG
                head_starts()
                values(M[1])
                gate_sigmoid(heads.at())
                norm()
                yield SEG

            def stick(par):
                for hh in range(2):
                    hd = 2 * par + hh
                    head_starts()
                    values(M[2])
                    act.wait_ge(on["sb_scores"], hd + 1)
                    parts = ((0, 512, M[3]), (OFF[1], WID[1], M[4]), (OFF[2], WID[2] + WID[3], M[5]))
                    for at, n, bank in parts:
                        last = fn(sb_x[:, at:at + n], bank[:, 0:n], ACT.Copy, scale=QSCALE)
                        if at < OFF[2]:
                            chain.put(last)
                    chain.sync()
                    last.then_inc(on["sb_x"], 1)
                    act.wait_ge(on["sb_masked"], 4 * hd + 4)
                    chain.link(fn(sb_l[:], sb_x[:], ACT.Abs))
                    chain.link(fn(sb_l[:], sb_l[:], ACT.Exp, scale=-1.0))
                    fn(sb_l[:], sb_l[:], ACT.Ln, bias=1.0).then_inc(on["sb_l"], 1)
                    yield SEG
                    act.wait_ge(on["sb_z"], hd + 1)
                    fn(sb_x[:], sb_x[:], ACT.Exp).then_inc(on["sb_w"], 1)
                    yield SEG
                    norm()
                    yield SEG

            window(mem_norm())
            mixer = tables()
            for _ in range(4):
                window(mixer)
            with act.Fori(0, NH // 2) as i:
                slabs.enter(i, 8)
                heads.enter(i, 2)
                chain.count.enter(i, 2 * RET_LINKS)
                for par in range(2):
                    mixer = retention()
                    for _ in range(4):
                        window(mixer)
            slabs.leave(NH // 2)
            heads.leave(NH // 2)
            chain.count.leave(NH // 2)
            with act.Fori(0, NH // 2) as i:
                slabs.enter(i, 8)
                heads.enter(i, 2)
                chain.count.enter(i, 2 * DN_LINKS)
                for par in range(2):
                    mixer = delta(i * 2 + par)
                    for _ in range(4):
                        window(mixer)
            slabs.leave(NH // 2)
            heads.leave(NH // 2)
            chain.count.leave(NH // 2)
            mixer = gla_logits()
            for _ in range(2):
                window(mixer)
            for par in range(2):
                mixer = gla(par)
                for _ in range(6):
                    window(mixer)
            mixer = stick(0)
            for _ in range(6):
                window(mixer)

            act.wait_ge(on["slab_mul"], slabs.at())
            act.wait_ge(on["mem_back"], 16)
            fn(act_hi[:, :, 0:NMEM], mem_back[:], ACT.Copy).then_inc(on["mem_hi"], 1)
            mixer = stick(1)
            for _ in range(6):
                window(mixer)
            with act.Fori(0, (KT - 6) // 2) as i:
                slabs.enter(i, 2)
                window()
                window()
            slabs.leave((KT - 6) // 2)

            def take_values(idx, slot):
                act.wait_ge(on["kv_turned"], idx + 1)
                act.wait_ge(kv_tile_parked[slot], (idx - slot) * 8 + 16 * (KT // 2))
                fn(v_t[:, slot], M[slot][:, 0:NMEM], ACT.Copy).then_inc(on["kv_vout"], 1)
                yield SEG

            window()
            window(take_values(0, 0))
            with act.Fori(1, KT // 2) as i:
                slabs.enter(i - 1, 2)
                window(take_values(i * 2 - 1, 1))
                window(take_values(i * 2, 0))
            slabs.leave(KT // 2 - 1)

            uses = Count()
            parts = Count()

            def activations(gain=None):
                for k in range(KT):
                    if k < KT - 1:
                        act.wait_ge(on["act_free"], (KT - 1) * uses.n + k + 1)
                    else:
                        act.wait_ge(on["slab_mul"], slabs.at())
                    yield k
                    scale = {} if gain is None else {"scale": vecs[:, gain + k:gain + k + 1]}
                    fn(act_hi[:, k], main[:, k], ACT.Copy, **scale).then_inc(on["xg_hi"], 1)
                uses.step()

            squares = Count()

            def square(k, ready):
                act.wait_ge(on["slab_out"], ready)
                if squares.n >= 2:
                    act.wait_ge(on["xacc_ready"], squares.n - 1)
                fn(xsq[:, k % 2], main[:, k], ACT.Square).then_inc(on["xsq_ready"], 1)
                squares.step()

            for k in activations():
                if k % 4 == 0:
                    act.wait_ge(main_back[k // 4], 16)
            run_segment(take_values(KT - 1, 1))
            window()
            for m in range(KT - 1):
                split_hi()
                square(m, slabs.at())
                slabs.step()
            square(KT - 1, slabs.at())
            for k in activations(V_CROSS):
                pass
            split_hi()
            act.wait_ge(on["x_total"], 1)
            rsqrt(rstd[:], M[5][:], 1.0 / D).then_inc(on["x_rstd"], 1)
            slabs.step()

            def attention(hd):
                act.wait_ge(on["cx_max"], hd + 1)
                for st in range(NT):
                    last = fn(prob[:, st], M[st // 2][:, (st % 2) * NMEM:(st % 2 + 1) * NMEM], ACT.Exp, scale=CSCALE,
                              bias=ccols[:, 1, st:st + 1], accum_out=ccols[:, 2, st:st + 1])
                    chain.put(last)
                chain.sync()
                nc.scalar.copy(cols[:, 19:20], cols[:, 18:19]).then_inc(on["cx_exp"], 1)
                act.wait_ge(on["cx_pt"], hd + 1)
                chain.put(fn(prob_t[:, 0], M[2][:], ACT.Copy))
                chain.sync()
                fn(prob_t[:, 1], M[3][:], ACT.Copy).then_inc(on["cx_ptok"], 1)
                yield SEG
                act.wait_ge(on["x_parked"], 2 * 16 * KT)
                for k in range(NH):
                    act.wait_ge(on["cx_o"], NH * hd + k + 1)
                    last = fn(main[:, NH * hd + k], M[(4, 5, 0, 1)[k]][:], ACT.Copy)
                    if k < NH - 1:
                        chain.put(last)
                chain.sync()
                last.then_inc(on["cx_done"], 1)
                yield SEG
                yield SEG
                yield SEG

            nc.scalar.copy(cols[:, 19:20], cols[:, 18:19]).then_inc(on["cx_done"], 2)
            for _ in range(3):
                window()
            for hd in range(NH - 1):
                mixer = attention(hd)
                for _ in range(4):
                    window(mixer)
            mixer = attention(NH - 1)
            for _ in range(4):
                run_segment(mixer)
            for k in activations():
                if k % 4 == 0:
                    act.wait_ge(on["cx_done"], k // 4 + 3)
            window()
            for m in range(KT - 1):
                split_hi()
                square(m, slabs.at())
                slabs.step()
            square(KT - 1, slabs.at())
            for k in activations(V_MLP):
                pass
            split_hi()
            act.wait_ge(on["x_total"], 2)
            rsqrt(rstd[:], M[5][:], 1.0 / D, power=-1.0).then_inc(on["x_rstd"], 1)
            slabs.step()

            def hidden(n, j):
                act.wait_ge(on["slab_mul"], slabs.at())
                fn(relu[:, j % 2], G[(slabs.first - 1) % 2][:], ACT.Relu).then_inc(on["mlp_relu"], 1)
                act.wait_ge(on["slab_out"], slabs.at())
                fn(u_hi[:, j], uf[:, j % 2], ACT.Copy).then_inc(on["mlp_uhi"], 1)

            def chunk(c, first, last):
                for w in range(2 * MC):
                    if w == 0 and first:
                        continue
                    if not (last and w == 2 * MC - 1):
                        split_hi()
                    if 1 <= w <= MC:
                        hidden(c * MC + (w - 1), w - 1)
                    slabs.step()

            chunk(0, True, False)
            with act.Fori(1, NCH - 1) as c:
                slabs.enter(c - 1, 2 * MC)
                chunk(c, False, False)
            slabs.leave(NCH - 2)
            chunk(NCH - 1, False, True)

            for k in range(KT):
                act.wait_ge(on["slab_out"], slabs.at())
                if k >= 2:
                    act.wait_ge(on["fin_sum"], k - 1)
                fn(xsq[:, k % 2], main[:, k], ACT.Square).then_inc(on["fin_sq"], 1)
            act.wait_ge(on["fin_sum"], KT)
            rsqrt(rstd[:], M[5][:], 1.0 / D).then_inc(on["fin_rstd"], 1)
            for n in range(0, NT * 4, 2):
                t, g = n // 4, n % 4
                act.wait_ge(on["fin_turned"], n + 1)
                if t >= 2:
                    act.wait_ge(out_done[t % 2], 16 * (t // 2))
                fn(w_raw[:, t % 2, g * S:(g + 1) * S], M[n % 4][:], ACT.Copy).then_inc(on["fin_even"], 1)

        @block.vector
        def _(dve):
            chain = Chain(dve, on["dve_chain"])
            slabs, heads, parked = Count(), Count(), Count()
            v = nc.vector
            tt, ts, stt = v.tensor_tensor, v.tensor_scalar, v.scalar_tensor_tensor
            RET_LINKS, DN_LINKS = 6, 23
            f32 = lambda t: t.bitcast(F32)

            def split_lo():
                slot = (slabs.first + 1) % 2
                dve.wait_ge(on["slab_hi"], slabs.at(2))
                tt(w_lo[:, slot], w_raw[:, slot], f32(w_hi[:, slot]), ALU.subtract).then_inc(on["slab_lo"], 1)

            def evict_scaled(dst):
                dve.wait_ge(on["slab_mul"], slabs.at())
                tt(dst, G[(slabs.first - 1) % 2][:], rstd[:], ALU.mult).then_inc(on["slab_out"], 1)

            def window(mixer, dst):
                evict_scaled(dst)
                split_lo()
                dve.wait_ge(on["slab_out"], slabs.at())
                run_segment(mixer)
                slabs.step()

            def y_out(tile, slot, hg, gated=True):
                gain = vecs[:, bass.ds(tile + V_HEAD, 1)]
                dve.wait_ge(on["norm_ready"], hg + 1)
                dve.wait_ge(y_parked[slot], hg * 8 + (16 - 8 * slot))
                if gated:
                    chain.link(stt(out=nrm[:], in0=M[0][:], scalar=gain, in1=nrm[:], op0=ALU.mult, op1=ALU.mult))
                    dve.wait_ge(on["gate_ready"], hg + 1)
                    tt(ytile[:, slot], nrm[:], gate[:], ALU.mult).then_inc(on["heads_done"], 1)
                else:
                    stt(out=ytile[:, slot], in0=M[0][:], scalar=gain, in1=nrm[:], op0=ALU.mult,
                        op1=ALU.mult).then_inc(on["heads_done"], 1)

            def clamp_gate(g):
                ts(gtmp[:], g, GATE_FLOOR, None, ALU.max).then_inc(on["gate_clamped"], 1)

            v.memset(w_raw[:, 0], 0.0).then_inc(on["raw_zero"], 1)
            v.memset(cols[0:1, 30:31], 0.0).then_inc(on["heads_done"], 1)
            dve.wait_ge(on["consts"], 1)
            dve.wait_ge(on["x_ssq"], 1)
            for t in range(NT):
                last = ts(diag_r[:, t], ident[:], cols[:, 8 + t:9 + t], None, ALU.mult)
            last.then_inc(on["x_diag"], 1)
            for k in range(1, KT, 2):
                dve.wait_ge(on["x_turned"], k + 1)
                v.tensor_copy(x_t[:, k], M[k % 6][:]).then_inc(on["x_odd"], 1)
            dve.wait_ge(on["slab_hi"], 1)
            tt(w_lo[:, 0], w_raw[:, 0], f32(w_hi[:, 0]), ALU.subtract).then_inc(on["slab_lo"], 1)
            dve.wait_ge(on["vec_ready"], 2)
            for k in range(KT):
                dve.wait_ge(on["xg_hi"], k + 1)
                stt(out=act_lo[:, k], in0=x_t[:, k], scalar=vecs[:, V_MIX + k:V_MIX + k + 1], in1=f32(act_hi[:, k]),
                    op0=ALU.mult, op1=ALU.subtract).then_inc(on["act_ready"], 1)

            split_lo()
            slabs.step()
            dve.wait_ge(on["rstd_ready"], 1)
            dve.wait_ge(on["act_ready"], KT)
            dve.wait_ge(on["mem_parked"], 16)
            dve.wait_ge(on["x_parked"], 16 * KT)

            def tables():
                b, a = slice(BETA, BETA + NH), slice(DECAY, DECAY + NH)
                chain.link(ts(rows[b], rows[b], -80.0, None, ALU.max))
                v.tensor_copy(cols[0:1, 29:30], cols[0:1, 30:31]).then_inc(on["rows_out"], 1)
                dve.wait_ge(on["pos_in"], 32)
                dve.wait_ge(on["dist_ready"], 1)
                v.tensor_copy(pos_rowf[:], pos_row[:]).then_inc(on["pos_ready"], 1)
                dve.wait_ge(on["pos_bcast"], 1)
                chain.link(ts(ang[:], M[0][:], freq_col[:], None, ALU.mult))
                chain.link(ts(ret_q[:], ang[:], 0.5 / math.pi, ROUND_MAGIC, ALU.mult, ALU.add))
                chain.link(ts(ret_q[:], ret_q[:], -ROUND_MAGIC, None, ALU.add))
                for part in TWO_PI_PARTS:
                    chain.link(stt(out=ang[:], in0=ret_q[:], scalar=-part, in1=ang[:], op0=ALU.mult, op1=ALU.add))
                chain.link(ts(sin_t[:], ang[:], -3.1415925, 3.1415925, ALU.max, ALU.min))
                chain.link(stt(out=cos_t[:], in0=sin_t[:], scalar=-1.0, in1=sin_t[:], op0=ALU.mult, op1=ALU.max))
                ts(cos_t[:], cos_t[:], -1.0, math.pi / 2, ALU.mult, ALU.add).then_inc(on["ang_ready"], 1)
                yield SEG
                dve.wait_ge(on["rows_act"], 1)
                chain.link(ts(sq[b], sq[b], 1.0, None, ALU.add))
                chain.put(v.reciprocal(rows[b], sq[b]))
                chain.put(v.memset(nrm[a], 1.0))
                chain.sync()
                chain.put(v.memset(nrm[a, 0::P], 0.0))
                chain.link(stt(out=gtmp[a], in0=gtmp[a], scalar=0.0, in1=sq[a], op0=ALU.max, op1=ALU.add))
                chain.link(ts(gtmp[a], gtmp[a], cols[a, 22:23], -1.0, ALU.mult, ALU.mult))
                v.tensor_tensor_scan(rows[a], nrm[a], gtmp[a], 0.0, ALU.mult, ALU.add).then_inc(on["rows_ready"], 1)
                yield SEG
                dve.wait_ge(on["dec_exp"], 1)
                chain.link(ts(ret_dec[:], ret_dec[:], P ** -0.5, None, ALU.mult))
                chain.link(v.memset(ret_dec[CH:P, :, 0:CH], 0.0))
                yield SEG
                dve.wait_ge(on["trig_ready"], 1)
                dve.wait_ge(on["cols_ready"], 1)
                dve.wait_ge(on["rows_ready"], 1)
                yield SEG

            def retention(par, hd):
                q, k = stage[:, par, 0], stage[:, par, 1]
                clamp_gate(stage[:, par, 3])
                dve.wait_ge(on["ret_rot"], hd + 1)
                for n, t in enumerate((q, k)):
                    dst = (ret_q, ret_k)[n]
                    chain.put(tt(dst[:], t, cos_t[:], ALU.mult))
                    chain.link(tt(ret_t[:, n], M[n][:], sin_t[:], ALU.mult))
                chain.put(tt(ret_q[:], ret_q[:], ret_t[:, 0], ALU.add))
                tt(ret_k[:], ret_k[:], ret_t[:, 1], ALU.add).then_inc(on["ret_qk"], 1)
                yield SEG
                dve.wait_ge(on["ret_scores"], hd + 1)
                for j in range(NT):
                    last = tt(packed(ret_wt, j), score_ps(j),
                              ret_dec[:, bass.ds(hd, 1), 0:WID[j]].rearrange("p a s -> p (a s)"), ALU.mult)
                last.then_inc(on["ret_w"], 1)
                yield SEG
                y_out(hd + Y_RET, par, hd + H_RET)
                yield SEG
                yield SEG

            def delta(par, hd):
                gcol = rcols[:, :, bass.ds(hd + NH, 1)]
                beta = rcols[:, :, bass.ds(hd, 1)]
                col = lambda n: dn_cols[:, n].unsqueeze(2)
                wide = lambda c: c.broadcast_to([P, NT, P])
                chain.put(ts(dn_rows[DECAY:DECAY + NH], rows[DECAY:DECAY + NH],
                             ident[DECAY:DECAY + NH, bass.ds(hd + DECAY, 1)], None, ALU.mult))
                ts(dn_rows[BETA:BETA + NH], rows[BETA:BETA + NH], ident[BETA:BETA + NH, bass.ds(hd + BETA, 1)], None,
                   ALU.mult).then_inc(on["bcast_rows"], 1)
                for i in range(CONV - 1, -1, -1):
                    d = CONV - 1 - i
                    for t in range(3):
                        w = convs[:, bass.ds(hd + (i * 3 * NH + t * NH), 1)]
                        if d == 0:
                            ins = ts(dn_c[:, t], stage[:, par, t], w, None, ALU.mult)
                        else:
                            ins = stt(out=dn_c[:, t, d:S], in0=stage[:, par, t, 0:S - d], scalar=w,
                                      in1=dn_c[:, t, d:S], op0=ALU.mult, op1=ALU.add)
                        chain.put(ins)
                    chain.sync()
                for t in range(3):
                    ts(dn_s[:, t], dn_c[:, t], GATE_FLOOR, None, ALU.max).then_inc(on["dn_clamped"], 1)
                dve.wait_ge(on["bcast_ps"], hd + 1)
                tt(flat3(dn_bs[:]), flat3(M[3][:]), every_tile(tri_strict[:]), ALU.mult).then_inc(on["dn_b2"], 1)
                dve.wait_ge(on["dn_gbev"], hd + 1)
                g_last = dn_gb[:, P - 1::P].unsqueeze(2)
                v.tensor_copy(col(4), gcol)
                tt(col(5), g_last, gcol, ALU.subtract)
                v.tensor_copy(col(6), g_last).then_inc(on["dn_cols"], 1)
                chain.link(tt(flat3(dn_dt[:]), flat3(dn_gb[:]), wide(gcol), ALU.subtract))
                ts(dn_dt[:], dn_dt[:], 0.0, None, ALU.min).then_inc(on["dn_dd"], 1)
                for t in range(3):
                    dve.wait_ge(on["dn_sig"], hd * 3 + (t + 1))
                    tt(dn_c[:, t], dn_c[:, t], dn_s[:, t], ALU.mult).then_inc(on["dn_silu"], 1)
                dve.wait_ge(on["dn_inv"], hd * 2 + 1)
                stt(out=dn_c[:, 0], in0=dn_c[:, 0], scalar=QSCALE, in1=dn_uu[:], op0=ALU.mult, op1=ALU.mult)
                dve.wait_ge(on["dn_inv"], hd * 2 + 2)
                tt(dn_c[:, 1], dn_c[:, 1], dn_xx[:], ALU.mult).then_inc(on["dn_qk"], 1)
                clamp_gate(stage[:, par, 3])
                yield SEG
                dve.wait_ge(on["vt_ready"], heads.at(1))
                tt(flat3(dn_bv[:]), flat3(M[4][:]), wide(beta), ALU.mult).then_inc(on["vtok_ready"], 1)
                dve.wait_ge(on["dn_colexp"], hd + 1)
                chain.link(tt(col(7), col(0), beta, ALU.mult))
                dve.wait_ge(on["dn_tok"], hd + 1)
                tt(flat3(dn_kbe), flat3(M[5][:]), wide(col(7)), ALU.mult)
                tt(flat3(dn_kdec[:]), flat3(M[5][:]), wide(col(1)), ALU.mult).then_inc(on["dn_bvk"], 1)
                dve.wait_ge(on["dn_b1"], hd + 1)
                chain.link(tt(dn_bs[:], dn_bs[:], dn_dt[:], ALU.mult))
                dve.wait_ge(on["dn_gram"], hd + 1)
                tt(dn_at[:], M[3][:], dn_dt[:], ALU.mult)
                tt(dn_lt[:], M[2][:], dn_bs[:], ALU.mult).then_inc(on["dn_pair"], 1)
                dve.wait_ge(on["dn_c1t"], hd + 1)
                chain.put(tt(flat3(dn_xx[:]), every_tile(ident[:]), flat3(M[4][:]), ALU.subtract))
                ins = tt(flat3(dn_xt[:]), every_tile(ident[:]), flat3(dn_ctt[:, 0]), ALU.subtract)
                ins.then_inc(on["dn_x"], 1)
                dve.wait_ge(on["dn_eg"], hd + 1)
                tt(dn_qg, dn_c[:, 0], dn_gb[:], ALU.mult).then_inc(on["dn_qg"], 1)
                for n in range(1, 7):
                    dve.wait_ge(on["dn_x"], hd * 7 + n)
                    if n in (2, 5):
                        yield SEG
                    dve.wait_ge(on["dn_v"], hd * 6 + n)
                    if n < 6:
                        chain.put(tt(dn_xx[:], dn_xx[:], M[3][:], ALU.subtract))
                    tt(dn_xt[:], dn_xt[:], M[4][:], ALU.subtract).then_inc(on["dn_x"], 1)
                for c in range(NT):
                    if c:
                        dve.wait_ge(on["dn_ws"], hd * 3 + c)
                        tt(dn_vn[:], dn_uu[:, c * P:(c + 1) * P], M[4][:, 0:P], ALU.subtract).then_inc(on["dn_vnew"], 1)
                    if c < NT - 1:
                        dve.wait_ge(on["dn_ds"], hd * 3 + (c + 1))
                        if c == 0:
                            ins = v.tensor_copy(dn_st[:], M[5][:, 0:P])
                        else:
                            dve.wait_ge(on["dn_state"], hd * 3 + c)
                            ins = stt(out=dn_st[:], in0=dn_st[:], scalar=dn_cols[:, 2, c:c + 1], in1=M[5][:, 0:P],
                                      op0=ALU.mult, op1=ALU.add)
                        ins.then_inc(on["dn_state"], 1)
                y_out(hd + Y_DN, par, hd + H_DN)
                heads.step()
                yield SEG

            def gla_logits():
                chain.put(v.memset(restart[:], 1.0))
                chain.sync()
                chain.put(v.memset(restart[:, 0::CH], 0.0))
                for p in range(2):
                    dve.wait_ge(on["gla_l"], p + 1)
                    chain.link(stt(out=gla_t[:, p], in0=gla_t[:, p], scalar=0.0, in1=gla_e[:, p], op0=ALU.min,
                                   op1=ALU.subtract))
                    chain.put(v.tensor_tensor_scan(b_loc[:, p], restart[:], gla_t[:, p], 0.0, ALU.mult, ALU.add))
                    chain.put(v.tensor_tensor_scan(b_all[:, p], gla_t[:, p], restart[:], 0.0, ALU.add, ALU.min))
                chain.sync()
                yield SEG
                yield SEG

            def gla(par):
                q, k = stage[:, par, 0], stage[:, par, 1]

                def halves(t, h):
                    t = t.rearrange("p (b two h) -> p b two h", two=2, h=h)
                    return t[:, :, 0, :], t[:, :, 1, :]

                def distances(n):
                    h = 256 >> n
                    lo, up = halves((b_all if h >= 64 else b_loc)[:, par], h)
                    e_lo, e_up = halves(gla_e[:, n % 2], h)
                    mid = lo[:, :, h - 1:h].broadcast_to([P, S // (2 * h), h])
                    chain.put(tt(e_up, up, mid, ALU.subtract))
                    tt(e_lo, mid, lo, ALU.subtract).then_inc(on["gla_d"], 1)

                def decayed(n):
                    h = 256 >> n
                    dve.wait_ge(on["gla_e"], par * 9 + n + 1)
                    if n >= 2:
                        dve.wait_ge(on["gla_lv"], par * 9 + n - 1)
                    e_lo, e_up = halves(gla_e[:, n % 2], h)
                    d_lo, d_up = halves(gla_qk[:, n % 2], h)
                    chain.put(tt(d_up, halves(gla_qs[:], h)[1], e_up, ALU.mult))
                    tt(d_lo, halves(k, h)[0], e_lo, ALU.mult).then_inc(on["gla_qe"], 1)
                    dve.wait_ge(on["gla_qe"], par * 9 + n + 1)

                def take(n):
                    dve.wait_ge(on["gla_lv"], par * 9 + n + 1)
                    mask = every_tile(lvl_mask[:, n - 2].bitcast(mybir.dt.uint32))
                    for hh in range(2):
                        bank = M[4 + hh] if n % 2 == 0 else M[2 + hh]
                        ins = v.copy_predicated(flat3(gla_s[:, hh]), mask, flat3(bank[:]))
                        if hh == 0:
                            chain.put(ins)
                    ins.then_inc(on["gla_lvout"], 1)

                chain.put(ts(gla_qs[:], q, DK ** -0.5, None, ALU.mult))
                v.tensor_copy(cols[0:1, 29:30], cols[0:1, 30:31]).then_inc(on["gla_qs"], 1)
                chain.sync()
                distances(0)
                distances(1)
                clamp_gate(stage[:, par, 4])
                dve.wait_ge(on["gla_diag"], par + 1)
                for hh in range(2):
                    ins = tt(flat3(gla_s[:, hh]), flat3(M[2 + hh][:]), every_tile(ident[:]), ALU.mult)
                ins.then_inc(on["gla_lvout"], 1)
                for n in range(9):
                    decayed(n)
                    if n < 7:
                        distances(n + 2)
                    if n == 3:
                        dve.wait_ge(on["gla_lvout"], par * 8 + 1)
                    if n > 3:
                        dve.wait_ge(on["gla_lvout"], par * 8 + n - 2)
                    if n >= 3:
                        take(n - 1)
                    if n in (1, 3, 5, 7):
                        yield SEG
                dve.wait_ge(on["gla_lvout"], par * 8 + 7)
                take(8)
                for hh in range(2):
                    if hh:
                        clamp_gate(stage[:, par, 5])
                    y_out(Y_GLA + 2 * par + hh, hh, H_GLA + 2 * par + hh)
                    yield SEG

            def stick(par):
                for hh in range(2):
                    hd = 2 * par + hh
                    dve.wait_ge(on["sb_l"], hd + 1)
                    chain.link(ts(sb_m[:], sb_x[:], -1.0, 0.0, ALU.mult, ALU.min))
                    tt(sb_m[:], sb_m[:], sb_l[:], ALU.subtract).then_inc(on["sb_lk"], 1)
                    yield SEG
                    dve.wait_ge(on["sb_cum"], hd + 1)
                    for at, n, bank in ((0, WID[0], M[3]), (OFF[1], WID[1], M[4]), (OFF[2], WID[2] + WID[3], M[5])):
                        ins = tt(sb_x[:, at:at + n], sb_x[:, at:at + n], bank[:, 0:n], ALU.add)
                    ins.then_inc(on["sb_z"], 1)
                    yield SEG
                    y_out(Y_SB + hd, hh, H_SB + hd, gated=False)
                    yield SEG

            mixer = tables()
            for j in range(4):
                window(mixer, stage[:, 0, j - 1] if j else rows[:])
            with dve.Fori(0, NH // 2) as i:
                slabs.enter(i, 8)
                chain.count.enter(i, 2 * RET_LINKS)
                for par in range(2):
                    mixer = retention(par, i * 2 + par)
                    for j in range(4):
                        window(mixer, stage[:, 1 - par, j - 1] if j else stage[:, par, 3])
            slabs.leave(NH // 2)
            chain.count.leave(NH // 2)
            heads.step(NH)
            with dve.Fori(0, NH // 2) as i:
                slabs.enter(i, 8)
                heads.enter(i, 2)
                chain.count.enter(i, 2 * DN_LINKS)
                for par in range(2):
                    mixer = delta(par, i * 2 + par)
                    for j in range(4):
                        window(mixer, stage[:, 1 - par, j - 1] if j else stage[:, par, 3])
            slabs.leave(NH // 2)
            heads.leave(NH // 2)
            chain.count.leave(NH // 2)
            mixer = gla_logits()
            for j in range(2):
                window(mixer, stage[:, 0, 3 + j])
            mixer = gla(0)
            for j in range(6):
                window(mixer, stage[:, 1, j - 1] if j else stage[:, 0, 5])
            mixer = gla(1)
            for j in range(6):
                window(mixer, stage[:, 0, j - 1] if j else stage[:, 1, 5])
            mixer = stick(0)
            for j in range(6):
                window(mixer, stage[:, 1, j - 1] if j else stage[:, 0, 5])

            dve.wait_ge(on["mem_hi"], 1)
            tt(act_lo[:, :, 0:NMEM], mem_back[:], f32(act_hi[:, :, 0:NMEM]), ALU.subtract).then_inc(on["mem_split"], 1)

            def kv_window(slot, mixer=None, split=True):
                dve.wait_ge(on["slab_mul"], slabs.at())
                v.tensor_copy(kv_t[:, slot], G[(slabs.first - 1) % 2][:, 0:NMEM]).then_inc(on["slab_out"], 1)
                if split:
                    split_lo()
                run_segment(mixer)

            mixer = stick(1)
            window(mixer, stage[:, 1, 5])
            for idx in range(5):
                if idx >= 2:
                    dve.wait_ge(kv_tile_parked[idx % 2], 16 * (idx // 2))
                kv_window(idx % 2, mixer)
                slabs.step()
            dve.wait_ge(kv_tile_parked[1], 16 * 2)
            kv_window(1)
            slabs.step()
            with dve.Fori(3, KT // 2) as i:
                slabs.enter(i - 3, 2)
                for slot in range(2):
                    dve.wait_ge(kv_tile_parked[slot], i * 16)
                    kv_window(slot)
                    slabs.step()
            slabs.leave(KT // 2 - 3)
            for idx in range(2):
                dve.wait_ge(kv_tile_parked[idx], 16 * (KT // 2))
                kv_window(idx)
                slabs.step()
            with dve.Fori(1, KT // 2 - 1) as i:
                slabs.enter(i - 1, 2)
                for slot in range(2):
                    dve.wait_ge(on["kv_turned"], i * 2 + (slot - 1))
                    kv_window(slot)
                    slabs.step()
            slabs.leave(KT // 2 - 2)
            dve.wait_ge(on["kv_turned"], KT - 3)
            kv_window(0)
            slabs.step()
            dve.wait_ge(on["kv_turned"], KT - 2)
            kv_window(1, split=False)

            splits = Count()

            def split_activations(gain=None):
                for k in range(KT):
                    splits.step()
                    dve.wait_ge(on["xg_hi"], KT + splits.n)
                    if gain is None:
                        ins = tt(act_lo[:, k], main[:, k], f32(act_hi[:, k]), ALU.subtract)
                    else:
                        ins = stt(out=act_lo[:, k], in0=main[:, k], scalar=vecs[:, gain + k:gain + k + 1],
                                  in1=f32(act_hi[:, k]), op0=ALU.mult, op1=ALU.subtract)
                    ins.then_inc(on["act_ready"], 1)
                split_lo()
                slabs.step()

            def add_to_main(m):
                dve.wait_ge(on["slab_mul"], slabs.at())
                tt(main[:, m], main[:, m], G[(slabs.first - 1) % 2][:], ALU.add).then_inc(on["slab_out"], 1)

            def residual(fill):
                for m in range(KT):
                    if m % 4 == 0:
                        dve.wait_ge(main_back[m // 4], 16 * fill)
                    add_to_main(m)
                    if m < KT - 1:
                        split_lo()
                        slabs.step()

            def attention(hd):
                dve.wait_ge(on["cx_scores"], hd + 1)
                for n in range(2):
                    ins = v.tensor_reduce(ccols[:, 0, 2 * n:2 * n + 2], M[n][:].rearrange("p (t m) -> p t m", m=NMEM),
                                          AX.X, ALU.max)
                    chain.put(ins)
                chain.sync()
                ts(ccols[:, 1], ccols[:, 0], -CSCALE, None, ALU.mult).then_inc(on["cx_max"], 1)
                dve.wait_ge(on["cx_exp"], hd + 1)
                chain.link(v.reciprocal(ccols[:, 3], ccols[:, 2]))
                tt(prob[:], prob[:], ccols[:, 3].unsqueeze(2).broadcast_to([P, NT, NMEM]), ALU.mult).then_inc(
                    on["cx_p"], 1)
                for _ in range(4):
                    yield SEG

            split_activations()
            residual(2)
            split_activations(V_CROSS)

            dve.wait_ge(on["x_rstd"], 1)
            mixer = None
            for m in range(KT - 1):
                if m % 4 == 3:
                    mixer = attention(m // 4)
                window(mixer, cstage[:, (m // 4) % 2, m % 4])
            evict_scaled(cstage[:, (NH - 1) % 2, NH - 1])
            run_segment(attention(NH - 1))
            split_activations()
            residual(3)
            split_activations(V_MLP)

            def chunk(c, first=False, last=False):
                for w in range(2 * MC):
                    if w == 0 and first:
                        continue
                    if not (last and w == 2 * MC - 1):
                        split_lo()
                    if 1 <= w <= MC:
                        j = w - 1
                        dve.wait_ge(on["mlp_relu"], c * MC + (j + 1))
                        tt(uf[:, j % 2], relu[:, j % 2], G[(slabs.first - 1) % 2][:], ALU.mult).then_inc(
                            on["slab_out"], 1)
                        dve.wait_ge(on["mlp_uhi"], c * MC + (j + 1))
                        tt(u_lo[:, j], uf[:, j % 2], f32(u_hi[:, j]), ALU.subtract).then_inc(on["u_ready"], 1)
                    else:
                        down_out((w - MC - 1) % MC)
                    slabs.step()

            def down_out(d):
                slot = (slabs.first - 1) % 2
                dve.wait_ge(on["slab_mul"], slabs.at())
                dve.wait_ge(on["slab_out"], slabs.at(-1))
                for j in range(2):
                    chain.put(tt(xsq[:, j], M[2 * slot + j][:], rstd[:], ALU.mult))
                chain.sync()
                for j in range(2):
                    ins = tt(main[:, 2 * d + j], main[:, 2 * d + j], xsq[:, j], ALU.add)
                ins.then_inc(on["slab_out"], 1)

            dve.wait_ge(on["x_rstd"], 2)
            chunk(0, True)
            with dve.Fori(1, NCH - 1) as c:
                slabs.enter(c - 1, 2 * MC)
                chain.count.enter(c - 1, 2 * MC)
                chunk(c)
            slabs.leave(NCH - 2)
            chain.count.leave(NCH - 2)
            chunk(NCH - 1, last=True)
            down_out(MC - 1)

            dve.wait_ge(on["fin_rstd"], 1)
            for k in range(KT):
                stt(out=main[:, k], in0=main[:, k], scalar=vecs[:, V_FINAL + k:V_FINAL + k + 1], in1=rstd[:],
                    op0=ALU.mult, op1=ALU.mult).then_inc(on["fin_x"], 1)
            for n in range(1, NT * 4, 2):
                t, g = n // 4, n % 4
                dve.wait_ge(on["fin_turned"], n + 1)
                if t >= 2:
                    dve.wait_ge(out_done[t % 2], 16 * (t // 2))
                v.tensor_copy(w_raw[:, t % 2, g * S:(g + 1) * S], M[n % 4][:]).then_inc(on["fin_odd"], 1)


_INS = ("x", "mem", "positions", "ln_mix", "w_in", "gla_w_up", "gla_b_up", "dn_conv_w", "dn_a_log", "dn_dt_bias",
        "mix_head_norm", "w_mix_out", "ln_cross", "ln_mem", "w_cross_q", "w_cross_kv", "w_cross_o", "ln_mlp",
        "w_mlp_up", "w_mlp_down", "ln_final")


def kernel(**inputs):
    import numpy as _np
    import concourse.bacc as _bacc
    from concourse import mybir as _mybir
    from concourse.bass_utils import run_bass_kernel_spmd as _run

    nc = _bacc.Bacc("TRN2", target_bir_lowering=False, num_devices=1)
    arrays = {f"in_{name}_dram": _np.ascontiguousarray(inputs[name]) for name in _INS}
    freq = (10000.0 ** (-_np.arange(0, P, 2) / P)).astype(_np.float32)
    arrays["in_inv_freq_dram"] = _np.concatenate([freq, freq])[:, None].copy()
    args = [nc.dram_tensor(name, a.shape, _mybir.dt.from_np(a.dtype), kind="ExternalInput").ap()
            for name, a in arrays.items()]
    shape = inputs["x"].shape
    args.append(nc.dram_tensor("out_0_dram", shape, F32, kind="ExternalOutput").ap())
    build(nc, *args)
    r = _run(nc, [arrays], core_ids=[0])
    return r.results[0]["out_0_dram"]
```

```python
import math
from contextlib import ExitStack

import concourse.bass as bass
from concourse import mybir

F32 = mybir.dt.float32
F32R = mybir.dt.float32r
I32 = mybir.dt.int32
ALU = mybir.AluOpType
ACT = mybir.ActivationFunctionType
AX = mybir.AxisListType

P = 128
EPS = 1e-6
HOP, SEG = "hop", "segment"
TWO_PI_PARTS = (6.28125, 0.0019350051879882812, 3.019916e-07)
ROUND_MAGIC = 12582912.0
FAR = -30000.0
GATE_FLOOR = -40.0


class Count:

    def __init__(self, start=0):
        self.outer, self.n, self.first, self.stack = 0, start, start, []

    def at(self, d=0):
        return self.outer + (self.n + d)

    def step(self, k=1):
        self.n += k
        self.first += k

    def enter(self, i, per):
        self.stack.append((self.outer, self.n, per))
        self.outer, self.n = i * per + (self.outer + self.n), 0

    def leave(self, times):
        outer, n, per = self.stack.pop()
        assert self.n == per, f"the loop's body counts {self.n}, not {per}"
        self.outer, self.n = outer, n + times * per
        self.first += (times - 1) * per


class Chain:

    def __init__(self, eng, sem):
        self.eng, self.sem, self.count = eng, sem, Count()

    def put(self, ins):
        ins.then_inc(self.sem, 1)
        self.count.step()

    def sync(self):
        self.eng.wait_ge(self.sem, self.count.at())

    def link(self, ins):
        self.put(ins)
        self.sync()


def run_segment(mixer):
    if mixer is not None:
        for step in mixer:
            if step == SEG:
                break


SEMS = """
 special_in vec_in small_in pos_in raw_zero slab_hi slab_lo slab_mul slab_out consts heads_done
x_turned x_even x_odd xg_hi act_ready act_free x_ssq x_diag x_bcast rstd_ready vec_turned vec_ready x_parked mem_in
mem_scaled mem_turned mem_out mem_parked mem_back y_back mem_hi mem_split
rows_ready cols_turned cols_ready bcast_ps
pos_bcast pos_ready ang_ready trig_ready dist_ready
gate_clamped gate_sig gate_ready o_ready sq_ready norm_sum norm_ready vt_ready vtok_ready
ret_rot ret_qk ret_scores ret_w
dn_clamped dn_sig dn_silu dn_sq dn_l2 dn_inv dn_qk dn_dd dn_dt dn_masked dn_at dn_pair dn_tok
dn_c1t dn_x dn_ct dn_u dn_uev dn_v dn_uw dn_uwev dn_eg dn_qg dn_ws dn_vnew dn_ds dn_state
gla_z gla_l gla_qs gla_diag gla_d gla_e gla_qe gla_lv gla_lvout gla_topout bcast_rows dn_gram dn_bvk dn_gbev dn_cols kv_turned
sb_scores sb_x sb_masked sb_l sb_lk sb_cum sb_z sb_w
kv_vout xsq_ready xacc_ready
cx_scores cx_max cx_exp cx_p cx_pt cx_ptok cx_o
up_in mlp_relu mlp_uhi u_ready fin_sum fin_rstd fin_x fin_turned fin_even fin_odd x_total x_rstd dec_exp dn_colexp cx_done rows_out rows_act
act_chain dve_chain pool_chain 
""".split()


def build(nc, x_in, mem_in, positions, ln_mix, w_in, gla_w_up, gla_b_up, dn_conv_w, dn_a_log, dn_dt_bias,
          mix_head_norm, w_mix_out, ln_cross, ln_mem, w_cross_q, w_cross_kv, w_cross_o, ln_mlp,
          w_mlp_up, w_mlp_down, ln_final, inv_freq, out, park="Internal"):
    S, D = x_in.shape[1], x_in.shape[2]
    NMEM = mem_in.shape[1]
    KT, NT, MT = D // P, S // P, NMEM // P
    DFF = w_mlp_up.shape[2]
    GW = D // 4
    NH = GW // P
    RANK = gla_w_up.shape[1]
    DK = P // 2
    CONV = dn_conv_w.shape[1]
    CH = 64
    C_RET, C_GLA = 0, 4 * GW
    C_LR = C_GLA + 3 * GW
    C_SB = C_LR + RANK
    C_DN = C_SB + 3 * GW
    C_B = C_DN + 4 * GW
    C_A = C_B + NH
    SLAB = KT * P
    MC = 1024 // P
    NCH = DFF // (MC * P)
    WID = [S - P * j for j in range(NT)]
    OFF = [sum(WID[:j]) for j in range(NT)]
    PK = sum(WID)
    LOG_GAMMA = [math.log1p(-2.0 ** (-5 - h)) for h in range(NH)]
    QSCALE, CSCALE = P ** -0.5, GW ** -0.5
    LEVELS = [64, 32, 16, 8, 4, 2, 1]
    Y_RET, Y_GLA, Y_SB, Y_DN = 0, NH, 2 * NH, 3 * NH
    H_RET, H_DN, H_GLA, H_SB = 0, NH, 2 * NH, 3 * NH
    V_MIX, V_HEAD, V_CROSS, V_MEM, V_MLP, V_FINAL = (KT * j for j in range(6))
    V_N = 6 * KT
    C_BUP = CONV * 3 * NH
    C_N = C_BUP + 2
    KV0 = 1 + 4 * NH + 4 * NH + 6 * NH // 2 + 6 * NH // 2
    OUT0 = KV0 + 2 * KT
    KV_SIDE = 12
    BETA, DECAY = 32, 64

    kview = lambda w: w[0].rearrange("(k p) n -> p k n", p=P)
    w_in_v, w_out_v, w_cq_v, w_ckv_v, w_co_v, w_up_v = map(
        kview, (w_in, w_mix_out, w_cross_q, w_cross_kv, w_cross_o, w_mlp_up))
    w_dn_v = kview(w_mlp_down)

    def dram(name, shape):
        return nc.dram_tensor(name, shape, F32, kind=park).ap()

    x_park = dram("x_park", (KT, P, S))
    y_park = dram("y_park", (KT, P, S))
    m_park = dram("m_park", (KT, P, NMEM))
    k_park = dram("k_park", (KT, P, NMEM))
    v_park = dram("v_park", (KT, P, NMEM))

    with ExitStack() as ctx:
        def alloc(scope):
            return lambda name, shape, dt=F32: scope.enter_context(nc.sbuf_tensor(name, shape, dt))

        on = {name: ctx.enter_context(nc.semaphore(name)) for name in SEMS}
        raw_in = [ctx.enter_context(nc.semaphore(f"raw_in{j}")) for j in range(2)]
        x_loaded = [ctx.enter_context(nc.semaphore(f"x_loaded{j}")) for j in range(2)]
        main_back = [ctx.enter_context(nc.semaphore(f"main_back{j}")) for j in range(4)]
        y_parked = [ctx.enter_context(nc.semaphore(f"y_parked{j}")) for j in range(2)]
        kv_tile_parked = [ctx.enter_context(nc.semaphore(f"kv_tile_parked{j}")) for j in range(2)]
        kv_loaded = [ctx.enter_context(nc.semaphore(f"kv_loaded{j}")) for j in range(2)]
        out_done = [ctx.enter_context(nc.semaphore(f"out_done{j}")) for j in range(2)]

        G = [ctx.enter_context(nc.psum_tensor(f"slab_ps{j}", [P, S], F32)) for j in range(2)]
        M = [ctx.enter_context(nc.psum_tensor(f"mix_ps{j}", [P, S], F32)) for j in range(6)]

        sb = alloc(ctx)
        act_hi = sb("act_hi", [P, KT, S], F32R)
        act_lo = sb("act_lo", [P, KT, S], F32R)
        w_raw = sb("w_raw", [P, 2, SLAB])
        w_hi = sb("w_hi", [P, 2, SLAB], F32R)
        w_lo = sb("w_lo", [P, 2, SLAB], F32R)
        ident = sb("ident", [P, P])
        ones = sb("ones", [P, P])
        vecs = sb("vecs", [P, V_N])
        convs = sb("convs", [P, C_N])
        rstd = sb("rstd", [P, S])
        eps_col = sb("eps_col", [P, 1])
        gla_up = sb("gla_up", [RANK, 2 * P])
        cols = sb("cols", [P, 32])
        rcols = sb("rcols", [P, NT, 2 * NH])

        mix = ctx.enter_context(ExitStack())
        sb = alloc(mix)
        tri_suffix = sb("tri_suffix", [P, P])
        tri_incl = sb("tri_incl", [P, P])
        tri_strict = sb("tri_strict", [P, P])
        lvl_mask = sb("lvl_mask", [P, 7, P])
        with ExitStack() as scope:
            sb = alloc(scope)
            x_t = sb("x_t", [P, KT, S])
            x_tok = sb("x_tok", [P, NT, D])
            mem_t = sb("mem_t", [P, KT, NMEM])
            vec_rows = sb("vec_rows", [V_N, P])
            conv_rows = sb("conv_rows", [C_N, P])
            diag_r = sb("diag_r", [P, NT, P])
        sb = alloc(mix)
        stage = sb("stage", [P, 2, 6, S])
        rows = sb("rows", [P, S])
        vtok = sb("vtok", [P, NT, P])
        gate = sb("gate", [P, S])
        gtmp = sb("gtmp", [P, S])
        sq = sb("sq", [P, S])
        nrm = sb("nrm", [P, S])
        ytile = sb("ytile", [P, 2, S])
        with ExitStack() as scope:
            sb = alloc(scope)
            rot = sb("rot", [P, P])
            cos_t = sb("cos_t", [P, S])
            sin_t = sb("sin_t", [P, S])
            ret_dec = sb("ret_dec", [P, NH, S])
            dist = sb("dist", [P, S])
            pos_row = sb("pos_row", [1, S], I32)
            pos_rowf = sb("pos_rowf", [1, S])
            freq_col = sb("freq_col", [P, 1])
            ang = sb("ang", [P, S])
            ret_q = sb("ret_q", [P, S])
            ret_k = sb("ret_k", [P, S])
            ret_t = sb("ret_t", [P, 2, S])
            ret_wt = sb("ret_wt", [P, PK])
        with ExitStack() as scope:
            sb = alloc(scope)
            dn_rows = sb("dn_rows", [P, S])
            dn_gb = sb("dn_gb", [P, S])
            dn_c = sb("dn_c", [P, 3, S])
            dn_s = sb("dn_s", [P, 3, S])
            dn_dt = sb("dn_dt", [P, S])
            dn_bs = sb("dn_bs", [P, S])
            dn_lt = sb("dn_lt", [P, S])
            dn_at = sb("dn_at", [P, S])
            dn_ctt = sb("dn_ctt", [P, 2, S])
            dn_xx = sb("dn_xx", [P, S])
            dn_xt = sb("dn_xt", [P, S])
            dn_uu = sb("dn_uu", [P, S])
            dn_bv = sb("dn_bv", [P, S])
            dn_kdec = sb("dn_kdec", [P, S])
            dn_st = sb("dn_st", [P, P])
            dn_vn = sb("dn_vn", [P, P])
            dn_cols = sb("dn_cols", [P, 8, NT])
        dn_temp = (dn_gb, dn_dt, dn_bs)
        dn_kbe, dn_wt, dn_qg = dn_s[:, 0], dn_s[:, 1], dn_s[:, 2]
        with ExitStack() as scope:
            sb = alloc(scope)
            b_loc = sb("b_loc", [P, 2, S])
            b_all = sb("b_all", [P, 2, S])
            gla_t = sb("gla_t", [P, 2, S])
            restart = sb("restart", [P, S])
            gla_qs = sb("gla_qs", [P, S])
            gla_e = sb("gla_e", [P, 2, S])
            gla_qk = sb("gla_qk", [P, 2, S])
            gla_s = sb("gla_s", [P, 2, S])
            gla_o = sb("gla_o", [P, 2, PK - S])
        with ExitStack() as scope:
            sb = alloc(scope)
            sb_x = sb("sb_x", [P, PK])
            sb_l = sb("sb_l", [P, PK])
            sb_m = sb("sb_m", [P, PK])
            mem_back = sb("mem_back", [P, KT, NMEM])
            kv_t = sb("kv_t", [P, 2, NMEM])
            v_t = sb("v_t", [P, 2, NMEM])
        mix.close()

        main = alloc(ctx)("main", [P, KT, S])
        sb = alloc(ctx)
        xsq = sb("xsq", [P, 2, S])
        xacc = sb("xacc", [P, S])
        with ExitStack() as scope:
            sb = alloc(scope)
            cstage = sb("cstage", [P, 2, NH, S])
            kh = sb("kh", [P, 2, NH, NMEM])
            vh = sb("vh", [P, 2, NH, NMEM])
            prob = sb("prob", [P, NT, NMEM])
            prob_t = sb("prob_t", [P, MT, S])
            ccols = sb("ccols", [P, 4, NT])
        with ExitStack() as scope:
            sb = alloc(scope)
            u_hi = sb("u_hi", [P, MC, S], F32R)
            u_lo = sb("u_lo", [P, MC, S], F32R)
            relu = sb("relu", [P, 2, S])
            uf = sb("uf", [P, 2, S])

        flat3 = lambda t: t.rearrange("p (t s) -> p t s", s=P)
        per_tile = lambda c: c.unsqueeze(2).broadcast_to([P, NT, P])
        every_tile = lambda m: m.unsqueeze(1).broadcast_to([P, NT, P])

        def packed(t, j):
            return t[:, OFF[j]:OFF[j] + WID[j]]

        SC = [(3, 0), (4, 0), (5, 0), (5, WID[2])]

        def score_ps(j):
            bank, at = SC[j]
            return M[bank][:, at:at + WID[j]]

        block = ctx.enter_context(nc.Block())

        @block.sync
        def _(sp):
            for half in range(2):
                cut = slice(half * D // 2, (half + 1) * D // 2)
                for t in range(NT):
                    sp.dma_start(x_tok[:, t, cut], x_in[0, t * P:(t + 1) * P, cut]).then_inc(x_loaded[half], 16)
            slabs = Count()

            first = w_raw[:, 0].rearrange("p (k n) -> p k n", k=KT)
            sp.wait_ge(on["raw_zero"], 1)
            for at, col, n in ((0, C_LR, RANK), (BETA, C_B, NH), (DECAY, C_A, NH)):
                sp.dma_start(first[:, :, at:at + n], w_in_v[:, :, col:col + n]).then_inc(on["special_in"], 16)
            slabs.step()

            def load(src):
                slot = slabs.first % 2
                if slabs.first >= 2:
                    sp.wait_ge(on["slab_lo"], slabs.at(-1))
                dst = w_raw[:, slot].rearrange("p (k n) -> p k n", k=src.shape[1])
                sp.dma_start(dst, src).then_inc(raw_in[slot], 16)
                slabs.step()

            def head4(col, after_first=None):
                for t in range(4):
                    load(w_in_v[:, :, bass.ds(col + t * GW, P)])
                    if t == 0 and after_first:
                        after_first()

            def load_mem():
                sp.wait_ge(on["x_turned"], KT)
                sp.wait_ge(on["x_ssq"], 1)
                for t in range(MT):
                    sp.dma_start(x_tok[:, t], mem_in[0, t * P:(t + 1) * P, :]).then_inc(on["mem_in"], 16)

            head4(C_RET, load_mem)
            with sp.Fori(1, NH) as h:
                slabs.enter(h - 1, 4)
                head4(h * P + C_RET)
            slabs.leave(NH - 1)
            with sp.Fori(0, NH) as h:
                slabs.enter(h, 4)
                head4(h * P + C_DN)
            slabs.leave(NH)
            with sp.Fori(0, 2) as p:
                slabs.enter(p, 6)
                load(w_in_v[:, :, bass.ds(p * P + C_GLA, P)])
                load(w_in_v[:, :, bass.ds(p * P + (C_GLA + GW // 2), P)])
                for t in (GW, 2 * GW):
                    for j in range(2):
                        load(w_in_v[:, :, bass.ds(p * 2 * P + (C_GLA + t + j * P), P)])
            slabs.leave(2)
            with sp.Fori(0, 2) as p:
                slabs.enter(p, 6)
                for j in range(2):
                    for t in range(3):
                        load(w_in_v[:, :, bass.ds(p * 2 * P + (C_SB + t * GW + j * P), P)])
            slabs.leave(2)

            def matrix(w, n):
                with sp.Fori(0, n // 2) as i:
                    slabs.enter(i, 2)
                    for j in range(2):
                        load(w[:, :, bass.ds(i * 2 * P + j * P, P)])
                slabs.leave(n // 2)

            matrix(w_ckv_v, 2 * KT)
            matrix(w_out_v, KT)
            matrix(w_cq_v, KT)
            matrix(w_co_v, KT)
            with sp.Fori(0, NCH) as c:
                slabs.enter(c, 2 * MC)
                for j in range(MC):
                    load(w_up_v[:, :, bass.ds(c * MC * P + j * P, P)])
                for j in range(MC):
                    load(w_dn_v[:, bass.ds(c * MC, MC), j * 2 * P:(j + 1) * 2 * P])
            slabs.leave(NCH)

            for t in range(NT):
                sp.wait_ge(on["fin_even"], 2 * t + 2)
                sp.wait_ge(on["fin_odd"], 2 * t + 2)
                sp.dma_start(out[0, t * P:(t + 1) * P, :], w_raw[:, t % 2]).then_inc(out_done[t % 2], 16)
            for j in range(2):
                sp.wait_ge(out_done[j], 16 * NT // 2)

        @block.gpsimd
        def _(pool):
            chain = Chain(pool, on["pool_chain"])
            chain.put(nc.gpsimd.memset(ident[:], 0.0))
            chain.put(nc.gpsimd.memset(ones[:], 1.0))
            chain.put(nc.gpsimd.memset(eps_col[:], EPS))
            chain.sync()
            nc.gpsimd.affine_select(out=ident[:], in_=ident[:], compare_op=ALU.not_equal, fill=1.0, base=0,
                                    pattern=[[-1, P]], channel_multiplier=1).then_inc(on["consts"], 1)
            at = 0
            for v in (ln_mix[0], mix_head_norm[0], ln_cross[0], ln_mem[0], ln_mlp[0], ln_final):
                pool.dma_start(vec_rows[at:at + KT, :], v.rearrange("(k p) -> k p", p=P)).then_inc(on["vec_in"], 16)
                at += KT
            pool.dma_start(conv_rows[0:C_BUP, :], dn_conv_w[0].rearrange("i (t p) -> (i t) p", p=P)).then_inc(
                on["vec_in"], 16)
            pool.dma_start(conv_rows[C_BUP:C_N, :], gla_b_up[0].rearrange("(t p) -> t p", p=P)).then_inc(
                on["vec_in"], 16)
            pool.dma_start(cols[DECAY:DECAY + NH, 20:21], dn_a_log.rearrange("a h -> h a")).then_inc(
                on["small_in"], 16)
            pool.dma_start(cols[DECAY:DECAY + NH, 21:22], dn_dt_bias.rearrange("a h -> h a")).then_inc(
                on["small_in"], 16)
            pool.dma_start(gla_up[:], gla_w_up[0]).then_inc(on["up_in"], 16)
            for slot in range(2):
                pool.dma_start(cols[DECAY:DECAY + NH, 24 + slot:25 + slot], dn_a_log.rearrange("a h -> h a")).then_inc(
                    y_parked[slot], 16)

            def triangle(t, sign, base, op):
                chain.link(nc.gpsimd.memset(t, 1.0))
                chain.put(nc.gpsimd.affine_select(out=t, in_=t, compare_op=op, fill=0.0, base=base,
                                                  pattern=[[-sign, P]], channel_multiplier=sign))

            triangle(tri_suffix[:], 1, 0, ALU.is_ge)
            triangle(tri_incl[:], -1, 0, ALU.is_ge)
            triangle(tri_strict[:], -1, 0, ALU.is_gt)
            for n, h in enumerate(LEVELS):
                nb = P // (2 * h)
                chain.link(nc.gpsimd.memset(lvl_mask[:, n], 0.0))
                upper = lvl_mask[:, n].rearrange("p (b two h) -> p b two h", two=2, h=h)[:, :, 1, :]
                chain.link(nc.gpsimd.memset(upper, 1.0))
                chain.link(nc.gpsimd.affine_select(out=upper, in_=upper, compare_op=ALU.is_ge, fill=0.0, base=0,
                                                   pattern=[[-2 * h, nb], [0, h]], channel_multiplier=1))
                chain.put(nc.gpsimd.affine_select(out=upper, in_=upper, compare_op=ALU.is_ge, fill=0.0, base=h - 1,
                                                  pattern=[[2 * h, nb], [0, h]], channel_multiplier=-1))
            chain.sync()
            nc.gpsimd.memset(cols[0:1, 31:32], 0.0).then_inc(on["consts"], 1)

            for k in range(KT):
                pool.wait_ge(on["x_even"], k // 2 + 1)
                if k % 2:
                    pool.wait_ge(on["x_odd"], k // 2 + 1)
                pool.dma_start(x_park[k], x_t[:, k]).then_inc(on["x_parked"], 16)
            pool.wait_ge(on["mem_out"], KT)
            pool.dma_start(m_park.rearrange("k p m -> p k m"), mem_t[:]).then_inc(on["mem_parked"], 16)

            pool.wait_ge(on["act_ready"], KT)
            pool.wait_ge(on["rstd_ready"], 1)
            pool.wait_ge(on["vec_ready"], 2)
            chain.link(nc.gpsimd.memset(rot[:], 0.0))
            for m0, base, fill in ((0, -CH, -1.0), (CH, 0, 1.0)):
                half = rot[:, m0:m0 + CH]
                chain.put(nc.gpsimd.affine_select(out=half, in_=half, compare_op=ALU.not_equal, fill=fill, base=base,
                                                  pattern=[[-1, CH]], channel_multiplier=1))
            pool.dma_start(pos_row[:], positions).then_inc(on["pos_in"], 16)
            pool.dma_start(freq_col[:], inv_freq).then_inc(on["pos_in"], 16)
            chain.link(nc.gpsimd.iota(dist[:], pattern=[[1, S]], base=0, channel_multiplier=-1,
                                      allow_small_or_imprecise_dtypes=True))
            nc.gpsimd.memset(pos_rowf[:], 0.0).then_inc(on["dist_ready"], 1)

            slabs, heads = Count(5), Count()

            def park_y(tile):
                pool.wait_ge(on["heads_done"], heads.at(2))
                slot = heads.first % 2
                pool.dma_start(y_park[bass.ds(tile, 1), :, :].rearrange("a p s -> p a s"),
                               ytile[:, slot:slot + 1, :]).then_inc(y_parked[slot], 16)
                heads.step()

            def make_gate(g):
                pool.wait_ge(on["gate_sig"], heads.at(1))
                nc.gpsimd.tensor_tensor(gate[:], g, gtmp[:], ALU.mult).then_inc(on["gate_ready"], 1)

            with pool.Fori(0, NH // 2) as i:
                slabs.enter(i, 8)
                heads.enter(i, 2)
                for par in range(2):
                    make_gate(stage[:, par, 3])
                    park_y(i * 2 + (Y_RET + par))
                    slabs.step(4)
            slabs.leave(NH // 2)
            heads.leave(NH // 2)

            with pool.Fori(0, NH // 2) as i:
                slabs.enter(i, 8)
                heads.enter(i, 2)
                for par in range(2):
                    hd = i * 2 + par
                    pool.wait_ge(on["dn_pair"], hd + 1)
                    for n in range(7):
                        if n == 2:
                            pool.wait_ge(on["dn_at"], hd + 1)
                            nc.gpsimd.tensor_tensor(flat3(dn_at[:]), flat3(dn_at[:]), every_tile(tri_incl[:]),
                                                    ALU.mult).then_inc(on["dn_masked"], 1)
                            pool.wait_ge(on["dn_x"], hd * 7 + 1)
                        if n >= 3:
                            pool.wait_ge(on["dn_u"], hd * 6 + (n - 2))
                        lvl = lvl_mask[:, 6 - n]
                        nc.gpsimd.tensor_tensor(flat3(dn_ctt[:, n % 2]), flat3(dn_lt[:]), every_tile(lvl),
                                                ALU.mult).then_inc(on["dn_ct"], 1)
                    make_gate(stage[:, par, 3])
                    park_y(i * 2 + (Y_DN + par))
                    slabs.step(4)
            slabs.leave(NH // 2)
            heads.leave(NH // 2)

            for par in range(2):
                for hh in range(2):
                    make_gate(stage[:, par, 4 + hh])
                    park_y(Y_GLA + 2 * par + hh)
                slabs.step(6)

            pool.dma_start(mem_back[:], m_park.rearrange("k p m -> p k m")).then_inc(on["mem_back"], 16)

            def park_kv(ready, base, tiles, dst, i, slot):
                pool.wait_ge(on[ready], i * 2 + (base + slot + 1))
                pool.dma_start(dst[bass.ds(i * 2 + slot, 1), :, :].rearrange("a p s -> p a s"),
                               tiles[:, slot:slot + 1, :]).then_inc(kv_tile_parked[slot], 16)

            def park_keys(first, n):
                for idx in range(first, first + n):
                    park_kv("slab_out", KV0, kv_t, k_park, idx // 2, idx % 2)

            for hd in range(NH):
                if hd == NH - 1:
                    park_keys(4, 2)
                pool.wait_ge(on["sb_x"], hd + 1)
                for j in range(NT):
                    d = packed(sb_x, j)[:, 0:P]
                    last = nc.gpsimd.affine_select(out=d, in_=d, compare_op=ALU.is_gt, fill=FAR, base=0,
                                                   pattern=[[1, P]], channel_multiplier=-1)
                    last.then_inc(on["sb_masked"], 1)
                if hd >= 2:
                    park_keys(6 * (hd - 2), 4)
                park_y(Y_SB + hd)

            park_keys(10, 2)
            pool.wait_ge(on["heads_done"], 4 * NH + 1)
            for j in range(2):
                pool.wait_ge(y_parked[j], 16 * (2 * NH + 1))

            def load_y(at, n):
                pool.dma_start(main[:, bass.ds(at, n)], y_park[bass.ds(at, n)].rearrange("k p s -> p k s")).then_inc(
                    on["y_back"], 16)

            with pool.Fori(KV_SIDE // 2, KT // 2) as i:
                load_y(i * 4 - 2 * KV_SIDE, 4)
                for slot in range(2):
                    park_kv("slab_out", KV0, kv_t, k_park, i, slot)
            with pool.Fori(0, KT // 4) as i:
                load_y(i * 2 + KT // 2, 2)
                for slot in range(2):
                    park_kv("kv_vout", 0, v_t, v_park, i, slot)
            with pool.Fori(KT // 4, KT // 2) as i:
                for slot in range(2):
                    park_kv("kv_vout", 0, v_t, v_park, i, slot)

            pool.wait_ge(on["x_parked"], 16 * KT)
            for q in range(4):
                pool.wait_ge(on["act_ready"], KT + 4 * q + 4)
                pool.dma_start(main[:, 4 * q:4 * q + 4], x_park[4 * q:4 * q + 4].rearrange("k p s -> p k s")).then_inc(
                    main_back[q], 16)

            squares = Count()

            def sum_squares(park=False, squared=xsq):
                for k in range(KT):
                    if park:
                        pool.wait_ge(on["slab_out"], OUT0 + k + 1)
                        pool.dma_start(x_park[k], main[:, k]).then_inc(on["x_parked"], 16)
                    pool.wait_ge(on["xsq_ready"], squares.at(1))
                    if k == 0:
                        ins = nc.gpsimd.tensor_copy(xacc[:], squared[:, 0])
                    else:
                        pool.wait_ge(on["xacc_ready"], squares.at())
                        ins = nc.gpsimd.tensor_tensor(xacc[:], xacc[:], squared[:, k % 2], ALU.add)
                    ins.then_inc(on["xacc_ready"], 1)
                    squares.step()

            sum_squares(park=True)

            for j in range(2):
                pool.wait_ge(kv_tile_parked[j], 16 * KT)
            with pool.Fori(0, NH // 2) as i:
                for par in range(2):
                    pool.wait_ge(on["cx_done"], i * 2 + (par + 1))
                    for dst, src in ((kh, k_park), (vh, v_park)):
                        pool.dma_start(dst[:, par], src[bass.ds(i * 2 * NH + par * NH, NH)].rearrange(
                            "k p m -> p k m")).then_inc(kv_loaded[par], 16)
            pool.wait_ge(on["x_parked"], 2 * 16 * KT)
            for q in range(4):
                pool.wait_ge(on["act_ready"], 3 * KT + 4 * q + 4)
                pool.dma_start(main[:, 4 * q:4 * q + 4], x_park[4 * q:4 * q + 4].rearrange("k p s -> p k s")).then_inc(
                    main_back[q], 16)
            sum_squares()
            sum_squares(squared=relu)

        @block.tensor
        def _(pe):
            slabs, act, act_out, heads, levels = Count(), Count(), Count(), Count(), Count()
            mm = nc.tensor.matmul

            def hi_lo(ps, wh, wl, xh, xl, first, last):
                mm(ps, wh, xh, start=first, stop=False)
                mm(ps, wh, xl, start=False, stop=False)
                return mm(ps, wl, xh, start=False, stop=last)

            def window(mixer=None, n=S, new_act=False, new_mem=False, last_use=False):
                slot = slabs.first % 2
                pe.wait_ge(on["slab_lo"], slabs.at(1))
                if slabs.first >= 2:
                    pe.wait_ge(on["slab_out"], slabs.at(-1))
                wh = w_hi[:, slot].rearrange("p (k n) -> p k n", k=KT)
                wl = w_lo[:, slot].rearrange("p (k n) -> p k n", k=KT)
                running = mixer is not None
                for k in range(KT):
                    if new_act:
                        pe.wait_ge(on["act_ready"], act.at(k + 1))
                    if new_mem:
                        pe.wait_ge(on["mem_split"], k + 1)
                    last = hi_lo(G[slot][:, 0:n], wh[:, k], wl[:, k], act_hi[:, k, 0:n], act_lo[:, k, 0:n],
                                 k == 0, k == KT - 1)
                    if k == KT - 1:
                        last.then_inc(on["slab_mul"], 1)
                    elif last_use:
                        last.then_inc(on["act_free"], 1)
                    if running and k >= 3:
                        running = next(mixer) != SEG
                if running:
                    run_segment(mixer)
                if new_act:
                    act.step(KT)
                slabs.step()

            def turn(dst, src, done, n=NT):
                for t in range(n):
                    last = nc.tensor.transpose(dst[:, t * P:(t + 1) * P], src(t), ident[:])
                last.then_inc(on[done], 1)

            def head_starts():
                pe.wait_ge(on["heads_done"], heads.at(1))

            def norm_sum():
                pe.wait_ge(on["sq_ready"], heads.at(1))
                mm(M[1][:], ones[:], sq[:], start=True, stop=True).then_inc(on["norm_sum"], 1)

            def scores(k, q, done):
                for j in range(NT):
                    last = mm(score_ps(j), k[:, j * P:(j + 1) * P], q[:, j * P:S], start=True, stop=True)
                last.then_inc(on[done], 1)

            def attend(weights):
                pe.wait_ge(on["vtok_ready"], heads.at(1))
                for j in range(NT):
                    last = mm(M[0][:, j * P:S], vtok[:, j], packed(weights, j), start=j == 0, stop=j == NT - 1)
                last.then_inc(on["o_ready"], 1)

            pe.wait_ge(on["consts"], 1)
            for k in range(KT):
                if k % (KT // 2) == 0:
                    pe.wait_ge(x_loaded[2 * k // KT], 16 * NT)
                if k >= 6:
                    pe.wait_ge(on["x_odd" if k % 2 else "x_even"], (k - 6) // 2 + 1)
                turn(M[k % 6], lambda t: x_tok[:, t, k * P:(k + 1) * P], "x_turned")
            pe.wait_ge(on["vec_in"], 16 * 8)
            nc.tensor.transpose(G[0][:, 0:V_N], vec_rows[:], ident[0:V_N, 0:V_N])
            nc.tensor.transpose(G[1][:, 0:C_N], conv_rows[:], ident[0:C_N, 0:C_N]).then_inc(on["vec_turned"], 1)
            pe.wait_ge(on["x_diag"], 1)
            pe.wait_ge(on["x_even"], KT // 2)
            mm(M[0][:], ones[:], diag_r[:].rearrange("p t s -> p (t s)"), start=True, stop=True).then_inc(
                on["x_bcast"], 1)

            def turn_mem():
                pe.wait_ge(on["x_odd"], KT // 2)
                pe.wait_ge(on["mem_scaled"], 1)
                for k in range(KT):
                    if k >= 8 and k % 2 == 0:
                        pe.wait_ge(on["mem_out"], k - 6)
                    for t in range(MT):
                        last = nc.tensor.transpose(M[2 + (k // 2) % 4][:, (k % 2) * NMEM + t * P:][:, 0:P],
                                                   x_tok[:, t, k * P:(k + 1) * P], ident[:])
                    if k % 2:
                        last.then_inc(on["mem_turned"], 1)
                    if k % 4 == 3:
                        yield HOP
                yield SEG

            def tables():
                pe.wait_ge(on["pos_ready"], 1)
                mm(M[0][:], ones[0:1, :], pos_rowf[:], start=True, stop=True).then_inc(on["pos_bcast"], 1)
                yield SEG
                yield SEG
                pe.wait_ge(on["rows_ready"], 1)
                for n, r in enumerate((BETA, DECAY)):
                    for t in range(NT):
                        last = nc.tensor.transpose(M[1 + n][:, t * NH:(t + 1) * NH], rows[r:r + NH, t * P:(t + 1) * P],
                                                   ident[r:r + NH, r:r + NH])
                last.then_inc(on["cols_turned"], 1)
                yield SEG

            def retention(par):
                q, k, v = (stage[:, par, t] for t in range(3))
                head_starts()
                pe.wait_ge(on["slab_out"], slabs.at())
                mm(M[0][:], rot[:], q, start=True, stop=True)
                mm(M[1][:], rot[:], k, start=True, stop=True).then_inc(on["ret_rot"], 1)
                turn(M[2], lambda t: v[:, t * P:(t + 1) * P], "vt_ready")
                yield SEG
                pe.wait_ge(on["ret_qk"], heads.at(1))
                scores(ret_k, ret_q, "ret_scores")
                yield SEG
                pe.wait_ge(on["ret_w"], heads.at(1))
                attend(ret_wt)
                yield HOP
                yield HOP
                yield HOP
                norm_sum()
                heads.step()
                yield SEG
                yield SEG

            def delta_norms(hd):
                for n, t in enumerate((dn_gb, dn_dt)):
                    pe.wait_ge(on["dn_sq"], hd * 2 + (n + 1))
                    mm(M[n][:], ones[:], t[:], start=True, stop=True).then_inc(on["dn_l2"], 1)

            def delta_first():
                yield SEG
                head_starts()
                yield HOP
                delta_norms(0)
                yield SEG

            def delta(par, hd):
                q, k, v = (dn_c[:, t] for t in range(3))
                tile = lambda t, c: t[:, c * P:(c + 1) * P]
                head_starts()
                pe.wait_ge(on["bcast_rows"], hd + 1)
                mm(M[0][:], ones[DECAY:DECAY + NH, :], dn_rows[DECAY:DECAY + NH, :], start=True, stop=True)
                mm(M[1][:], ones[BETA:BETA + NH, :], dn_rows[BETA:BETA + NH, :], start=True, stop=True).then_inc(
                    on["bcast_ps"], 1)
                yield HOP
                pe.wait_ge(on["dn_qk"], hd + 1)
                turn(M[4], lambda t: tile(v, t), "vt_ready")
                yield HOP
                for c in range(NT):
                    mm(tile(M[2], c), tile(k, c), tile(k, c), start=True, stop=True)
                    last = mm(tile(M[3], c), tile(k, c), tile(q, c), start=True, stop=True)
                last.then_inc(on["dn_gram"], 1)
                yield HOP
                turn(M[5], lambda t: tile(k, t), "dn_tok")
                for _ in range(3):
                    yield HOP
                pe.wait_ge(on["vtok_ready"], heads.at(1))
                pe.wait_ge(on["dn_ct"], hd * 7 + 1)
                turn(M[4], lambda t: dn_ctt[:, 0, t * P:(t + 1) * P], "dn_c1t")
                yield HOP
                yield HOP
                for n in range(1, 7):
                    pe.wait_ge(on["dn_ct"], hd * 7 + (n + 1))
                    pe.wait_ge(on["dn_x"], hd * 7 + n)
                    for c in range(NT):
                        last = mm(tile(M[2], c), tile(dn_ctt[:, n % 2], c), tile(dn_xx, c), start=True, stop=True)
                    last.then_inc(on["dn_u"], 1)
                    yield HOP
                    yield HOP
                    pe.wait_ge(on["dn_uev"], hd * 6 + n)
                    for c in range(NT):
                        if n < 6:
                            mm(tile(M[3], c), tile(dn_xt, c), tile(dn_uu, c), start=True, stop=True)
                        last = mm(tile(M[4], c), tile(dn_uu, c), tile(dn_xt, c), start=True, stop=True)
                    last.then_inc(on["dn_v"], 1)
                    if n in (1, 4):
                        yield SEG
                    elif n == 5:
                        yield HOP
                        delta_norms(hd + 1)
                        yield HOP
                    else:
                        yield HOP
                        yield HOP
                pe.wait_ge(on["dn_x"], hd * 7 + 7)
                pe.wait_ge(on["dn_bvk"], hd + 1)
                for c in range(NT):
                    mm(tile(M[2], c), tile(dn_xt, c), tile(dn_bv, c), start=True, stop=True)
                    last = mm(tile(M[3], c), tile(dn_kbe, c), tile(dn_xt, c), start=True, stop=True)
                last.then_inc(on["dn_uw"], 1)
                yield SEG
                pe.wait_ge(on["dn_uwev"], hd + 1)
                pe.wait_ge(on["dn_qg"], hd + 1)
                pe.wait_ge(on["dn_masked"], hd + 1)
                pe.wait_ge(on["dn_inv"], hd * 2 + 4)
                for c in range(NT):
                    if c:
                        pe.wait_ge(on["dn_state"], hd * 3 + c)
                        mm(M[4][:, 0:P], tile(dn_wt, c), dn_st[:], start=True, stop=True).then_inc(on["dn_ws"], 1)
                        mm(tile(M[0], c), dn_st[:], tile(dn_qg, c), start=True, stop=False)
                        yield HOP
                        pe.wait_ge(on["dn_vnew"], hd * 3 + c)
                    v_new = dn_vn[:] if c else tile(dn_uu, 0)
                    if c < NT - 1:
                        mm(M[5][:, 0:P], tile(dn_kdec, c), v_new, start=True, stop=True).then_inc(on["dn_ds"], 1)
                    last = mm(tile(M[0], c), v_new, tile(dn_at, c), start=c == 0, stop=True)
                    if c < NT - 1:
                        yield HOP
                last.then_inc(on["o_ready"], 1)
                yield HOP
                yield HOP
                norm_sum()
                heads.step()
                yield SEG

            def gla_logits():
                pe.wait_ge(on["up_in"], 16)
                for p in range(2):
                    mm(M[p][:], gla_up[:, p * P:(p + 1) * P], rows[0:RANK, :], start=True, stop=True).then_inc(
                        on["gla_z"], 1)

            def gla(par):
                half = lambda t, hh: t[hh * DK:(hh + 1) * DK]
                cut = lambda t, a, b: t[:, a * P:b * P]
                k = stage[:, par, 1]
                head_starts()
                if par == 0:
                    gla_logits()
                    yield HOP
                pe.wait_ge(on["gla_qs"], par + 1)
                for hh in range(2):
                    for c in range(NT):
                        last = mm(cut(M[2 + hh], c, c + 1), cut(half(k, hh), c, c + 1),
                                  cut(half(gla_qs, hh), c, c + 1), start=True, stop=True)
                last.then_inc(on["gla_diag"], 1)
                yield HOP
                if par == 0:
                    pe.wait_ge(on["gla_l"], 1)
                turn(M[0], lambda t: stage[:, par, 2, t * P:(t + 1) * P], "vt_ready")
                yield HOP
                for n in range(9):
                    for _ in range((7 - 3 * par, 2)[n] if n < 2 else 3 if n % 2 else 5):
                        yield HOP
                    qk = gla_qk[:, n % 2]
                    pe.wait_ge(on["gla_qe"], par * 9 + n + 1)
                    ps = [M[4 + hh] if n % 2 == 0 else M[2 + hh] for hh in range(2)]
                    if n == 1:
                        pe.wait_ge(on["gla_lvout"], par * 8 + 1)
                    elif n in (2, 3):
                        pe.wait_ge(on["gla_topout"], par * 2 + n - 1)
                    elif n >= 4:
                        pe.wait_ge(on["gla_lvout"], par * 8 + n - 2)
                    for hh in range(2):
                        if n == 0:
                            for c in range(2):
                                last = mm(cut(ps[hh], 2 * c, 2 * c + 2), cut(half(qk, hh), c, c + 1),
                                          cut(half(qk, hh), 2, 4), start=True, stop=True)
                        elif n == 1:
                            for c in range(2):
                                last = mm(cut(ps[hh], c, c + 1), cut(half(qk, hh), 2 * c, 2 * c + 1),
                                          cut(half(qk, hh), 2 * c + 1, 2 * c + 2), start=True, stop=True)
                        else:
                            for c in range(NT):
                                last = mm(cut(ps[hh], c, c + 1), cut(half(qk, hh), c, c + 1),
                                          cut(half(qk, hh), c, c + 1), start=True, stop=True)
                    last.then_inc(on["gla_lv"], 1)
                    yield SEG if n in (1, 3, 5, 7) else HOP
                for hh in range(2):
                    if hh:
                        head_starts()
                        turn(M[1], lambda t: stage[:, par, 3, t * P:(t + 1) * P], "vt_ready")
                        yield HOP
                        yield HOP
                    pe.wait_ge(on["gla_lvout"], par * 8 + 8)
                    pe.wait_ge(on["gla_topout"], par * 2 + 2)
                    pe.wait_ge(on["vtok_ready"], heads.at(1))
                    s, o = gla_s[:, hh], gla_o[:, hh]
                    for c in range(NT):
                        for kt in range(c):
                            at = (0, 3 * P, 5 * P)[kt] + (c - 1 - kt) * P
                            mm(cut(M[0], c, c + 1), vtok[:, kt], o[:, at:at + P], start=kt == 0, stop=False)
                        last = mm(cut(M[0], c, c + 1), vtok[:, c], cut(s, c, c + 1), start=c == 0, stop=True)
                    last.then_inc(on["o_ready"], 1)
                    yield HOP
                    yield HOP
                    norm_sum()
                    heads.step()
                    yield SEG

            def stick(par):
                for hh in range(2):
                    q, k, v = (stage[:, par, 3 * hh + t] for t in range(3))
                    hd = 2 * par + hh
                    head_starts()
                    if hh == 0:
                        pe.wait_ge(on["slab_out"], slabs.at())
                    turn(M[2], lambda t: v[:, t * P:(t + 1) * P], "vt_ready")
                    scores(k, q, "sb_scores")
                    yield SEG
                    pe.wait_ge(on["sb_lk"], hd + 1)
                    for i in range(NT):
                        bank, at = SC[i]
                        for j in range(i, NT):
                            w = WID[j]
                            last = mm(M[bank][:, at + (j - i) * P:at + WID[i]], (tri_suffix if j == i else ones)[:],
                                      packed(sb_m, j), start=j == i, stop=j == NT - 1)
                    last.then_inc(on["sb_cum"], 1)
                    yield SEG
                    pe.wait_ge(on["sb_w"], hd + 1)
                    attend(sb_x)
                    yield HOP
                    yield HOP
                    norm_sum()
                    heads.step()
                    yield SEG

            window(new_act=True)
            window(turn_mem())
            mixer = tables()
            for _ in range(3):
                window(mixer)
            with pe.Fori(0, NH // 2) as i:
                slabs.enter(i, 8)
                heads.enter(i, 2)
                for par in range(2):
                    mixer = retention(par)
                    for _ in range(4):
                        window(mixer)
            slabs.leave(NH // 2)
            heads.leave(NH // 2)
            mixer = delta_first()
            for _ in range(2):
                window(mixer)
            with pe.Fori(0, NH // 2) as i:
                slabs.enter(i, 8)
                heads.enter(i, 2)
                for par in range(2):
                    mixer = delta(par, i * 2 + par)
                    for _ in range(4):
                        window(mixer)
            slabs.leave(NH // 2)
            heads.leave(NH // 2)
            for par in range(2):
                mixer = gla(par)
                for _ in range(6):
                    window(mixer)
            mixer = stick(0)
            for n in range(6):
                window(mixer, last_use=n == 5)

            mixer = stick(1)
            for j in range(KV_SIDE):
                window(None if j % 2 else mixer, n=NMEM, new_mem=j == 0)
            with pe.Fori(0, (KT - KV_SIDE) // 2) as i:
                slabs.enter(i, 2)
                for _ in range(2):
                    window(n=NMEM)
            slabs.leave((KT - KV_SIDE) // 2)

            def turn_values(idx, slot):
                pe.wait_ge(on["slab_out"], slabs.at())
                for t in range(MT):
                    last = nc.tensor.transpose(M[slot][:, t * P:(t + 1) * P], kv_t[:, slot, t * P:(t + 1) * P], ident[:])
                last.then_inc(on["kv_turned"], 1)
                yield SEG

            window(n=NMEM)
            window(turn_values(0, 0), n=NMEM)
            with pe.Fori(1, KT // 2 - 1) as i:
                slabs.enter(i - 1, 2)
                window(turn_values(i * 2 - 1, 1), n=NMEM)
                window(turn_values(i * 2, 0), n=NMEM)
            slabs.leave(KT // 2 - 2)
            window(turn_values(KT - 3, 1), n=NMEM)
            window(turn_values(KT - 2, 0), n=NMEM, last_use=True)
            window(turn_values(KT - 1, 1), new_act=True)

            def matrix(n):
                with pe.Fori(0, n // 2) as i:
                    slabs.enter(i, 2)
                    window()
                    window()
                slabs.leave(n // 2)

            def total(n):
                for _ in range(6):
                    yield HOP
                pe.wait_ge(on["xacc_ready"], n * KT)
                mm(M[5][:], ones[:], xacc[:], start=True, stop=True).then_inc(on["x_total"], 1)
                yield SEG

            matrix(KT - 2)
            window(last_use=True)

            def attention(par, hd, beside=False):
                tile = lambda t, c: t[:, c * P:(c + 1) * P]
                pe.wait_ge(on["slab_out"], slabs.at())
                pe.wait_ge(on["cx_done"], hd + 2)
                pe.wait_ge(kv_loaded[par], 32 * (hd // 2 + 1))
                for st in range(NT):
                    for k in range(NH):
                        last = mm(M[st // 2][:, (st % 2) * NMEM:(st % 2 + 1) * NMEM], tile(cstage[:, par, k], st),
                                  kh[:, par, k], start=k == 0, stop=k == NH - 1)
                last.then_inc(on["cx_scores"], 1)
                for _ in range(6 if beside else 9):
                    yield HOP
                pe.wait_ge(on["cx_p"], hd + 1)
                for st in range(NT):
                    for mt in range(MT):
                        last = nc.tensor.transpose(tile(M[2 + mt], st), prob[:, st, mt * P:(mt + 1) * P], ident[:])
                last.then_inc(on["cx_pt"], 1)
                yield HOP if beside else SEG
                if beside:
                    yield HOP
                pe.wait_ge(on["cx_ptok"], hd + 1)
                for k in range(NH):
                    bank = (4, 5, 0, 1)[k]
                    for mt in range(MT):
                        last = mm(M[bank][:], vh[:, par, k, mt * P:(mt + 1) * P], prob_t[:, mt], start=mt == 0,
                                  stop=mt == MT - 1)
                    last.then_inc(on["cx_o"], 1)
                yield SEG
                yield SEG
                yield SEG

            window(total(1), new_act=True)
            for _ in range(3):
                window()
            for hd in range(NH - 1):
                mixer = attention(hd % 2, hd)
                for n in range(4):
                    window(mixer, last_use=hd == NH - 2 and n == 3)

            window(attention((NH - 1) % 2, NH - 1, beside=True), new_act=True)
            matrix(KT - 2)
            window(last_use=True)

            def down(c):
                slot = slabs.first % 2
                pe.wait_ge(on["slab_lo"], slabs.at(1))
                pe.wait_ge(on["slab_out"], slabs.at(-1))
                wh = w_hi[:, slot].rearrange("p (k n) -> p k n", k=MC)
                wl = w_lo[:, slot].rearrange("p (k n) -> p k n", k=MC)
                for j in range(2):
                    for k in range(MC):
                        pe.wait_ge(on["u_ready"], c * MC + (k + 1))
                        last = hi_lo(M[2 * slot + j][:], wh[:, k, j * P:(j + 1) * P], wl[:, k, j * P:(j + 1) * P],
                                     u_hi[:, k], u_lo[:, k], k == 0, k == MC - 1)
                last.then_inc(on["slab_mul"], 1)
                slabs.step()

            window(total(2), new_act=True)
            for _ in range(MC - 1):
                window()
            for _ in range(MC):
                down(0)
            with pe.Fori(1, NCH) as c:
                slabs.enter(c - 1, 2 * MC)
                for _ in range(MC):
                    window()
                for _ in range(MC):
                    down(c)
            slabs.leave(NCH - 1)

            pe.wait_ge(on["slab_out"], slabs.at())
            for n in range(NT * 4):
                t, g = n // 4, n % 4
                if t == 0:
                    pe.wait_ge(on["fin_x"], 4 * g + 4)
                if n >= 4:
                    pe.wait_ge(on["fin_odd" if n % 2 else "fin_even"], (n - 4) // 2 + 1)
                turn(M[n % 4], lambda k: main[:, 4 * g + k, t * P:(t + 1) * P], "fin_turned")
                if n == 3:
                    pe.wait_ge(on["xacc_ready"], 3 * KT)
                    for j in range(NT):
                        last = mm(M[4][:, j:j + 1], xacc[:, j * P:(j + 1) * P], ones[:, 0:1], start=True, stop=True)
                    last.then_inc(on["fin_sum"], 1)

        @block.scalar
        def _(act):
            chain = Chain(act, on["act_chain"])
            slabs, heads = Count(), Count()
            fn = nc.scalar.activation
            RET_LINKS, DN_LINKS = 3, 13

            def split_hi():
                nxt = slabs.first + 1
                slot = nxt % 2
                act.wait_ge(raw_in[slot], slabs.at(1) * 8 + 8 * slot)
                if nxt >= 2:
                    act.wait_ge(on["slab_mul"], slabs.at())
                fn(w_hi[:, slot], w_raw[:, slot], ACT.Copy).then_inc(on["slab_hi"], 1)

            def window(mixer=None):
                split_hi()
                run_segment(mixer)
                slabs.step()

            def silu_part(t):
                chain.link(fn(t, t, ACT.Exp, scale=-1.0))
                chain.link(fn(t, t, ACT.Ln, bias=1.0))
                return fn(t, t, ACT.Exp, scale=-1.0)

            def rsqrt(dst, src, scale, eps=True, power=-0.5):
                chain.link(fn(dst, src, ACT.Ln, scale=scale, bias=eps_col[:]))
                return fn(dst, dst, ACT.Exp, scale=power)

            def head_starts():
                act.wait_ge(on["heads_done"], heads.at(1))

            def values(bank):
                act.wait_ge(on["vt_ready"], heads.at(1))
                fn(vtok[:].rearrange("p t s -> p (t s)"), bank[:], ACT.Copy).then_inc(on["vtok_ready"], 1)

            def gate_sigmoid(gated):
                act.wait_ge(on["gate_clamped"], gated + 1)
                silu_part(gtmp[:]).then_inc(on["gate_sig"], 1)

            def norm():
                act.wait_ge(on["o_ready"], heads.at(1))
                fn(sq[:], M[0][:], ACT.Square).then_inc(on["sq_ready"], 1)
                act.wait_ge(on["norm_sum"], heads.at(1))
                rsqrt(nrm[:], M[1][:], 1.0 / P).then_inc(on["norm_ready"], 1)
                heads.step()

            nc.scalar.preload_act_table_set("natural_log_exp_and_others")
            def square_x(half):
                act.wait_ge(x_loaded[half], 16 * NT)
                for t in range(NT):
                    chain.put(fn(mem_t[:].rearrange("p k m -> p (k m)")[:, t * D // 2:(t + 1) * D // 2],
                                 x_tok[:, t, half * D // 2:(half + 1) * D // 2], ACT.Square,
                                 accum_out=cols[:, 12 * half + t:12 * half + t + 1]))
                chain.sync()

            def take_even(k):
                act.wait_ge(on["x_turned"], k + 1)
                fn(x_t[:, k], M[k % 6][:], ACT.Copy).then_inc(on["x_even"], 1)

            square_x(0)
            for k in range(0, KT // 2, 2):
                take_even(k)
            square_x(1)
            for t in range(NT):
                chain.put(fn(cols[:, t:t + 1], cols[:, t:t + 1], ACT.Identity, bias=cols[:, 12 + t:13 + t]))
            act.wait_ge(on["consts"], 1)
            chain.sync()
            chain.link(rsqrt(cols[:, 4:8], cols[:, 0:4], 1.0 / D))
            nc.scalar.copy(cols[:, 8:12], cols[:, 4:8]).then_inc(on["x_ssq"], 1)
            for k in range(KT // 2, KT, 2):
                take_even(k)
            act.wait_ge(on["vec_turned"], 1)
            fn(vecs[:], G[0][:, 0:V_N], ACT.Copy).then_inc(on["vec_ready"], 1)
            fn(convs[:], G[1][:, 0:C_N], ACT.Copy).then_inc(on["vec_ready"], 1)
            act.wait_ge(on["special_in"], 48)
            fn(w_hi[:, 0], w_raw[:, 0], ACT.Copy).then_inc(on["slab_hi"], 1)
            act.wait_ge(on["vec_ready"], 2)
            for k in range(KT):
                act.wait_ge(on["x_odd" if k % 2 else "x_even"], k // 2 + 1)
                fn(act_hi[:, k], x_t[:, k], ACT.Copy, scale=vecs[:, V_MIX + k:V_MIX + k + 1]).then_inc(on["xg_hi"], 1)
            act.wait_ge(on["x_bcast"], 1)
            fn(rstd[:], M[0][:], ACT.Copy).then_inc(on["rstd_ready"], 1)

            def mem_norm():
                act.wait_ge(on["mem_in"], 16 * MT)
                for t in range(MT):
                    chain.put(fn(mem_t[:].rearrange("p k m -> p (k m)")[:, t * D:(t + 1) * D], x_tok[:, t],
                                 ACT.Square, accum_out=cols[:, 12 + t:13 + t]))
                chain.sync()
                chain.link(rsqrt(cols[:, 14:14 + MT], cols[:, 12:12 + MT], 1.0 / D))
                for t in range(MT):
                    chain.put(fn(x_tok[:, t], x_tok[:, t], ACT.Copy, scale=cols[:, 14 + t:15 + t]))
                chain.sync()
                nc.scalar.copy(cols[:, 16:17], cols[:, 14:15]).then_inc(on["mem_scaled"], 1)
                yield SEG
                for k in range(KT):
                    act.wait_ge(on["mem_turned"], k // 2 + 1)
                    fn(mem_t[:, k], M[2 + (k // 2) % 4][:, (k % 2) * NMEM:(k % 2 + 1) * NMEM], ACT.Copy,
                       scale=vecs[:, V_MEM + k:V_MEM + k + 1]).then_inc(on["mem_out"], 1)
                yield SEG

            def tables():
                b, a = slice(BETA, BETA + NH), slice(DECAY, DECAY + NH)
                act.wait_ge(on["small_in"], 32)
                act.wait_ge(on["rows_out"], 1)
                chain.put(fn(sq[b], rows[b], ACT.Exp, scale=-1.0))
                chain.put(fn(cols[a, 22:23], cols[a, 20:21], ACT.Exp))
                chain.link(fn(gtmp[a], rows[a], ACT.Identity, bias=cols[a, 21:22]))
                chain.link(fn(sq[a], gtmp[a], ACT.Abs))
                chain.link(fn(sq[a], sq[a], ACT.Exp, scale=-1.0))
                fn(sq[a], sq[a], ACT.Ln, bias=1.0).then_inc(on["rows_act"], 1)
                yield SEG
                act.wait_ge(on["dist_ready"], 1)
                chain.link(fn(dist[:], dist[:], ACT.Abs))
                for h in range(NH):
                    last = fn(ret_dec[:, h], dist[:], ACT.Exp, scale=LOG_GAMMA[h])
                    if h < NH - 1:
                        chain.put(last)
                last.then_inc(on["dec_exp"], 1)
                chain.sync()
                act.wait_ge(on["ang_ready"], 1)
                chain.put(fn(sin_t[:], sin_t[:], ACT.Sin))
                chain.link(fn(cos_t[:], cos_t[:], ACT.Sin))
                nc.scalar.copy(cols[:, 17:18], cols[:, 16:17]).then_inc(on["trig_ready"], 1)
                nc.scalar.preload_act_table_set("natural_log_exp_and_others")
                yield SEG
                act.wait_ge(on["cols_turned"], 1)
                for n in range(2):
                    last = fn(rcols[:, :, n * NH:(n + 1) * NH], M[1 + n][:, 0:NT * NH].rearrange("p (t h) -> p t h", h=NH),
                              ACT.Copy)
                last.then_inc(on["cols_ready"], 1)
                yield SEG

            def retention():
                head_starts()
                values(M[2])
                gate_sigmoid(heads.at())
                yield SEG
                yield SEG
                norm()
                yield SEG
                yield SEG

            def delta_silu(hd, t, temp):
                act.wait_ge(on["dn_clamped"], hd * 3 + (t + 1))
                silu_part(temp[:]).then_inc(on["dn_sig"], 1)

            def delta_squares(hd):
                for n, t in enumerate((dn_gb, dn_dt)):
                    act.wait_ge(on["dn_silu"], hd * 3 + (n + 1))
                    fn(t[:], dn_c[:, n], ACT.Square).then_inc(on["dn_sq"], 1)

            def delta_norms(hd):
                for n, t in enumerate((dn_gb, dn_dt)):
                    act.wait_ge(on["dn_l2"], hd * 2 + (n + 1))
                    rsqrt(t[:], M[n][:], 1.0).then_inc(on["dn_inv"], 1)

            def delta_first():
                for t in range(2):
                    delta_silu(0, t, dn_temp[t])
                delta_squares(0)
                yield SEG
                delta_norms(0)
                delta_silu(0, 2, dn_temp[2])
                yield SEG

            def delta(hd):
                act.wait_ge(on["bcast_ps"], hd + 1)
                fn(dn_gb[:], M[0][:], ACT.Copy).then_inc(on["dn_gbev"], 1)
                act.wait_ge(on["dn_dd"], hd + 1)
                fn(dn_dt[:], dn_dt[:], ACT.Exp).then_inc(on["dn_dt"], 1)
                act.wait_ge(on["dn_cols"], hd + 1)
                chain.link(fn(dn_cols[:, 0:3].rearrange("p a t -> p (a t)"),
                              dn_cols[:, 4:7].rearrange("p a t -> p (a t)"), ACT.Exp))
                nc.scalar.copy(cols[:, 18:19], cols[:, 17:18]).then_inc(on["dn_colexp"], 1)
                fn(dn_gb[:], dn_gb[:], ACT.Exp).then_inc(on["dn_eg"], 1)

                def take_u(n):
                    act.wait_ge(on["dn_u"], hd * 6 + n)
                    fn(dn_uu[:], M[2][:], ACT.Copy).then_inc(on["dn_uev"], 1)

                take_u(1)
                yield SEG
                take_u(2)
                take_u(3)
                delta_silu(hd + 1, 0, dn_temp[0])
                take_u(4)
                delta_silu(hd + 1, 1, dn_temp[1])
                yield SEG
                take_u(5)
                delta_squares(hd + 1)
                take_u(6)
                delta_norms(hd + 1)
                act.wait_ge(on["dn_uw"], hd + 1)
                chain.put(fn(dn_uu[:], M[2][:], ACT.Copy))
                chain.sync()
                fn(dn_wt[:], M[3][:], ACT.Copy).then_inc(on["dn_uwev"], 1)
                yield SEG
                delta_silu(hd + 1, 2, dn_temp[2])
                gate_sigmoid(heads.at())
                norm()
                yield SEG

            def gla_logits():
                for p in range(2):
                    act.wait_ge(on["gla_z"], p + 1)
                    chain.link(fn(gla_t[:, p], M[p][:], ACT.Identity, bias=convs[:, C_BUP + p:C_BUP + p + 1]))
                    chain.link(fn(gla_e[:, p], gla_t[:, p], ACT.Abs))
                    chain.link(fn(gla_e[:, p], gla_e[:, p], ACT.Exp, scale=-1.0))
                    fn(gla_e[:, p], gla_e[:, p], ACT.Ln, bias=1.0).then_inc(on["gla_l"], 1)

            def gla(par):
                head_starts()
                if par == 0:
                    gla_logits()
                values(M[0])
                gate_sigmoid(heads.at())
                for n in range(9):
                    act.wait_ge(on["gla_d"], par * 9 + n + 1)
                    fn(gla_e[:, n % 2], gla_e[:, n % 2], ACT.Exp, scale=1.0 / 16).then_inc(on["gla_e"], 1)
                    if n < 2:
                        act.wait_ge(on["gla_lv"], par * 9 + n + 1)
                        for hh in range(2):
                            bank, o = M[4 - 2 * n + hh], gla_o[:, hh]
                            if n == 0:
                                last = fn(o[:, P:5 * P], bank[:], ACT.Copy)
                            else:
                                chain.put(fn(o[:, 0:P], bank[:, 0:P], ACT.Copy))
                                last = fn(o[:, 5 * P:6 * P], bank[:, P:2 * P], ACT.Copy)
                            if hh == 0:
                                chain.put(last)
                        chain.sync()
                        last.then_inc(on["gla_topout"], 1)
                    if n in (1, 3, 5, 7):
                        yield SEG
                norm()
                yield SEG
                head_starts()
                values(M[1])
                gate_sigmoid(heads.at())
                norm()
                yield SEG

            def stick(par):
                for hh in range(2):
                    hd = 2 * par + hh
                    head_starts()
                    values(M[2])
                    act.wait_ge(on["sb_scores"], hd + 1)
                    parts = ((0, 512, M[3]), (OFF[1], WID[1], M[4]), (OFF[2], WID[2] + WID[3], M[5]))
                    for at, n, bank in parts:
                        last = fn(sb_x[:, at:at + n], bank[:, 0:n], ACT.Copy, scale=QSCALE)
                        if at < OFF[2]:
                            chain.put(last)
                    chain.sync()
                    last.then_inc(on["sb_x"], 1)
                    act.wait_ge(on["sb_masked"], 4 * hd + 4)
                    chain.link(fn(sb_l[:], sb_x[:], ACT.Abs))
                    chain.link(fn(sb_l[:], sb_l[:], ACT.Exp, scale=-1.0))
                    fn(sb_l[:], sb_l[:], ACT.Ln, bias=1.0).then_inc(on["sb_l"], 1)
                    yield SEG
                    act.wait_ge(on["sb_z"], hd + 1)
                    fn(sb_x[:], sb_x[:], ACT.Exp).then_inc(on["sb_w"], 1)
                    yield SEG
                    norm()
                    yield SEG

            mixer = mem_norm()
            for _ in range(2):
                window(mixer)
            mixer = tables()
            for _ in range(3):
                window(mixer)
            with act.Fori(0, NH // 2) as i:
                slabs.enter(i, 8)
                heads.enter(i, 2)
                chain.count.enter(i, 2 * RET_LINKS)
                for par in range(2):
                    mixer = retention()
                    for _ in range(4):
                        window(mixer)
            slabs.leave(NH // 2)
            heads.leave(NH // 2)
            chain.count.leave(NH // 2)
            mixer = delta_first()
            for _ in range(2):
                window(mixer)
            with act.Fori(0, NH // 2) as i:
                slabs.enter(i, 8)
                heads.enter(i, 2)
                chain.count.enter(i, 2 * DN_LINKS)
                for par in range(2):
                    mixer = delta(i * 2 + par)
                    for _ in range(4):
                        window(mixer)
            slabs.leave(NH // 2)
            heads.leave(NH // 2)
            chain.count.leave(NH // 2)
            for par in range(2):
                mixer = gla(par)
                for _ in range(6):
                    window(mixer)
            mixer = stick(0)
            for _ in range(6):
                window(mixer)

            uses = Count()

            def wait_free(k):
                if k < KT - 1:
                    act.wait_ge(on["act_free"], (KT - 1) * uses.n + k + 1)
                else:
                    act.wait_ge(on["slab_mul"], slabs.at())
                    uses.step()

            act.wait_ge(on["mem_back"], 16)
            for k in range(KT):
                wait_free(k)
                fn(act_hi[:, k, 0:NMEM], mem_back[:, k], ACT.Copy).then_inc(on["mem_hi"], 1)
            mixer = stick(1)
            for j in range(KV_SIDE):
                window(None if j % 2 else mixer)
            with act.Fori(0, (KT - KV_SIDE) // 2) as i:
                slabs.enter(i, 2)
                window()
                window()
            slabs.leave((KT - KV_SIDE) // 2)

            def take_values(idx, slot):
                act.wait_ge(on["kv_turned"], idx + 1)
                act.wait_ge(kv_tile_parked[slot], (idx - slot) * 8 + 16 * (KT // 2))
                fn(v_t[:, slot], M[slot][:, 0:NMEM], ACT.Copy).then_inc(on["kv_vout"], 1)
                yield SEG

            window()
            window(take_values(0, 0))
            with act.Fori(1, KT // 2) as i:
                slabs.enter(i - 1, 2)
                window(take_values(i * 2 - 1, 1))
                window(take_values(i * 2, 0))
            slabs.leave(KT // 2 - 1)


            def activations(gain=None):
                for k in range(KT):
                    wait_free(k)
                    yield k
                    scale = {} if gain is None else {"scale": vecs[:, gain + k:gain + k + 1]}
                    fn(act_hi[:, k], main[:, k], ACT.Copy, **scale).then_inc(on["xg_hi"], 1)

            squares = Count()

            def square(k, ready, to=xsq):
                act.wait_ge(on["slab_out"], ready)
                if squares.n >= 2:
                    act.wait_ge(on["xacc_ready"], squares.n - 1)
                fn(to[:, k % 2], main[:, k], ACT.Square).then_inc(on["xsq_ready"], 1)
                squares.step()

            for k in activations():
                if k == 0:
                    act.wait_ge(on["y_back"], 16 * 6)
            run_segment(take_values(KT - 1, 1))
            window()
            for m in range(KT - 1):
                split_hi()
                square(m, slabs.at())
                slabs.step()
            for k in activations(V_CROSS):
                if k == KT - 1:
                    square(k, slabs.at())
            split_hi()
            act.wait_ge(on["x_total"], 1)
            rsqrt(rstd[:], M[5][:], 1.0 / D).then_inc(on["x_rstd"], 1)
            slabs.step()

            def attention(hd):
                act.wait_ge(on["cx_max"], hd + 1)
                for st in range(NT):
                    last = fn(prob[:, st], M[st // 2][:, (st % 2) * NMEM:(st % 2 + 1) * NMEM], ACT.Exp, scale=CSCALE,
                              bias=ccols[:, 1, st:st + 1], accum_out=ccols[:, 2, st:st + 1])
                    chain.put(last)
                chain.sync()
                nc.scalar.copy(cols[:, 19:20], cols[:, 18:19]).then_inc(on["cx_exp"], 1)
                act.wait_ge(on["cx_pt"], hd + 1)
                chain.put(fn(prob_t[:, 0], M[2][:], ACT.Copy))
                chain.sync()
                fn(prob_t[:, 1], M[3][:], ACT.Copy).then_inc(on["cx_ptok"], 1)
                yield SEG
                act.wait_ge(on["x_parked"], 2 * 16 * KT)
                for k in range(NH):
                    act.wait_ge(on["cx_o"], NH * hd + k + 1)
                    last = fn(main[:, NH * hd + k], M[(4, 5, 0, 1)[k]][:], ACT.Copy)
                    if k < NH - 1:
                        chain.put(last)
                chain.sync()
                last.then_inc(on["cx_done"], 1)
                yield SEG
                yield SEG
                yield SEG

            nc.scalar.copy(cols[:, 19:20], cols[:, 18:19]).then_inc(on["cx_done"], 2)
            for _ in range(3):
                window()
            for hd in range(NH - 1):
                mixer = attention(hd)
                for _ in range(4):
                    window(mixer)
            mixer = attention(NH - 1)
            for k in activations():
                if k == KT - NH:
                    for _ in range(4):
                        run_segment(mixer)
                if k % 4 == 0:
                    act.wait_ge(on["cx_done"], k // 4 + 3)
            window()
            for m in range(KT - 1):
                split_hi()
                square(m, slabs.at())
                slabs.step()
            for k in activations(V_MLP):
                if k == KT - 1:
                    square(k, slabs.at())
            split_hi()
            act.wait_ge(on["x_total"], 2)
            rsqrt(rstd[:], M[5][:], 1.0 / D, power=-1.0).then_inc(on["x_rstd"], 1)
            slabs.step()

            def hidden(n, j):
                act.wait_ge(on["slab_mul"], slabs.at())
                fn(relu[:, j % 2], G[(slabs.first - 1) % 2][:], ACT.Relu).then_inc(on["mlp_relu"], 1)
                act.wait_ge(on["slab_out"], slabs.at())
                fn(u_hi[:, j], uf[:, j % 2], ACT.Copy).then_inc(on["mlp_uhi"], 1)

            def chunk(c, first, last):
                for w in range(2 * MC):
                    if w == 0 and first:
                        continue
                    if 1 <= w <= MC:
                        hidden(c * MC + (w - 1), w - 1)
                    if not (last and w == 2 * MC - 1):
                        split_hi()
                    if last and w > MC:
                        final_squares(w - MC - 1)
                    slabs.step()

            def final_squares(d):
                for j in range(2):
                    square(2 * d + j, slabs.at(), relu)

            chunk(0, True, False)
            with act.Fori(1, NCH - 1) as c:
                slabs.enter(c - 1, 2 * MC)
                chunk(c, False, False)
            slabs.leave(NCH - 2)
            chunk(NCH - 1, False, True)

            final_squares(MC - 1)
            act.wait_ge(on["fin_sum"], 1)
            rsqrt(cols[:, 0:NT], M[4][:, 0:NT], 1.0 / D).then_inc(on["fin_rstd"], 1)
            act.wait_ge(on["fin_rstd"], 1)
            for n in range(0, NT * 4, 2):
                t, g = n // 4, n % 4
                act.wait_ge(on["fin_turned"], n + 1)
                if t >= 2:
                    act.wait_ge(out_done[t % 2], 16 * (t // 2))
                fn(w_raw[:, t % 2, g * S:(g + 1) * S], M[n % 4][:], ACT.Copy, scale=cols[:, t:t + 1]).then_inc(
                    on["fin_even"], 1)

        @block.vector
        def _(dve):
            chain = Chain(dve, on["dve_chain"])
            slabs, heads, parked = Count(), Count(), Count()
            v = nc.vector
            tt, ts, stt = v.tensor_tensor, v.tensor_scalar, v.scalar_tensor_tensor
            RET_LINKS, DN_LINKS = 6, 23
            f32 = lambda t: t.bitcast(F32)

            def split_lo():
                slot = (slabs.first + 1) % 2
                dve.wait_ge(on["slab_hi"], slabs.at(2))
                tt(w_lo[:, slot], w_raw[:, slot], f32(w_hi[:, slot]), ALU.subtract).then_inc(on["slab_lo"], 1)

            def evict_scaled(dst):
                dve.wait_ge(on["slab_mul"], slabs.at())
                tt(dst, G[(slabs.first - 1) % 2][:], rstd[:], ALU.mult).then_inc(on["slab_out"], 1)

            def window(mixer, dst):
                evict_scaled(dst)
                if mixer is not None:
                    dve.wait_ge(on["slab_out"], slabs.at())
                    early = next(mixer)
                    assert early == HOP
                split_lo()
                run_segment(mixer)
                slabs.step()

            def y_out(tile, slot, hg, gated=True):
                gain = vecs[:, bass.ds(tile + V_HEAD, 1)]
                dve.wait_ge(on["norm_ready"], hg + 1)
                dve.wait_ge(y_parked[slot], hg * 8 + (16 - 8 * slot))
                if gated:
                    chain.link(stt(out=nrm[:], in0=M[0][:], scalar=gain, in1=nrm[:], op0=ALU.mult, op1=ALU.mult))
                    dve.wait_ge(on["gate_ready"], hg + 1)
                    tt(ytile[:, slot], nrm[:], gate[:], ALU.mult).then_inc(on["heads_done"], 1)
                else:
                    stt(out=ytile[:, slot], in0=M[0][:], scalar=gain, in1=nrm[:], op0=ALU.mult,
                        op1=ALU.mult).then_inc(on["heads_done"], 1)

            def clamp_gate(g):
                ts(gtmp[:], g, GATE_FLOOR, None, ALU.max).then_inc(on["gate_clamped"], 1)

            v.memset(w_raw[:, 0], 0.0).then_inc(on["raw_zero"], 1)
            v.memset(cols[0:1, 30:31], 0.0).then_inc(on["heads_done"], 1)
            for k in range(1, KT, 2):
                dve.wait_ge(on["x_turned"], k + 1)
                v.tensor_copy(x_t[:, k], M[k % 6][:]).then_inc(on["x_odd"], 1)
            dve.wait_ge(on["consts"], 1)
            dve.wait_ge(on["x_ssq"], 1)
            for t in range(NT):
                last = ts(diag_r[:, t], ident[:], cols[:, 8 + t:9 + t], None, ALU.mult)
            last.then_inc(on["x_diag"], 1)
            dve.wait_ge(on["slab_hi"], 1)
            tt(w_lo[:, 0], w_raw[:, 0], f32(w_hi[:, 0]), ALU.subtract).then_inc(on["slab_lo"], 1)
            dve.wait_ge(on["vec_ready"], 2)
            for k in range(KT):
                dve.wait_ge(on["xg_hi"], k + 1)
                stt(out=act_lo[:, k], in0=x_t[:, k], scalar=vecs[:, V_MIX + k:V_MIX + k + 1], in1=f32(act_hi[:, k]),
                    op0=ALU.mult, op1=ALU.subtract).then_inc(on["act_ready"], 1)

            split_lo()
            slabs.step()
            dve.wait_ge(on["rstd_ready"], 1)
            dve.wait_ge(on["act_ready"], KT)
            dve.wait_ge(on["x_parked"], 16 * KT)

            def tables():
                b, a = slice(BETA, BETA + NH), slice(DECAY, DECAY + NH)
                yield HOP
                dve.wait_ge(on["mem_out"], KT)
                chain.link(ts(rows[b], rows[b], -80.0, None, ALU.max))
                v.tensor_copy(cols[0:1, 29:30], cols[0:1, 30:31]).then_inc(on["rows_out"], 1)
                dve.wait_ge(on["pos_in"], 32)
                dve.wait_ge(on["dist_ready"], 1)
                v.tensor_copy(pos_rowf[:], pos_row[:]).then_inc(on["pos_ready"], 1)
                dve.wait_ge(on["pos_bcast"], 1)
                chain.link(ts(ang[:], M[0][:], freq_col[:], None, ALU.mult))
                chain.link(ts(ret_q[:], ang[:], 0.5 / math.pi, ROUND_MAGIC, ALU.mult, ALU.add))
                chain.link(ts(ret_q[:], ret_q[:], -ROUND_MAGIC, None, ALU.add))
                for part in TWO_PI_PARTS:
                    chain.link(stt(out=ang[:], in0=ret_q[:], scalar=-part, in1=ang[:], op0=ALU.mult, op1=ALU.add))
                chain.link(ts(sin_t[:], ang[:], -3.1415925, 3.1415925, ALU.max, ALU.min))
                chain.link(stt(out=cos_t[:], in0=sin_t[:], scalar=-1.0, in1=sin_t[:], op0=ALU.mult, op1=ALU.max))
                ts(cos_t[:], cos_t[:], -1.0, math.pi / 2, ALU.mult, ALU.add).then_inc(on["ang_ready"], 1)
                yield SEG
                yield HOP
                dve.wait_ge(on["rows_act"], 1)
                chain.link(ts(sq[b], sq[b], 1.0, None, ALU.add))
                chain.put(v.reciprocal(rows[b], sq[b]))
                chain.put(v.memset(nrm[a], 1.0))
                chain.sync()
                chain.put(v.memset(nrm[a, 0::P], 0.0))
                chain.link(stt(out=gtmp[a], in0=gtmp[a], scalar=0.0, in1=sq[a], op0=ALU.max, op1=ALU.add))
                chain.link(ts(gtmp[a], gtmp[a], cols[a, 22:23], -1.0, ALU.mult, ALU.mult))
                v.tensor_tensor_scan(rows[a], nrm[a], gtmp[a], 0.0, ALU.mult, ALU.add).then_inc(on["rows_ready"], 1)
                dve.wait_ge(on["dec_exp"], 1)
                chain.link(ts(ret_dec[:], ret_dec[:], P ** -0.5, None, ALU.mult))
                chain.link(v.memset(ret_dec[CH:P, :, 0:CH], 0.0))
                yield SEG
                yield HOP
                dve.wait_ge(on["trig_ready"], 1)
                dve.wait_ge(on["cols_ready"], 1)
                dve.wait_ge(on["rows_ready"], 1)
                dve.wait_ge(on["mem_parked"], 16)
                yield SEG

            def retention(par, hd):
                q, k = stage[:, par, 0], stage[:, par, 1]
                yield HOP
                clamp_gate(stage[:, par, 3])
                dve.wait_ge(on["ret_rot"], hd + 1)
                for n, t in enumerate((q, k)):
                    dst = (ret_q, ret_k)[n]
                    chain.put(tt(dst[:], t, cos_t[:], ALU.mult))
                    chain.link(tt(ret_t[:, n], M[n][:], sin_t[:], ALU.mult))
                chain.put(tt(ret_q[:], ret_q[:], ret_t[:, 0], ALU.add))
                tt(ret_k[:], ret_k[:], ret_t[:, 1], ALU.add).then_inc(on["ret_qk"], 1)
                yield SEG
                yield HOP
                dve.wait_ge(on["ret_scores"], hd + 1)
                for j in range(NT):
                    last = tt(packed(ret_wt, j), score_ps(j),
                              ret_dec[:, bass.ds(hd, 1), 0:WID[j]].rearrange("p a s -> p (a s)"), ALU.mult)
                last.then_inc(on["ret_w"], 1)
                yield SEG
                yield HOP
                y_out(hd + Y_RET, par, hd + H_RET)
                yield SEG
                yield HOP
                yield SEG

            def delta_conv(par, hd, t):
                for i in range(CONV - 1, -1, -1):
                    d = CONV - 1 - i
                    w = convs[:, bass.ds(hd + (i * 3 * NH + t * NH), 1)]
                    if d == 0:
                        chain.link(ts(dn_c[:, t], stage[:, par, t], w, None, ALU.mult))
                    else:
                        chain.link(stt(out=dn_c[:, t, d:S], in0=stage[:, par, t, 0:S - d], scalar=w,
                                       in1=dn_c[:, t, d:S], op0=ALU.mult, op1=ALU.add))
                ts(dn_temp[t][:], dn_c[:, t], GATE_FLOOR, None, ALU.max).then_inc(on["dn_clamped"], 1)

            def delta_silu(hd, tiles=(0, 1, 2)):
                for t in tiles:
                    dve.wait_ge(on["dn_sig"], hd * 3 + (t + 1))
                    tt(dn_c[:, t], dn_c[:, t], dn_temp[t][:], ALU.mult).then_inc(on["dn_silu"], 1)

            def delta_scaled(hd):
                dve.wait_ge(on["dn_silu"], hd * 3 + 3)
                dve.wait_ge(on["dn_inv"], hd * 2 + 1)
                stt(out=dn_c[:, 0], in0=dn_c[:, 0], scalar=QSCALE, in1=dn_gb[:], op0=ALU.mult, op1=ALU.mult)
                dve.wait_ge(on["dn_inv"], hd * 2 + 2)
                tt(dn_c[:, 1], dn_c[:, 1], dn_dt[:], ALU.mult).then_inc(on["dn_qk"], 1)

            def delta_first():
                yield HOP
                for t in range(2):
                    delta_conv(0, 0, t)
                delta_silu(0, (0, 1))
                yield SEG
                yield HOP
                delta_conv(0, 0, 2)
                delta_silu(0, (2,))
                delta_scaled(0)
                yield SEG

            def delta(par, hd):
                gcol = rcols[:, :, bass.ds(hd + NH, 1)]
                beta = rcols[:, :, bass.ds(hd, 1)]
                col = lambda n: dn_cols[:, n].unsqueeze(2)
                wide = lambda c: c.broadcast_to([P, NT, P])
                ts(dn_rows[DECAY:DECAY + NH], rows[DECAY:DECAY + NH],
                   ident[DECAY:DECAY + NH, bass.ds(hd + DECAY, 1)], None, ALU.mult)
                ts(dn_rows[BETA:BETA + NH], rows[BETA:BETA + NH], ident[BETA:BETA + NH, bass.ds(hd + BETA, 1)], None,
                   ALU.mult).then_inc(on["bcast_rows"], 1)
                yield HOP
                dve.wait_ge(on["dn_qk"], hd + 1)
                dve.wait_ge(on["bcast_ps"], hd + 1)
                chain.put(tt(flat3(dn_bs[:]), flat3(M[1][:]), every_tile(tri_strict[:]), ALU.mult))
                dve.wait_ge(on["dn_gbev"], hd + 1)
                chain.link(tt(flat3(dn_dt[:]), flat3(dn_gb[:]), wide(gcol), ALU.subtract))
                ts(dn_dt[:], dn_dt[:], 0.0, None, ALU.min).then_inc(on["dn_dd"], 1)
                g_last = dn_gb[:, P - 1::P].unsqueeze(2)
                v.tensor_copy(col(4), gcol)
                tt(col(5), g_last, gcol, ALU.subtract)
                v.tensor_copy(col(6), g_last).then_inc(on["dn_cols"], 1)
                dve.wait_ge(on["vt_ready"], heads.at(1))
                tt(flat3(dn_bv[:]), flat3(M[4][:]), wide(beta), ALU.mult).then_inc(on["vtok_ready"], 1)
                dve.wait_ge(on["dn_dt"], hd + 1)
                chain.link(tt(dn_bs[:], dn_bs[:], dn_dt[:], ALU.mult))
                dve.wait_ge(on["dn_gram"], hd + 1)
                tt(dn_lt[:], M[2][:], dn_bs[:], ALU.mult).then_inc(on["dn_pair"], 1)
                tt(dn_at[:], M[3][:], dn_dt[:], ALU.mult).then_inc(on["dn_at"], 1)
                dve.wait_ge(on["dn_colexp"], hd + 1)
                chain.link(tt(col(7), col(0), beta, ALU.mult))
                dve.wait_ge(on["dn_tok"], hd + 1)
                tt(flat3(dn_kbe), flat3(M[5][:]), wide(col(7)), ALU.mult)
                tt(flat3(dn_kdec[:]), flat3(M[5][:]), wide(col(1)), ALU.mult).then_inc(on["dn_bvk"], 1)
                dve.wait_ge(on["dn_c1t"], hd + 1)
                chain.put(tt(flat3(dn_xx[:]), every_tile(ident[:]), flat3(M[4][:]), ALU.subtract))
                ins = tt(flat3(dn_xt[:]), every_tile(ident[:]), flat3(dn_ctt[:, 0]), ALU.subtract)
                ins.then_inc(on["dn_x"], 1)
                dve.wait_ge(on["dn_eg"], hd + 1)
                tt(dn_qg, dn_c[:, 0], dn_gb[:], ALU.mult).then_inc(on["dn_qg"], 1)

                def take_v(n):
                    dve.wait_ge(on["dn_x"], hd * 7 + n)
                    dve.wait_ge(on["dn_v"], hd * 6 + n)
                    if n < 6:
                        chain.put(tt(dn_xx[:], dn_xx[:], M[3][:], ALU.subtract))
                    tt(dn_xt[:], dn_xt[:], M[4][:], ALU.subtract).then_inc(on["dn_x"], 1)

                yield SEG
                take_v(1)
                yield HOP
                dve.wait_ge(on["dn_at"], hd + 1)
                dve.wait_ge(on["dn_qg"], hd + 1)
                for t in range(2):
                    take_v(t + 2)
                    delta_conv(1 - par, hd + 1, t)
                yield SEG
                take_v(4)
                delta_silu(hd + 1, (0, 1))
                yield HOP
                take_v(5)
                delta_conv(1 - par, hd + 1, 2)
                take_v(6)
                clamp_gate(stage[:, par, 3])
                yield SEG
                yield HOP
                for c in range(NT):
                    if c:
                        dve.wait_ge(on["dn_ws"], hd * 3 + c)
                        tt(dn_vn[:], dn_uu[:, c * P:(c + 1) * P], M[4][:, 0:P], ALU.subtract).then_inc(on["dn_vnew"], 1)
                    if c < NT - 1:
                        dve.wait_ge(on["dn_ds"], hd * 3 + (c + 1))
                        if c == 0:
                            ins = v.tensor_copy(dn_st[:], M[5][:, 0:P])
                        else:
                            dve.wait_ge(on["dn_state"], hd * 3 + c)
                            ins = stt(out=dn_st[:], in0=dn_st[:], scalar=dn_cols[:, 2, c:c + 1], in1=M[5][:, 0:P],
                                      op0=ALU.mult, op1=ALU.add)
                        ins.then_inc(on["dn_state"], 1)
                    if c == 0:
                        delta_silu(hd + 1, (2,))
                        delta_scaled(hd + 1)
                y_out(hd + Y_DN, par, hd + H_DN)
                heads.step()
                yield SEG

            def gla_logits():
                chain.link(v.memset(restart[:], 1.0))
                chain.put(v.memset(restart[:, 0::CH], 0.0))
                for p in range(2):
                    dve.wait_ge(on["gla_l"], p + 1)
                    chain.link(stt(out=gla_t[:, p], in0=gla_t[:, p], scalar=0.0, in1=gla_e[:, p], op0=ALU.min,
                                   op1=ALU.subtract))
                    chain.put(v.tensor_tensor_scan(b_loc[:, p], restart[:], gla_t[:, p], 0.0, ALU.mult, ALU.add))
                    chain.put(v.tensor_tensor_scan(b_all[:, p], gla_t[:, p], restart[:], 0.0, ALU.add, ALU.min))
                chain.sync()

            def gla(par):
                q, k = stage[:, par, 0], stage[:, par, 1]

                def halves(t, h):
                    t = t.rearrange("p (b two h) -> p b two h", two=2, h=h)
                    return t[:, :, 0, :], t[:, :, 1, :]

                def distances(n):
                    h = 256 >> n
                    lo, up = halves((b_all if h >= 64 else b_loc)[:, par], h)
                    e_lo, e_up = halves(gla_e[:, n % 2], h)
                    mid = lo[:, :, h - 1:h].broadcast_to([P, S // (2 * h), h])
                    chain.put(tt(e_up, up, mid, ALU.subtract))
                    tt(e_lo, mid, lo, ALU.subtract).then_inc(on["gla_d"], 1)

                def decayed(n):
                    h = 256 >> n
                    dve.wait_ge(on["gla_e"], par * 9 + n + 1)
                    if n >= 2:
                        dve.wait_ge(on["gla_lv"], par * 9 + n - 1)
                    e_lo, e_up = halves(gla_e[:, n % 2], h)
                    d_lo, d_up = halves(gla_qk[:, n % 2], h)
                    chain.put(tt(d_up, halves(gla_qs[:], h)[1], e_up, ALU.mult))
                    tt(d_lo, halves(k, h)[0], e_lo, ALU.mult).then_inc(on["gla_qe"], 1)
                    dve.wait_ge(on["gla_qe"], par * 9 + n + 1)

                def take(n):
                    dve.wait_ge(on["gla_lv"], par * 9 + n + 1)
                    mask = every_tile(lvl_mask[:, n - 2].bitcast(mybir.dt.uint32))
                    for hh in range(2):
                        bank = M[4 + hh] if n % 2 == 0 else M[2 + hh]
                        ins = v.copy_predicated(flat3(gla_s[:, hh]), mask, flat3(bank[:]))
                        if hh == 0:
                            chain.put(ins)
                    ins.then_inc(on["gla_lvout"], 1)

                chain.link(ts(gla_qs[:], q, DK ** -0.5, None, ALU.mult))
                v.tensor_copy(cols[0:1, 29:30], cols[0:1, 30:31]).then_inc(on["gla_qs"], 1)
                yield HOP
                if par == 0:
                    gla_logits()
                distances(0)
                distances(1)
                clamp_gate(stage[:, par, 4])
                dve.wait_ge(on["gla_diag"], par + 1)
                for hh in range(2):
                    ins = tt(flat3(gla_s[:, hh]), flat3(M[2 + hh][:]), every_tile(ident[:]), ALU.mult)
                ins.then_inc(on["gla_lvout"], 1)
                for n in range(9):
                    decayed(n)
                    if n < 7:
                        distances(n + 2)
                    if n == 3:
                        dve.wait_ge(on["gla_lvout"], par * 8 + 1)
                    if n > 3:
                        dve.wait_ge(on["gla_lvout"], par * 8 + n - 2)
                    if n >= 3:
                        take(n - 1)
                    if n in (1, 3, 5, 7):
                        yield SEG
                        yield HOP
                dve.wait_ge(on["gla_lvout"], par * 8 + 7)
                take(8)
                for hh in range(2):
                    if hh:
                        clamp_gate(stage[:, par, 5])
                    y_out(Y_GLA + 2 * par + hh, hh, H_GLA + 2 * par + hh)
                    yield SEG
                    if hh == 0:
                        yield HOP

            def stick(par):
                for hh in range(2):
                    hd = 2 * par + hh
                    yield HOP
                    dve.wait_ge(on["sb_l"], hd + 1)
                    chain.link(ts(sb_m[:], sb_x[:], -1.0, 0.0, ALU.mult, ALU.min))
                    tt(sb_m[:], sb_m[:], sb_l[:], ALU.subtract).then_inc(on["sb_lk"], 1)
                    yield SEG
                    yield HOP
                    dve.wait_ge(on["sb_cum"], hd + 1)
                    for at, n, bank in ((0, WID[0], M[3]), (OFF[1], WID[1], M[4]), (OFF[2], WID[2] + WID[3], M[5])):
                        ins = tt(sb_x[:, at:at + n], sb_x[:, at:at + n], bank[:, 0:n], ALU.add)
                    ins.then_inc(on["sb_z"], 1)
                    yield SEG
                    yield HOP
                    y_out(Y_SB + hd, hh, H_SB + hd, gated=False)
                    yield SEG

            window(None, rows[:])
            mixer = tables()
            for j in range(3):
                window(mixer, stage[:, 0, j])
            with dve.Fori(0, NH // 2) as i:
                slabs.enter(i, 8)
                chain.count.enter(i, 2 * RET_LINKS)
                for par in range(2):
                    mixer = retention(par, i * 2 + par)
                    for j in range(4):
                        window(mixer, stage[:, 1 - par, j - 1] if j else stage[:, par, 3])
            slabs.leave(NH // 2)
            chain.count.leave(NH // 2)
            heads.step(NH)
            mixer = delta_first()
            window(mixer, stage[:, 0, 3])
            window(mixer, stage[:, 1, 0])
            stage_tiles = stage[:].rearrange("p a t s -> p (a t) s")
            with dve.Fori(0, NH // 2) as i:
                slabs.enter(i, 8)
                heads.enter(i, 2)
                chain.count.enter(i, 2 * DN_LINKS)
                for par in range(2):
                    mixer = delta(par, i * 2 + par)
                    for j in range(3):
                        window(mixer, stage[:, 1 - par, j + 1])
                    window(mixer, stage_tiles[:, bass.ds(i * -2 + 6, 1)].rearrange("p a s -> p (a s)") if par
                           else stage[:, 0, 0])
            slabs.leave(NH // 2)
            heads.leave(NH // 2)
            chain.count.leave(NH // 2)
            mixer = gla(0)
            for j in range(6):
                window(mixer, stage[:, 1, j - 1] if j else stage[:, 0, 5])
            mixer = gla(1)
            for j in range(6):
                window(mixer, stage[:, 0, j - 1] if j else stage[:, 1, 5])
            mixer = stick(0)
            for j in range(6):
                window(mixer, stage[:, 1, j - 1] if j else stage[:, 0, 5])

            for k in range(KT):
                dve.wait_ge(on["mem_hi"], k + 1)
                tt(act_lo[:, k, 0:NMEM], mem_back[:, k], f32(act_hi[:, k, 0:NMEM]), ALU.subtract).then_inc(
                    on["mem_split"], 1)

            def kv_out(slot):
                dve.wait_ge(on["slab_mul"], slabs.at())
                v.tensor_copy(kv_t[:, slot], G[(slabs.first - 1) % 2][:, 0:NMEM]).then_inc(on["slab_out"], 1)

            def kv_window(slot, mixer=None):
                kv_out(slot)
                if mixer is not None:
                    next(mixer)
                split_lo()
                run_segment(mixer)

            mixer = stick(1)
            window(mixer, stage[:, 1, 5])
            for idx in range(KV_SIDE):
                if idx >= 2:
                    dve.wait_ge(kv_tile_parked[idx % 2], 16 * (idx // 2))
                kv_window(idx % 2, mixer if idx % 2 and idx < KV_SIDE - 1 else None)
                slabs.step()
            with dve.Fori(KV_SIDE // 2, KT // 2) as i:
                slabs.enter(i - KV_SIDE // 2, 2)
                for slot in range(2):
                    dve.wait_ge(kv_tile_parked[slot], i * 16)
                    kv_window(slot)
                    slabs.step()
            slabs.leave(KT // 2 - KV_SIDE // 2)
            for idx in range(2):
                dve.wait_ge(kv_tile_parked[idx], 16 * (KT // 2))
                kv_window(idx)
                slabs.step()
            with dve.Fori(1, KT // 2 - 1) as i:
                slabs.enter(i - 1, 2)
                for slot in range(2):
                    dve.wait_ge(on["kv_turned"], i * 2 + (slot - 1))
                    kv_window(slot)
                    slabs.step()
            slabs.leave(KT // 2 - 2)
            dve.wait_ge(on["kv_turned"], KT - 3)
            kv_window(0)
            slabs.step()

            splits = Count()

            def split_activations(gain=None, beside=None, take_last=None):
                for k in range(KT):
                    if take_last is not None and k == KT - 1:
                        take_last()
                        dve.wait_ge(on["slab_out"], slabs.at())
                    if beside is not None and k in (5, KT - NH):
                        next(beside)
                    splits.step()
                    dve.wait_ge(on["xg_hi"], KT + splits.n)
                    if gain is None:
                        ins = tt(act_lo[:, k], main[:, k], f32(act_hi[:, k]), ALU.subtract)
                    else:
                        ins = stt(out=act_lo[:, k], in0=main[:, k], scalar=vecs[:, gain + k:gain + k + 1],
                                  in1=f32(act_hi[:, k]), op0=ALU.mult, op1=ALU.subtract)
                    ins.then_inc(on["act_ready"], 1)
                split_lo()
                slabs.step()

            def add_to_main(m):
                dve.wait_ge(on["slab_mul"], slabs.at())
                tt(main[:, m], main[:, m], G[(slabs.first - 1) % 2][:], ALU.add).then_inc(on["slab_out"], 1)

            def residual(fill):
                for m in range(KT - 1):
                    if m % 4 == 0:
                        dve.wait_ge(main_back[m // 4], 16 * fill)
                    add_to_main(m)
                    split_lo()
                    slabs.step()

            def attention(hd):
                yield HOP
                dve.wait_ge(on["cx_scores"], hd + 1)
                for n in range(2):
                    ins = v.tensor_reduce(ccols[:, 0, 2 * n:2 * n + 2], M[n][:].rearrange("p (t m) -> p t m", m=NMEM),
                                          AX.X, ALU.max)
                    chain.put(ins)
                chain.sync()
                ts(ccols[:, 1], ccols[:, 0], -CSCALE, None, ALU.mult).then_inc(on["cx_max"], 1)
                yield HOP
                dve.wait_ge(on["cx_exp"], hd + 1)
                chain.link(v.reciprocal(ccols[:, 3], ccols[:, 2]))
                tt(prob[:], prob[:], ccols[:, 3].unsqueeze(2).broadcast_to([P, NT, NMEM]), ALU.mult).then_inc(
                    on["cx_p"], 1)
                yield SEG
                for _ in range(3):
                    yield HOP
                    yield SEG

            dve.wait_ge(on["kv_turned"], KT - 2)
            kv_out(1)
            split_activations()
            residual(1)
            split_activations(V_CROSS, take_last=lambda: add_to_main(KT - 1))

            dve.wait_ge(on["x_rstd"], 1)
            mixer = None
            for m in range(KT - 1):
                if m % 4 == 3:
                    mixer = attention(m // 4)
                window(mixer, cstage[:, (m // 4) % 2, m % 4])
            evict_scaled(cstage[:, (NH - 1) % 2, NH - 1])
            mixer = attention(NH - 1)
            next(mixer)
            split_activations(beside=mixer)
            residual(2)
            split_activations(V_MLP, take_last=lambda: add_to_main(KT - 1))

            def chunk(c, first=False, last=False):
                for w in range(2 * MC):
                    if w == 0 and first:
                        continue
                    if 1 <= w <= MC:
                        j = w - 1
                        dve.wait_ge(on["mlp_relu"], c * MC + (j + 1))
                        tt(uf[:, j % 2], relu[:, j % 2], G[(slabs.first - 1) % 2][:], ALU.mult).then_inc(
                            on["slab_out"], 1)
                        dve.wait_ge(on["mlp_uhi"], c * MC + (j + 1))
                        tt(u_lo[:, j], uf[:, j % 2], f32(u_hi[:, j]), ALU.subtract).then_inc(on["u_ready"], 1)
                    else:
                        down_out((w - MC - 1) % MC)
                    if not (last and w == 2 * MC - 1):
                        split_lo()
                    if last and w > MC + 1:
                        final_gain(w - MC - 2)
                    slabs.step()

            def down_out(d):
                slot = (slabs.first - 1) % 2
                dve.wait_ge(on["slab_mul"], slabs.at())
                dve.wait_ge(on["slab_out"], slabs.at(-1))
                for j in range(2):
                    chain.put(tt(xsq[:, j], M[2 * slot + j][:], rstd[:], ALU.mult))
                chain.sync()
                for j in range(2):
                    ins = tt(main[:, 2 * d + j], main[:, 2 * d + j], xsq[:, j], ALU.add)
                ins.then_inc(on["slab_out"], 1)

            def final_gain(d):
                for k in (2 * d, 2 * d + 1):
                    dve.wait_ge(on["xsq_ready"], 2 * KT + k + 1)
                    ts(main[:, k], main[:, k], vecs[:, V_FINAL + k:V_FINAL + k + 1], None, ALU.mult).then_inc(
                        on["fin_x"], 1)

            dve.wait_ge(on["x_rstd"], 2)
            chunk(0, True)
            with dve.Fori(1, NCH - 1) as c:
                slabs.enter(c - 1, 2 * MC)
                chain.count.enter(c - 1, 2 * MC)
                chunk(c)
            slabs.leave(NCH - 2)
            chain.count.leave(NCH - 2)
            chunk(NCH - 1, last=True)
            down_out(MC - 1)

            final_gain(MC - 2)
            final_gain(MC - 1)
            dve.wait_ge(on["fin_rstd"], 1)
            for n in range(1, NT * 4, 2):
                t, g = n // 4, n % 4
                dve.wait_ge(on["fin_turned"], n + 1)
                if t >= 2:
                    dve.wait_ge(out_done[t % 2], 16 * (t // 2))
                ts(w_raw[:, t % 2, g * S:(g + 1) * S], M[n % 4][:], cols[:, t:t + 1], None, ALU.mult).then_inc(
                    on["fin_odd"], 1)


_INS = ("x", "mem", "positions", "ln_mix", "w_in", "gla_w_up", "gla_b_up", "dn_conv_w", "dn_a_log", "dn_dt_bias",
        "mix_head_norm", "w_mix_out", "ln_cross", "ln_mem", "w_cross_q", "w_cross_kv", "w_cross_o", "ln_mlp",
        "w_mlp_up", "w_mlp_down", "ln_final")


def kernel(**inputs):
    import numpy as _np
    import concourse.bacc as _bacc
    from concourse import mybir as _mybir
    from concourse.bass_utils import run_bass_kernel_spmd as _run

    nc = _bacc.Bacc("TRN2", target_bir_lowering=False, num_devices=1)
    arrays = {f"in_{name}_dram": _np.ascontiguousarray(inputs[name]) for name in _INS}
    freq = (10000.0 ** (-_np.arange(0, P, 2) / P)).astype(_np.float32)
    arrays["in_inv_freq_dram"] = _np.concatenate([freq, freq])[:, None].copy()
    args = [nc.dram_tensor(name, a.shape, _mybir.dt.from_np(a.dtype), kind="ExternalInput").ap()
            for name, a in arrays.items()]
    shape = inputs["x"].shape
    args.append(nc.dram_tensor("out_0_dram", shape, F32, kind="ExternalOutput").ap())
    build(nc, *args)
    r = _run(nc, [arrays], core_ids=[0])
    return r.results[0]["out_0_dram"]
```
